# Optimizing a Trainium2 kernel written in Bass

```python
import functools
import jax, jax.numpy as jnp
from jax import lax
import numpy as np

D_MODEL = 1024
BATCH = 1
SEQ = 1024
DEPTH = 1
DEC_BATCH = 8
DEC_SEQ = 1
PAST_LEN = 256
PAGE_SIZE = 128

POOL_WINDOWS = (2, 4, 8, 16)
POOL_GROUPS = 4
POOL_GROUP = D_MODEL // 8
POOL_WIDTH = POOL_GROUPS * POOL_GROUP
POOL_BUF = max(POOL_WINDOWS) - 1
CHUNK = 128
SG_GROUPS = 4
SG_GROUP = D_MODEL // 8
SG_WIDTH = SG_GROUPS * SG_GROUP
SB_HEADS = 8
SB_HEAD_DIM = D_MODEL // 16
SB_WIDTH = SB_HEADS * SB_HEAD_DIM
SB_BLOCK = 128
SB_SCALE = SB_HEAD_DIM ** -0.5
SB_BIAS_INIT = -5.0
N_BRANCH = 3
BRANCH_WIDTH = 512
IN_SPLITS = (POOL_WIDTH,
             POOL_WIDTH + SG_WIDTH,
             POOL_WIDTH + 2 * SG_WIDTH,
             POOL_WIDTH + 2 * SG_WIDTH + SB_WIDTH,
             POOL_WIDTH + 2 * SG_WIDTH + 2 * SB_WIDTH,
             POOL_WIDTH + 2 * SG_WIDTH + 3 * SB_WIDTH)
IN_WIDTH = IN_SPLITS[-1] + N_BRANCH * D_MODEL
FFN_DIM = ((8 * D_MODEL // 3 + 127) // 128) * 128
CONV_WIDTH = 3
EPS = 1e-6

kernel_name = 'hybrid_pool_sgmlp_stickbreak_decode_step'

def rms_norm(x, g):
    xf = x.astype(jnp.float32)
    y = xf * lax.rsqrt(jnp.mean(xf * xf, axis=-1, keepdims=True) + EPS)
    return (y * g.astype(jnp.float32)).astype(x.dtype)

def pool_mixer(xa, prefix, pos0, pool_w, pool_scale):
    B, T, _ = xa.shape
    ext = jnp.concatenate([prefix.astype(xa.dtype), xa], axis=1)
    c = jnp.cumsum(ext.astype(jnp.float32), axis=1)
    c = jnp.pad(c, ((0, 0), (1, 0), (0, 0)))
    pos = (pos0 + jnp.arange(T)).astype(jnp.float32)
    groups = []
    for gi, w in enumerate(POOL_WINDOWS):
        sl = slice(gi * POOL_GROUP, (gi + 1) * POOL_GROUP)
        s = c[:, POOL_BUF + 1:POOL_BUF + 1 + T, sl] - c[:, POOL_BUF + 1 - w:POOL_BUF + 1 - w + T, sl]
        cnt = jnp.minimum(pos + 1.0, float(w))[None, :, None]
        groups.append(s / cnt)
    mean = jnp.stack(groups, axis=2)
    d = (mean - xa.reshape(B, T, POOL_GROUPS, POOL_GROUP).astype(jnp.float32)).astype(xa.dtype)
    y = jnp.einsum('btgc,gcd->btgd', d, pool_w).reshape(B, T, POOL_WIDTH)
    return y * pool_scale, ext[:, -POOL_BUF:]

def spatial_gate(u, v, sg_w, sg_b):
    B, T, _ = v.shape
    L = min(T, CHUNK)
    n = T // L
    w = jnp.tril(sg_w[:, :L, :L])
    vc = v.reshape(B, n, L, SG_GROUPS, SG_GROUP)
    mixed = jnp.einsum('gts,bnsgc->bntgc', w, vc) + sg_b[:, :L].T[None, None, :, :, None]
    return u * mixed.reshape(B, T, SG_WIDTH)

def stick_breaking(q, k, v, bias, qpos):
    kpos = jnp.arange(k.shape[1])
    z = (jnp.einsum('bqhd,bkhd->bhqk', q, k).astype(jnp.float32) * SB_SCALE
         + bias.astype(jnp.float32)[None, :, None, None])
    mask = kpos[None, :] < qpos[:, None]
    log_rest = jnp.where(mask, jax.nn.log_sigmoid(-z), 0.0)
    after = lax.cumsum(log_rest, axis=3, reverse=True) - log_rest
    a = jnp.where(mask, jnp.exp(jax.nn.log_sigmoid(z) + after), 0.0)
    return jnp.einsum('bhqk,bkhd->bqhd', a.astype(v.dtype), v)

def sb_prompt(q, k, v, bias):
    B, S, H, Dh = q.shape
    nb = S // SB_BLOCK
    qb = q.reshape(B, nb, SB_BLOCK, H, Dh).transpose(1, 0, 2, 3, 4)

    def one(args):
        qi, i = args
        return stick_breaking(qi, k, v, bias, i * SB_BLOCK + jnp.arange(SB_BLOCK))

    out = lax.map(one, (qb, jnp.arange(nb)))
    return out.transpose(1, 0, 2, 3, 4).reshape(B, S, H, Dh)

def sb_sample(q, k, v, bias, k_past, v_past, past_len):
    kk = jnp.concatenate([k_past.astype(k.dtype), k], axis=1)
    vv = jnp.concatenate([v_past.astype(v.dtype), v], axis=1)
    return stick_breaking(q, kk, vv, bias, past_len + jnp.arange(q.shape[1]))

def conv_ffn(h, prefix, w_up, conv_w, conv_b, w_down):
    up = h @ w_up
    T = up.shape[1]
    ext = jnp.concatenate([prefix.astype(up.dtype), up], axis=1)
    c = conv_b + sum(ext[:, j:j + T] * conv_w[j] for j in range(CONV_WIDTH))
    gate, val = jnp.split(c, 2, axis=-1)
    return (jax.nn.gelu(gate) * val) @ w_down, ext[:, -(CONV_WIDTH - 1):]

def layer(x, pos0, pool_prefix, conv_prefix, attend, p):
    (g_mix_pre, g_mix_post, g_ffn_pre, g_ffn_post, w_in, pool_w, pool_scale,
     sg_w, sg_b, sb_bias, w_branch, w_out, w_up, conv_w, conv_b, w_down) = p
    B, T, _ = x.shape
    h = rms_norm(x, g_mix_pre)
    a, u, v, q, k, vv, gates = jnp.split(h @ w_in, IN_SPLITS, axis=-1)
    ya, pool_state = pool_mixer(a, pool_prefix, pos0, pool_w, pool_scale)
    yb = spatial_gate(u, v, sg_w, sg_b)
    q = q.reshape(B, T, SB_HEADS, SB_HEAD_DIM)
    k = k.reshape(B, T, SB_HEADS, SB_HEAD_DIM)
    vv = vv.reshape(B, T, SB_HEADS, SB_HEAD_DIM)
    yc = attend(q, k, vv, sb_bias).reshape(B, T, SB_WIDTH)
    br = jnp.einsum('btnc,ncd->btnd', jnp.stack([ya, yb, yc], axis=2), w_branch)
    g = jax.nn.sigmoid(gates.reshape(B, T, N_BRANCH, D_MODEL))
    mixed = jnp.sum(g * br, axis=2) @ w_out
    x = x + rms_norm(mixed, g_mix_post)
    f, conv_state = conv_ffn(rms_norm(x, g_ffn_pre), conv_prefix, w_up, conv_w, conv_b, w_down)
    x = x + rms_norm(f, g_ffn_post)
    return x, pool_state, k, vv, v, conv_state

def setup_inputs(seed: int = 0) -> dict:
    key = jax.random.key(seed)
    ks = jax.random.split(key, 23)
    n_pages = PAST_LEN // PAGE_SIZE
    n_used = DEC_BATCH * n_pages
    n_pool = n_used + n_used // 4

    def nrm(k, shape, scale):
        return jax.random.normal(k, shape, jnp.float32) * scale

    def gain(k):
        return 1.0 + nrm(k, (DEPTH, D_MODEL), 0.05)

    page_table = jax.random.permutation(ks[5], n_pool)[:n_used].reshape(DEC_BATCH, n_pages).astype(jnp.int32)
    return {
        'x_prompt': nrm(ks[0], (BATCH, SEQ, D_MODEL), 1.0),
        'x_sample': nrm(ks[1], (DEC_BATCH, DEC_SEQ, D_MODEL), 1.0),
        'state_pool': nrm(ks[2], (DEPTH, DEC_BATCH, POOL_BUF, POOL_WIDTH), 1.0),
        'cache_k': nrm(ks[3], (DEPTH, n_pool, PAGE_SIZE, SB_HEADS, SB_HEAD_DIM), 1.0),
        'cache_v': nrm(ks[4], (DEPTH, n_pool, PAGE_SIZE, SB_HEADS, SB_HEAD_DIM), 1.0),
        'page_table': page_table,
        'state_conv': nrm(ks[6], (DEPTH, DEC_BATCH, CONV_WIDTH - 1, 2 * FFN_DIM), 1.0),
        'norm_mix_pre': gain(ks[7]),
        'norm_mix_post': gain(ks[8]),
        'norm_ffn_pre': gain(ks[9]),
        'norm_ffn_post': gain(ks[10]),
        'w_in': nrm(ks[11], (DEPTH, D_MODEL, IN_WIDTH), D_MODEL ** -0.5),
        'pool_w': nrm(ks[12], (DEPTH, POOL_GROUPS, POOL_GROUP, POOL_GROUP), POOL_GROUP ** -0.5),
        'pool_scale': 1.0 + nrm(ks[13], (DEPTH, POOL_WIDTH), 0.05),
        'sg_w': nrm(ks[14], (DEPTH, SG_GROUPS, CHUNK, CHUNK), CHUNK ** -0.5),
        'sg_b': 1.0 + nrm(ks[15], (DEPTH, SG_GROUPS, CHUNK), 0.05),
        'sb_bias': SB_BIAS_INIT + nrm(ks[22], (DEPTH, SB_HEADS), 0.1),
        'w_branch': nrm(ks[16], (DEPTH, N_BRANCH, BRANCH_WIDTH, D_MODEL), BRANCH_WIDTH ** -0.5),
        'w_out': nrm(ks[17], (DEPTH, D_MODEL, D_MODEL), D_MODEL ** -0.5),
        'w_up': nrm(ks[18], (DEPTH, D_MODEL, 2 * FFN_DIM), D_MODEL ** -0.5),
        'conv_w': nrm(ks[19], (DEPTH, CONV_WIDTH, 2 * FFN_DIM), CONV_WIDTH ** -0.5),
        'conv_b': nrm(ks[20], (DEPTH, 2 * FFN_DIM), 0.02),
        'w_down': nrm(ks[21], (DEPTH, FFN_DIM, D_MODEL), FFN_DIM ** -0.5),
    }

def reference(x_prompt, x_sample, state_pool, cache_k, cache_v, page_table, state_conv,
              norm_mix_pre, norm_mix_post, norm_ffn_pre, norm_ffn_post, w_in, pool_w,
              pool_scale, sg_w, sg_b, sb_bias, w_branch, w_out, w_up, conv_w, conv_b, w_down):
    B = x_prompt.shape[0]
    DB = x_sample.shape[0]
    past_len = page_table.shape[1] * cache_k.shape[2]
    weights = (norm_mix_pre, norm_mix_post, norm_ffn_pre, norm_ffn_post, w_in, pool_w,
               pool_scale, sg_w, sg_b, sb_bias, w_branch, w_out, w_up, conv_w, conv_b, w_down)
    xp, xs = x_prompt, x_sample
    pool_p, pool_s, k_p, v_p, k_s, v_s, sgv_s, conv_p, conv_s = ([] for _ in range(9))
    for l in range(DEPTH):
        p = tuple(w[l] for w in weights)
        zero_pool = jnp.zeros((B, POOL_BUF, POOL_WIDTH), xp.dtype)
        zero_conv = jnp.zeros((B, CONV_WIDTH - 1, 2 * FFN_DIM), xp.dtype)
        xp, pp, kp, vp, _, cp = layer(xp, 0, zero_pool, zero_conv, sb_prompt, p)
        k_past = cache_k[l][page_table].reshape(DB, past_len, SB_HEADS, SB_HEAD_DIM)
        v_past = cache_v[l][page_table].reshape(DB, past_len, SB_HEADS, SB_HEAD_DIM)
        attend = functools.partial(sb_sample, k_past=k_past, v_past=v_past, past_len=past_len)
        xs, ps, ks_, vs_, sgv, cs = layer(xs, past_len, state_pool[l], state_conv[l], attend, p)
        pool_p.append(pp); pool_s.append(ps)
        k_p.append(kp); v_p.append(vp); k_s.append(ks_); v_s.append(vs_)
        sgv_s.append(sgv); conv_p.append(cp); conv_s.append(cs)
    return (xp, xs, jnp.stack(pool_p), jnp.stack(pool_s), jnp.stack(k_p), jnp.stack(v_p),
            jnp.stack(k_s), jnp.stack(v_s), jnp.stack(sgv_s), jnp.stack(conv_p), jnp.stack(conv_s))


_drawn_inputs = setup_inputs


def setup_inputs(seed=0):
    import zlib

    import numpy as np

    out = dict(_drawn_inputs(seed))
    spreads = {}
    factors = {'sb_bias': 8.0, 'conv_b': 3.374}
    for name, (base, spread) in spreads.items():
        noise = np.random.default_rng([zlib.crc32(name.encode()), seed]).standard_normal(out[name].shape)
        drawn = base * np.exp(spread * noise) if base else spread * noise
        out[name] = __import__('jax').numpy.asarray(drawn.astype(out[name].dtype))
    for name, factor in factors.items():
        out[name] = (out[name] * factor).astype(out[name].dtype)
    return out
```

```python
from contextlib import ExitStack

import concourse.bass as bass
from concourse import mybir

F32 = mybir.dt.float32
F32R = mybir.dt.float32r
BF16 = mybir.dt.bfloat16
I32 = mybir.dt.int32
ALU = mybir.AluOpType
ACT = mybir.ActivationFunctionType
AX_X = mybir.AxisListType.X

P = 128


def build(nc, x_prompt, x_sample, state_pool, cache_k, cache_v, page_table, state_conv,
          norm_mix_pre, norm_mix_post, norm_ffn_pre, norm_ffn_post, w_in, pool_w, pool_scale,
          sg_w, sg_b, sb_bias, w_branch, w_out, w_up, conv_w, conv_b, w_down, outs):
    (y_prompt, y_sample, pool_prompt, pool_sample, k_prompt, v_prompt, k_sample, v_sample,
     sgv_sample, conv_prompt, conv_sample) = outs

    D = x_prompt.shape[2]
    TP = x_prompt.shape[1]
    NS = x_sample.shape[0]
    T = TP + NS
    NCH = 3
    CH = T // NCH
    KT = D // P
    NT = TP // P
    SG = pool_w.shape[1]
    BT = w_branch.shape[2] // P
    H = sb_bias.shape[1]
    DH = k_prompt.shape[4]
    HP = H // 2
    NPOOL = cache_k.shape[1]
    NPG = page_table.shape[1]
    NE = NS * NPG
    F = w_down.shape[1]
    FT = F // P
    PB = state_pool.shape[2]
    WINDOWS = (2, 4, 8, 16)
    PAD = max(WINDOWS)
    SCALE = DH ** -0.5
    HALF = 512
    TAIL = 2 + NS
    PTAIL = PB + NS
    NEG = -1.0e30
    assert T == NCH * CH and CH % 2 == 0 and CH <= 512 and cache_k.shape[2] == P
    assert DH * 2 == P and BT == SG == HP and x_sample.shape[1] == 1 and NPG == 2

    C_A, C_U, C_V, C_Q, C_K, C_VV, C_G = (n * BT for n in range(7))
    FFN_GROUPS = [(0, 8), (8, 7), (15, 7)]
    assert sum(n for _, n in FFN_GROUPS) == FT

    U_ATT = 0
    U_SG = U_ATT + 4 * HP
    U_MIXC = U_SG + SG
    U_MIXA = U_MIXC + 2 * KT
    U_U = U_MIXA + 2 * KT
    U_MIXB = U_U + SG
    U_OUT = U_MIXB + 2 * KT
    U_UP, U_DOWN = [], []
    n = U_OUT + KT
    for _, size in FFN_GROUPS:
        U_UP.append(n)
        U_DOWN.append(n + 2 * size)
        n += 2 * size + KT
    U_END = n

    USES = {}
    n0 = n1 = 0
    for name, a, b in ([("in", 5, 4), ("att", 2 * HP, 2 * HP), ("sg", 2, 2), ("mixc", KT, KT),
                        ("pool", 2, 2), ("mixa", KT, KT), ("u", 2, 2), ("mixb", KT, KT),
                        ("out", KT // 2, KT // 2), ("ss_m", 1, 0), ("xt", KT // 2, KT // 2),
                        ("ss_x", 1, 0)]
                       + [x for g, (_, size) in enumerate(FFN_GROUPS)
                          for x in ((f"up{g}", size, size), (f"down{g}", KT // 2, KT // 2))]
                       + [("ss_f", 1, 0), ("yt", 5, 4)]):
        USES[name] = (n0, n1)
        n0, n1 = n0 + a, n1 + b

    def freed(stage, par, k):
        return k + (USES[stage][par] + 1)

    CHUNKS = []
    for hh in range(2):
        for half in reversed(range(TP // HALF)):
            top = (half + 1) * HALF // P - 1
            for kb in reversed(range(top + 1)):
                q0 = max(kb * P, half * HALF)
                CHUNKS.append((hh, kb, q0, (half + 1) * HALF - q0, kb == top, kb == 0))
    NCK = len(CHUNKS)
    later_upto = [0]
    for n, (_, _, _, W, top, last) in enumerate(CHUNKS):
        wider = not top and W > CHUNKS[n - 1][3]
        later_upto.append(later_upto[-1] + (0 if last else 1 + wider))
    NLATER = later_upto[NCK]
    assert NCK % 12 == 0
    LAG_CUM, LAG_PV, LAG_EXP = 3, 5, 4

    ctx = ExitStack()
    with ctx:
        def sb(name, shape, dt=F32, scope=ctx):
            return scope.enter_context(nc.sbuf_tensor(name, shape, dt))

        h_hi = sb("h_hi", [P, KT, T], F32R)
        h_lo = sb("h_lo", [P, KT, T], F32R)
        stage = [sb(f"stage{i}", [P, KT, P]) for i in range(2)]
        w_hi = [sb(f"w_hi{i}", [P, KT, P], F32R) for i in range(2)]
        w_lo = [sb(f"w_lo{i}", [P, KT, P], F32R) for i in range(2)]
        ident = sb("ident", [P, P])
        ones = sb("ones", [P, P])
        neg_ones = sb("neg_ones", [P, P])
        neg_tri = sb("neg_tri", [P, P], F32R)
        ident_b = sb("ident_b", [P, P], BF16)
        mask_b = sb("mask_b", [P, P], BF16)
        NORM_COLS = 3 * KT + SG
        par_t = sb("par_t", [P, NORM_COLS + 4 * 2 * FT])
        g_post, g_ffn, g_fpost = (par_t[:, n * KT:(n + 1) * KT] for n in range(3))
        a_scale = par_t[:, 3 * KT:NORM_COLS]
        conv_par = par_t[:, NORM_COLS:].rearrange("p (j f) -> p j f", j=4)
        bias_h = sb("bias_h", [P, H])
        bias_p = sb("bias_p", [P, 2])
        nbias_p = sb("nbias_p", [P, 2])
        w00 = sb("w00", [P, SG])
        b0 = sb("b0", [P, SG])
        conv_st = sb("conv_st", [P, 2 * FT, NS, 2])
        tails = sb("tails", [P, 2 * FT, TAIL])
        inv_cnt = sb("inv_cnt", [P, PB])
        edge = sb("edge", [P, PB])
        pre = sb("pre", [P, NS])
        eps = sb("eps", [P, 1])
        ss = sb("ss", [P, NT + 1])
        std = sb("std", [P, NT + 1])
        rs = sb("rs", [P, NT + 1])
        work = [sb(f"work{i}", [P, PAD + TP]) for i in range(3)]
        rstd, ss_acc, sq = (w[:, 0:T] for w in work)
        sgv_tok = work[1][0:NS, 0:SG * P]
        win = work[0:2]
        small_tok = work[0][0:PTAIL, 0:4 * P].rearrange("p (a b) -> p a b", a=4)

        s_in = ExitStack()
        x_tok = sb("x_tok", [P, NT + 1, D], F32, s_in)
        g_pre = sb("g_pre", [P, D], F32, s_in)
        st_rows = sb("st_rows", [NS * 2, 2 * F], F32, s_in)
        norm_rows = sb("norm_rows", [NORM_COLS, P], F32, s_in)
        conv_rows = sb("conv_rows", [2 * FT, 4, P], F32, s_in)
        s_in.close()

        s_pair = ExitStack()
        q_hi, q_lo, k_hi, k_lo = (sb(n, [P, T], F32R, s_pair) for n in ("q_hi", "q_lo", "k_hi", "k_lo"))
        k_f, v_f = (sb(n, [P, T], F32, s_pair) for n in ("k_f", "v_f"))
        k_tok, v_tok = (sb(n, [P, NT, P], F32, s_pair) for n in ("k_tok", "v_tok"))
        s_pair.close()
        s_dec = ExitStack()
        q_bc = sb("q_bc", [P, 4, HP * P], F32, s_dec)
        kv_pg = sb("kv_pg", [P, 4, HP * P], F32, s_dec)
        kq = sb("kq", [P, HP * P], F32, s_dec)
        sp_rows = sb("sp_rows", [NS * PB, SG * P], F32, s_dec)
        sgw_rows = sb("sgw_rows", [P, SG, P], F32, s_dec)
        vsg_tok = sb("vsg_tok", [P, NT, P], F32, s_dec)
        z_dec, t_dec, a_dec = (sb(n, [P, NPG, NS, H], F32, s_dec) for n in ("z_dec", "t_dec", "a_dec"))
        s_dec.close()
        trunk = sb("trunk", [P, KT, T])

        s_mix = ExitStack()
        y_hi = sb("y_hi", [P, BT, T], F32R, s_mix)
        y_lo = sb("y_lo", [P, BT, T], F32R, s_mix)
        a_raw = sb("a_raw", [P, SG, PAD + T], F32, s_mix)
        s_att = ExitStack()
        zl = [sb(f"zl{i}", [P, HALF], F32, s_att) for i in range(4)]
        sp_hi = [sb(f"sp_hi{i}", [P, HALF], F32R, s_att) for i in range(3)]
        sp_lo = [sb(f"sp_lo{i}", [P, HALF], F32R, s_att) for i in range(3)]
        later = [sb(f"later{i}", [P, HALF], F32, s_att) for i in range(4)]
        att = [sb(f"att{i}", [P, HALF], F32, s_att) for i in range(2)]
        q_dec = sb("q_dec", [P, NS], F32, s_att)
        a_tail = sb("a_tail", [P, PTAIL], F32, s_att)
        s_att.close()
        spat = sb("spat", [P, SG, T], F32, s_mix)
        pool_st = sb("pool_st", [P, SG, NS * PB], F32, s_mix)
        sgw_t = sb("sgw_t", [P, SG, P], F32, s_mix)
        sgb_row = sb("sgb_row", [1, SG * P], F32, s_mix)
        poolw = sb("poolw", [P, SG, P], F32, s_mix)
        s_sg = ExitStack()
        vsg_dec = sb("vsg_dec", [P, SG, NS], F32, s_sg)
        pt_sb = sb("pt_sb", [1, NE], I32, s_sg)
        vsg_f = [work[2][:, 0:T], sb("vsg_f1", [P, T], F32, s_sg)[:, :]]
        s_sg.close()
        s_gate = ExitStack()
        gate = [sb(f"gate{i}", [P, T], F32, s_gate) for i in range(2)]
        s_gate.close()
        s_mix.close()
        s_res = ExitStack()
        xr_tok = sb("xr_tok", [P, NT + 1, D], F32, s_res)
        hn = [sb(f"hn{i}", [P, T], F32, s_res) for i in range(2)]
        s_res.close()
        s_ffn = ExitStack()
        GMAX = max(n for _, n in FFN_GROUPS)
        g_hi = sb("g_hi", [P, GMAX, T], F32R, s_ffn)
        g_lo = sb("g_lo", [P, GMAX, T], F32R, s_ffn)
        up = [sb(f"up{i}", [P, T], F32, s_ffn) for i in range(2)]
        conv = [sb(f"conv{i}", [P, T], F32, s_ffn) for i in range(2)]
        s_ffn.close()
        x1_back = sb("x1_back", [P, KT, T])
        y_tok = sb("y_tok", [P, 4, D])

        ps_all = [ctx.enter_context(nc.psum_tensor(f"ps{i}", [P, NCH, 512], F32)) for i in range(2)]
        misc_t = ctx.enter_context(nc.psum_tensor("misc", [P, 2 * 512], F32))
        ps = [t[:, :, 0:CH] for t in ps_all]
        ps_flat = [t[:, :, :].rearrange("p a b -> p (a b)") for t in ps_all]
        misc = misc_t[:, :]
        z_bank = [ps_all[i // NCH][:, i % NCH, :] for i in range(2 * NCH)]
        DEC0 = TP - (NCH - 1) * CH

        def chunks(ap):
            return ap.rearrange("p (a b) -> p a b", a=NCH)

        def last_cols(par, n):
            return ps_all[par][:, NCH - 1, CH - n:CH]

        x1_dram = nc.dram_tensor("x1_scratch", [P, KT, T], F32, kind="Internal").ap()
        q_dram = nc.dram_tensor("q_scratch", [NS, HP * P], F32, kind="Internal").ap()

        win_v, wout_v, wup_v, wdn_v = (w.rearrange("o (k p) n -> p (o k) n", p=P)
                                       for w in (w_in, w_out, w_up, w_down))
        wbr_v = w_branch.rearrange("o b (k p) n -> p (o b) k n", p=P)

        sems = {}

        def sem(name):
            if name not in sems:
                sems[name] = ctx.enter_context(nc.semaphore(name))
            return sems[name]

        w_landed = [sem("w_landed0"), sem("w_landed1")]
        ps_free = [sem("ps_free0"), sem("ps_free1")]
        tail_out = [sem("tail_out0"), sem("tail_out1")]
        y_out_done = [sem(f"y_out_done{i}") for i in range(4)]
        page_in = [sem(f"page_in{i}") for i in range(4)]
        qbc_in = [sem(f"qbc_in{i}") for i in range(4)]
        x_in = [sem(f"x_in{i}") for i in range(3)]
        (params_in, gpre_in, consts, par_ps, par_sb, ss_made, std_made, rs_made, xn_made, xt_ps, h_hi_made,
         w_hi_made, w_lo_made, unit_done, biasp_made, q_hi_made, kf_made, k_hi_made, ktok_ps,
         ktok_made, vtok_ps, vtok_made, small_ps, small_made, tok_out, z_ready, abs_made, e_made,
         l_ready, spn_ready, hi_ready, sp_ready, later_ready, cum_ready, att_ready,
         pv_done, yc_hi_made, yc_made) = (sem(n) for n in (
             "params_in", "gpre_in", "consts", "par_ps", "par_sb", "ss_made", "std_made", "rs_made",
             "xn_made", "xt_ps", "h_hi_made", "w_hi_made", "w_lo_made", "unit_done",
             "biasp_made", "q_hi_made", "kf_made", "k_hi_made", "ktok_ps", "ktok_made", "vtok_ps",
             "vtok_made", "small_ps", "small_made", "tok_out", "z_ready", "abs_made", "e_made",
             "l_ready", "spn_ready", "hi_ready", "sp_ready", "later_ready",
             "cum_ready", "att_ready", "pv_done", "yc_hi_made", "yc_made"))
        (st_in, pt_in, sgw_masked, sg_ps, sg_sb, vsgtok_ps, vsgtok_made, mixed_ps, spat_made,
         kq_made, zd_made, zb_made, dec_abs, dec_e, dec_l, dec_sp, dec_cum, dec_arg, dec_att, dec_pv,
         ydec_hi, ydec_made, sgv_ps, sgv_sb, pads_made, win_step, pool_edge, pool_pre,
         pool_d) = (
             sem(n) for n in (
                 "st_in", "pt_in", "sgw_masked", "sg_ps", "sg_sb", "vsgtok_ps", "vsgtok_made",
                 "mixed_ps", "spat_made", "kq_made", "zd_made", "zb_made", "dec_abs", "dec_e", "dec_l",
                 "dec_sp", "dec_cum", "dec_arg", "dec_att", "dec_pv", "ydec_hi", "ydec_made",
                 "sgv_ps", "sgv_sb", "pads_made", "win_step", "pool_edge", "pool_pre",
                 "pool_d"))
        (ya_ps, y_hi_made, y_made, gated, mix_made, yb_made, mhi_made, m_split, sq_made, ss_added,
         ss_ps, std_t, rstd_t, xr_in, xt_done, mr_made, x1_made, hn_made, hn_hi, h2_made, x1_out,
         conv_step, gelu_made, gv_made, g_hi_made, g_made, acc_made, tail_ps, tail_sb,
         x1r_in, yr_made, yf_made, yt_ps, yt_left, yt_right, hi_begun, out_done, ss_zero) = (
             sem(n) for n in (
                 "ya_ps", "y_hi_made", "y_made", "gated", "mix_made", "yb_made", "mhi_made",
                 "m_split", "sq_made", "ss_added", "ss_ps", "std_t", "rstd_t", "xr_in",
                 "xt_done", "mr_made", "x1_made", "hn_made", "hn_hi", "h2_made", "x1_out",
                 "conv_step", "gelu_made", "gv_made", "g_hi_made", "g_made",
                 "acc_made", "tail_ps", "tail_sb", "x1r_in", "yr_made", "yf_made",
                 "yt_ps", "yt_left", "yt_right", "hi_begun", "out_done", "ss_zero"))
        BEGIN = [(ps_free[0], 1), (ps_free[1], 1), (w_lo_made, 2), (sp_ready, 3), (cum_ready, 3),
                 (pv_done, 2), (tok_out, 16), (yc_made, 1), (mix_made, 2), (g_made, 1),
                 (ss_added, 1), (ss_made, 1)]
        TOK_DMAS = 7
        NCONST = 5 + PB
        NPARAMS = 10
        IN_BATCHES = [range(0, 4), range(4, NT), range(NT, NT + 1)]
        PAR_COLS = NORM_COLS + 4 * 2 * FT
        ST_AT = 212
        ST0 = (512 - ST_AT) // (2 * NS)
        LAST_DOWN = f"down{len(FFN_GROUPS) - 1}"
        dec_o = misc[:, 512:512 + HP * NS * 2].rearrange("p (a b h) -> p a b h", a=HP, b=NS)

        block = ctx.enter_context(nc.Block())

        @block.sync
        def _(sp):
            for s, n in BEGIN:
                sp.sem_inc(s, n)

            def fetch(u, par, src):
                sp.wait_ge(w_lo_made, u + 1)
                sp.dma_start(stage[par][:, 0:src.shape[1], :], src).then_inc(w_landed[par], 16)

            def col(v, c):
                return v[:, :, bass.ds(c * P, P)]

            def mix_tiles(d, first, branch):
                fetch(d * 2 + first, 0, col(win_v, d + (C_G + branch * KT)))
                fetch(d * 2 + (first + 1), 1, wbr_v[:, branch, :, bass.ds(d * P, P)])

            def fetch_mix(first, branch, begin=0):
                with sp.Fori(begin, KT) as d:
                    mix_tiles(d, first, branch)

            for n in range(NT):
                sp.dma_start(x_tok[:, n, :], x_prompt[0, n * P:(n + 1) * P, :]).then_inc(x_in[n // 4], 16)
            sp.dma_start(x_tok[0:NS, NT, :], x_sample.rearrange("b t d -> (b t) d")).then_inc(x_in[2], 16)
            with sp.Fori(0, HP) as p:
                for j, c in enumerate((C_Q, C_K, C_VV, C_A)):
                    fetch(p * 4 + j, j % 2, col(win_v, p + c))
                sp.wait_ge(ktok_made, p + 1)
                sp.dma_start(k_prompt[0, 0, :, bass.ds(p * 2, 2), :].rearrange("(n q) h d -> q n (h d)", q=P),
                             k_tok[:, :, :]).then_inc(tok_out, 16)
                sp.wait_ge(vtok_made, p + 1)
                sp.dma_start(v_prompt[0, 0, :, bass.ds(p * 2, 2), :].rearrange("(n q) h d -> q n (h d)", q=P),
                             v_tok[:, :, :]).then_inc(tok_out, 16)
                sp.wait_ge(small_made, p * 2 + 2)
                sp.dma_start(q_dram[:, bass.ds(p * P, P)], small_tok[0:NS, 0, :]).then_inc(tok_out, 16)
                for j, dst in ((1, k_sample), (2, v_sample)):
                    sp.dma_start(dst[0, :, 0, bass.ds(p * 2, 2), :].rearrange("b h d -> b (h d)"),
                                 small_tok[0:NS, j, :]).then_inc(tok_out, 16)
                sp.dma_start(pool_prompt[0, 0, :, bass.ds(p * P, P)], small_tok[0:PB, 3, :]).then_inc(tok_out, 16)
                sp.dma_start(pool_sample[0, :, PB - 1, bass.ds(p * P, P)],
                             small_tok[PB:PTAIL, 3, :]).then_inc(tok_out, 16)
            for g in range(SG):
                fetch(U_SG + g, g % 2, win_v[:, :, (C_V + g) * P:(C_V + g + 1) * P])
            sp.wait_ge(yc_made, HP + 1)
            sp.wait_ge(tok_out, 16 * (TOK_DMAS * HP + 1))
            sp.dma_start(sp_rows[:, :], state_pool.rearrange("o b j c -> (o b j) c")).then_inc(st_in, 16)
            sp.dma_start(sgw_rows[:, :, :], sg_w.rearrange("o g t s -> t (o g) s")).then_inc(st_in, 16)
            sp.dma_start(sgb_row[:, :], sg_b.rearrange("o g t -> o (g t)")).then_inc(st_in, 16)
            sp.dma_start(poolw[:, :, :], pool_w.rearrange("o g c d -> c (o g) d")).then_inc(st_in, 16)
            sp.dma_start(pt_sb[:, :], page_table.rearrange("(o b) j -> o (b j)", o=1)).then_inc(pt_in, 16)
            sp.wait_ge(pt_in, 16)
            for which, cache in enumerate((cache_k, cache_v)):
                for e in range(NE):
                    n = which * NE + e
                    if 4 <= n < NE + 4:
                        sp.wait_ge(kq_made, n - 3)
                    elif n >= NE + 4:
                        sp.wait_ge(dec_pv, n - 3 - NE)
                    if which == 0 and e % NPG == 0:
                        b = e // NPG
                        if b >= 4:
                            sp.wait_ge(kq_made, (b - 3) * NPG)
                        sp.dma_start(q_bc[:, b % 4, :], q_dram[b, :].partition_broadcast(P)
                                     ).then_inc(qbc_in[b % 4], 16)
                    page = sp.value_load(pt_sb[0:1, e:e + 1], min_val=0, max_val=NPOOL - 1)
                    sp.dma_start(kv_pg[:, n % 4, :],
                                 cache[0, bass.ds(page, 1), :, :, :].rearrange("o t h d -> (o t) (h d)")
                                 ).then_inc(page_in[n % 4], 16)
                    if n == NE // 2:
                        mix_tiles(0, U_MIXC, 2)
            fetch_mix(U_MIXC, 2, 1)
            sp.wait_ge(sgv_sb, 1)
            sp.dma_start(sgv_sample[0, :, 0, :], sgv_tok[:, :]).then_inc(out_done, 16)
            fetch_mix(U_MIXA, 0)
            with sp.Fori(0, SG // 2) as i:
                for j in range(2):
                    fetch(i * 2 + (U_U + j), j, col(win_v, i * 2 + (C_U + j)))
            fetch_mix(U_MIXB, 1)
            with sp.Fori(0, KT // 2) as i:
                for j in range(2):
                    fetch(i * 2 + (U_OUT + j), j, col(wout_v, i * 2 + j))
            sp.wait_ge(m_split, KT)
            sp.dma_start(xr_tok[:, 0:NT, :], x_prompt.rearrange("o (n q) d -> q (o n) d", q=P)).then_inc(xr_in, 16)
            sp.dma_start(xr_tok[0:NS, NT, :], x_sample.rearrange("b t d -> (b t) d")).then_inc(xr_in, 16)
            for g, (f0, size) in enumerate(FFN_GROUPS):
                def up_tiles(j):
                    fetch(j * 2 + U_UP[g], 0, col(wup_v, j + f0))
                    fetch(j * 2 + (U_UP[g] + 1), 1, col(wup_v, j + (f0 + FT)))
                if g == 0:
                    up_tiles(0)
                    for par in range(2):
                        sp.wait_ge(ps_free[par], freed("xt", par, KT // 2))
                    sp.dma_start(x1_dram, trunk[:, :, :]).then_inc(x1_out, 16)
                with sp.Fori(1 if g == 0 else 0, size) as j:
                    up_tiles(j)
                with sp.Fori(0, KT // 2) as i:
                    for j in range(2):
                        fetch(i * 2 + (U_DOWN[g] + j), j,
                              wdn_v[:, f0:f0 + size, bass.ds((i * 2 + j) * P, P)])
            sp.wait_ge(unit_done, U_END)
            sp.wait_ge(x1_out, 16)
            sp.dma_start(x1_back[:, :, :], x1_dram).then_inc(x1r_in, 16)
            for n in range(2 * FT // 4):
                sp.wait_ge(tail_sb, n + 1)
                rows = up[n % 2][0:TAIL, 0:4 * P]
                sp.dma_start(conv_prompt[0, 0, :, n * 4 * P:(n + 1) * 4 * P], rows[0:2, :]).then_inc(tail_out[n % 2], 16)
                sp.dma_start(conv_sample[0, :, 1, n * 4 * P:(n + 1) * 4 * P], rows[2:TAIL, :]).then_inc(tail_out[n % 2], 16)
            for n in range(NT):
                sp.wait_ge(yt_left, n + 1)
                sp.wait_ge(yt_right, n + 1)
                sp.dma_start(y_prompt[0, n * P:(n + 1) * P, :], y_tok[:, n % 4, :]).then_inc(y_out_done[n % 4], 16)
            sp.wait_ge(yt_left, NT + 1)
            sp.wait_ge(yt_right, NT + 1)
            sp.dma_start(y_sample.rearrange("b t d -> (b t) d"), y_tok[0:NS, NT % 4, :]).then_inc(y_out_done[NT % 4], 16)
            for k in range(4):
                sp.wait_ge(y_out_done[k], 16 * ((NT + 4 - k) // 4))
            sp.wait_ge(out_done, 16 * 3)
            for k in range(2):
                sp.wait_ge(tail_out[k], 32 * ((2 * FT // 4 + 1 - k) // 2))
            sp.wait_ge(tok_out, 16 * (TOK_DMAS * HP + 1))

        @block.gpsimd
        def _(pool):
            def split_hi(par, n16, u):
                pool.wait_ge(w_landed[par], n16)
                if u is not None:
                    pool.wait_ge(unit_done, u - 1)
                    pool.sem_inc(hi_begun, 1)
                nc.gpsimd.tensor_scalar(w_hi[par][:, :, :], stage[par][:, :, :], 1.0, 0.0,
                                        ALU.mult, ALU.add).then_inc(w_hi_made, 1)

            def split_stage(first, count):
                with pool.Fori(0, count // 2) as i:
                    for j in range(2):
                        split_hi(j, i * 16 + 16 * (first // 2 + 2), i * 2 + (first + 2 + j))

            nc.gpsimd.memset(ident[:, :], 0.0).then_inc(consts, 1)
            nc.gpsimd.memset(ones[:, :], 1.0).then_inc(consts, 1)
            nc.gpsimd.memset(neg_ones[:, :], -1.0).then_inc(consts, 1)
            nc.gpsimd.memset(mask_b[:, :], NEG).then_inc(consts, 1)
            nc.gpsimd.memset(eps[:, :], 1e-6).then_inc(consts, 1)
            for t in range(PB):
                nc.gpsimd.memset(inv_cnt[:, t:t + 1], 1.0 / (t + 1)).then_inc(consts, 1)
            pool.wait_ge(consts, NCONST)
            nc.gpsimd.affine_select(out=ident[:, :], in_=ident[:, :], compare_op=ALU.not_equal, fill=1.0,
                                    base=0, pattern=[[-1, P]], channel_multiplier=1).then_inc(consts, 1)
            nc.gpsimd.affine_select(out=neg_tri[:, :], in_=neg_ones[:, :], compare_op=ALU.is_ge, fill=0.0,
                                    base=0, pattern=[[-1, P]], channel_multiplier=1).then_inc(consts, 1)
            nc.gpsimd.affine_select(out=mask_b[:, :], in_=mask_b[:, :], compare_op=ALU.is_ge, fill=0.0,
                                    base=0, pattern=[[-1, P]], channel_multiplier=1).then_inc(consts, 1)
            pool.wait_ge(consts, NCONST + 1)
            nc.gpsimd.tensor_copy(ident_b[:, :], ident[:, :]).then_inc(consts, 1)
            split_hi(0, 16, None)
            split_hi(1, 16, None)
            with pool.Fori(0, HP) as p:
                for j in range(4):
                    split_hi(j % 2, p * 32 + 16 * (2 + j // 2), p * 4 + (2 + j))
                for c, (hh, kb, q0, W, top, last) in enumerate(CHUNKS):
                    pool.wait_ge(spn_ready, p * NCK + (c + 1))
                    pool.wait_ge(cum_ready, p * NCK + (c + 1))
                    pool.sem_inc(hi_begun, 1)
                    nc.gpsimd.tensor_scalar(sp_hi[c % 3][:, 0:W], zl[c % 4][:, 0:W], bias_p[:, hh:hh + 1], 1.0,
                                            ALU.add, ALU.mult).then_inc(hi_ready, 1)
            pool.wait_ge(yc_made, HP + 1)
            pool.wait_ge(tok_out, 16 * (TOK_DMAS * HP + 1))
            nc.gpsimd.memset(a_raw[:, :, 0:PAD], 0.0).then_inc(pads_made, 1)
            for w in win:
                nc.gpsimd.memset(w[:, 0:PAD], 0.0).then_inc(pads_made, 1)
            pool.wait_ge(st_in, 64)
            for g in range(SG):
                nc.gpsimd.affine_select(out=sgw_rows[:, g, :], in_=sgw_rows[:, g, :], compare_op=ALU.is_ge,
                                        fill=0.0, base=0, pattern=[[-1, P]], channel_multiplier=1
                                        ).then_inc(sgw_masked, 1)
            pool.wait_ge(pads_made, 3)
            step = 0
            for g in range(SG):
                split_hi(g % 2, 16 * (U_SG // 2 + 2 + g // 2), U_SG + 2 + g)
                src = a_raw[:, g, 0:PAD + TP]
                for m in range(g + 1):
                    if g > 0 and m == 0:
                        pool.wait_ge(pool_d, 3 * g)
                    if m > 0:
                        pool.wait_ge(win_step, step)
                    dst = win[m % 2]
                    nc.gpsimd.tensor_tensor(dst[:, PAD:PAD + TP], src[:, PAD:PAD + TP],
                                            src[:, PAD - 2 ** m:PAD + TP - 2 ** m], ALU.add
                                            ).then_inc(win_step, 1)
                    step += 1
                    src = dst
            split_stage(U_MIXC, U_END - 2 - U_MIXC)

        @block.scalar
        def _(act):
            A = nc.scalar.activation

            act.dma_start(g_pre[:, :], norm_mix_pre[0, :].partition_broadcast(P)).then_inc(gpre_in, 16)
            rows = [(norm_rows[n * KT:(n + 1) * KT, :], v.rearrange("o (k p) -> (o k) p", p=P))
                    for n, v in enumerate((norm_mix_post, norm_ffn_pre, norm_ffn_post))]
            rows += [(norm_rows[3 * KT:NORM_COLS, :], pool_scale.rearrange("o (k p) -> (o k) p", p=P)),
                     (conv_rows[:, 0:3, :], conv_w.rearrange("o j (f p) -> f (o j) p", p=P)),
                     (conv_rows[:, 3, :], conv_b.rearrange("o (f p) -> (o f) p", p=P)),
                     (st_rows[:, :], state_conv.rearrange("o b j c -> (o b j) c")),
                     (bias_h[:, :], sb_bias[0, :].partition_broadcast(P))]
            for dst, src in rows:
                act.dma_start(dst, src).then_inc(params_in, 16)
            with nc.allow_non_contiguous_dma(reason="one element of each group"):
                act.dma_start(w00[:, :], sg_w[0, :, 0, 0].partition_broadcast(P)).then_inc(params_in, 16)
                act.dma_start(b0[:, :], sg_b[0, :, 0].partition_broadcast(P)).then_inc(params_in, 16)
            act.dma_start(pool_sample[0, :, 0:PB - 1, :], state_pool[0, :, 1:PB, :]).then_inc(out_done, 16)
            act.dma_start(conv_sample[0, :, 0, :], state_conv[0, :, 1, :]).then_inc(out_done, 16)

            act.preload_act_table_set("sqrt_and_others")
            act.wait_ge(consts, NCONST + 4)
            for b, tiles in enumerate(IN_BATCHES):
                act.wait_ge(x_in[b], 16 * len(tiles))
                for n in tiles:
                    m = P if n < NT else NS
                    act.wait_ge(ss_made, n + 1)
                    A(sq[0:m, 0:D], x_tok[0:m, n, :], ACT.Square, accum_out=ss[0:m, n:n + 1]).then_inc(ss_made, 1)
                n0_, n1_ = tiles[0], tiles[-1] + 1
                m = P if n0_ < NT else NS
                act.wait_ge(ss_made, n1_ + 1)
                A(std[0:m, n0_:n1_], ss[0:m, n0_:n1_], ACT.Sqrt, bias=eps[0:m, :], scale=1.0 / D).then_inc(std_made, 1)
                if b == 0:
                    act.wait_ge(par_ps, 1)
                    A(par_t[:, :], misc[:, 0:PAR_COLS], ACT.Copy).then_inc(par_sb, 1)
                    A(conv_st[:, 0:ST0, :, :].rearrange("p f b j -> p (f b j)"),
                      misc[:, ST_AT:ST_AT + ST0 * 2 * NS], ACT.Copy).then_inc(par_sb, 1)
                    A(conv_st[:, ST0:, :, :].rearrange("p f b j -> p (f b j)"),
                      misc[:, 512:512 + (2 * FT - ST0) * 2 * NS], ACT.Copy).then_inc(par_sb, 1)
                for n in tiles:
                    m = P if n < NT else NS
                    act.wait_ge(xt_ps, n + 1)
                    A(h_hi[:, :, n * P:n * P + m],
                      ps_flat[n % 2][:, 0:KT * m].rearrange("p (k t) -> p k t", k=KT), ACT.Copy).then_inc(h_hi_made, 1)

            act.preload_act_table_set("natural_log_exp_and_others")
            with act.Fori(0, HP) as p:
                act.wait_ge(unit_done, p * 4 + 1)
                A(q_dec[:, :], last_cols(0, NS), ACT.Copy, scale=SCALE)
                A(chunks(q_hi[:, :]), ps[0], ACT.Copy, scale=SCALE).then_inc(q_hi_made, 1)
                act.wait_ge(unit_done, p * 4 + 2)
                A(chunks(k_f[:, :]), ps[1], ACT.Copy).then_inc(kf_made, 1)
                A(chunks(k_hi[:, :]), ps[1], ACT.Copy).then_inc(k_hi_made, 1)
                act.wait_ge(unit_done, p * 4 + 3)
                A(chunks(v_f[:, :]), ps[0], ACT.Copy).then_inc(ps_free[0], 1)
                act.wait_ge(unit_done, p * 4 + 4)
                A(a_tail[:, :], last_cols(1, PTAIL), ACT.Copy)
                A(a_raw[:, bass.ds(p, 1), PAD:PAD + T].rearrange("p o (a b) -> p (o a) b", a=NCH), ps[1],
                  ACT.Copy).then_inc(ps_free[1], 1)
                act.wait_ge(vtok_ps, p + 1)
                act.wait_ge(tok_out, p * (16 * TOK_DMAS) + 16)
                A(v_tok[:, :, :].rearrange("p a b -> p (a b)"), misc, ACT.Copy).then_inc(vtok_made, 1)
                act.wait_ge(small_ps, p + 1)
                A(small_tok[0:NS, 0:3, :].rearrange("p a b -> p (a b)"), misc[0:NS, 0:3 * P],
                  ACT.Copy).then_inc(small_made, 1)
                A(small_tok[:, 3, :], misc[0:PTAIL, 3 * P:4 * P], ACT.Copy).then_inc(small_made, 1)
                act.wait_ge(biasp_made, p * 2 + 2)

                def soft(c):
                    hh, kb, q0, W, top, last = CHUNKS[c]
                    t = zl[c % 4][:, 0:W]
                    act.wait_ge(z_ready, p * NCK + (c + 1))
                    act.wait_ge(sp_ready, p * NCK + (c + 1))
                    A(t, z_bank[c % 6][:, 0:W], ACT.Abs, bias=bias_p[:, hh:hh + 1]).then_inc(abs_made, 1)
                    act.wait_ge(abs_made, p * NCK + (c + 1))
                    A(t, t, ACT.Exp, scale=-1.0).then_inc(e_made, 1)
                    act.wait_ge(e_made, p * NCK + (c + 1))
                    A(t, t, ACT.Ln, bias=ones[:, 0:1]).then_inc(l_ready, 1)

                def weights(c):
                    hh, kb, q0, W, top, last = CHUNKS[c]
                    act.wait_ge(cum_ready, p * NCK + (c + 4))
                    act.wait_ge(pv_done, p * NCK + (c + 1))
                    A(att[c % 2][:, 0:W], z_bank[c % 6][:, 0:W], ACT.Exp, bias=bias_p[:, hh:hh + 1]
                      ).then_inc(att_ready, 1)

                for c in range(NCK + LAG_EXP):
                    if c < NCK:
                        soft(c)
                    if c >= LAG_EXP:
                        weights(c - LAG_EXP)
                act.wait_ge(pv_done, p * NCK + (NCK + 2))
                A(y_hi[:, bass.ds(p, 1), 0:TP].rearrange("p o t -> p (o t)"), misc, ACT.Copy).then_inc(yc_hi_made, 1)

            def vsg_out(g):
                par = g % 2
                act.wait_ge(unit_done, U_SG + g + 1)
                if g == 0:
                    act.wait_ge(yc_made, HP + 1)
                    act.wait_ge(tok_out, 16 * (TOK_DMAS * HP + 1))
                A(chunks(vsg_f[par]), ps[par], ACT.Copy)
                A(vsg_dec[:, g, :], last_cols(par, NS), ACT.Copy)
                A(spat[:, g, TP:T], last_cols(par, NS), ACT.Identity, bias=b0[:, g:g + 1],
                  scale=w00[:, g:g + 1]).then_inc(ps_free[par], 1)

            def mix_out(g):
                act.wait_ge(mixed_ps, g + 1)
                A(spat[:, g, 0:TP], misc, ACT.Copy).then_inc(spat_made, 1)

            vsg_out(0)
            vsg_out(1)
            act.wait_ge(sg_ps, 1)
            A(sgw_t[:, :, :].rearrange("p g t -> p (g t)"), misc[:, 0:SG * P], ACT.Copy).then_inc(sg_sb, 1)
            A(pool_st[:, :, :].rearrange("p g t -> p (g t)"), misc[:, 512:512 + SG * NS * PB], ACT.Copy
              ).then_inc(sg_sb, 1)
            vsg_out(2)
            mix_out(0)
            vsg_out(3)
            for g in range(1, SG):
                mix_out(g)
            act.wait_ge(zb_made, 1)
            A(t_dec[:], z_dec[:], ACT.Abs).then_inc(dec_abs, 1)
            act.wait_ge(dec_abs, 1)
            A(t_dec[:], t_dec[:], ACT.Exp, scale=-1.0).then_inc(dec_e, 1)
            act.wait_ge(dec_e, 1)
            A(t_dec[:], t_dec[:], ACT.Ln, bias=ones[:, 0:1]).then_inc(dec_l, 1)
            act.wait_ge(dec_arg, 1)
            A(a_dec[:], z_dec[:], ACT.Exp).then_inc(dec_att, 1)
            act.wait_ge(sgv_ps, 1)
            A(sgv_tok[:, :], misc[0:NS, 0:SG * P], ACT.Copy).then_inc(sgv_sb, 1)
            act.wait_ge(dec_pv, NE)
            for hh in range(2):
                r = slice(hh * DH, (hh + 1) * DH)
                A(y_hi[r, :, TP:T], dec_o[r, :, :, hh], ACT.Copy).then_inc(ydec_hi, 1)

            act.preload_act_table_set("sigmoid_and_others")

            def gates(name, first, adds):
                with act.Fori(0, KT // 2) as i:
                    for k in range(2):
                        act.wait_ge(unit_done, i * 4 + (first + 2 * k + 1))
                        if adds is None:
                            act.wait_ge(ps_free[1], i * 2 + freed(name, 1, k - 1))
                        else:
                            act.wait_ge(mix_made, i * 2 + (adds + k + 1))
                        A(chunks(gate[k][:, :]), ps[0], ACT.Sigmoid).then_inc(ps_free[0], 1)

            gates("mixc", U_MIXC, None)
            for g in range(SG):
                act.wait_ge(ya_ps, g + 1)
                A(chunks(y_hi[:, g, :]), ps[g % 2], ACT.Copy, scale=a_scale[:, g:g + 1]).then_inc(y_hi_made, 1)
            gates("mixa", U_MIXA, 0)
            with act.Fori(0, SG // 2) as i:
                for k in range(2):
                    act.wait_ge(ps_free[k], i + freed("u", k, 1))
                    A(y_hi[:, bass.ds(i * 2 + k, 1), :], spat[:, bass.ds(i * 2 + k, 1), :], ACT.Copy
                      ).then_inc(y_hi_made, 1)
            gates("mixb", U_MIXB, KT)
            act.preload_act_table_set("sqrt_and_others")
            act.wait_ge(unit_done, U_OUT)
            with act.Fori(0, KT) as k:
                act.wait_ge(mix_made, k + (2 + KT + 1))
                A(h_hi[:, bass.ds(k, 1), :], trunk[:, bass.ds(k, 1), :], ACT.Copy).then_inc(mhi_made, 1)

            act.wait_ge(m_split, KT)
            with act.Fori(0, KT // 2) as i:
                for k in range(2):
                    act.wait_ge(unit_done, i * 2 + (U_OUT + k + 1))
                    A(trunk[:, bass.ds(i * 2 + k, 1), :].rearrange("p o (a b) -> p (o a) b", a=NCH), ps[k], ACT.Copy)
                    act.wait_ge(ss_added, i * 2 + (k + 1))
                    A(chunks(sq), ps[k], ACT.Square).then_inc(ps_free[k], 1)

            def std_from(n):
                act.wait_ge(ss_ps, n + 1)
                A(chunks(rstd), ps[0], ACT.Sqrt, bias=eps[:, :], scale=1.0 / D).then_inc(ps_free[0], 1)

            std_from(0)
            with act.Fori(0, KT // 2) as i:
                for k in range(2):
                    act.wait_ge(ps_free[k], i + freed("xt", k, 1))
                    act.wait_ge(ss_added, i * 2 + (KT + k + 1))
                    A(sq, trunk[:, bass.ds(i * 2 + k, 1), :].rearrange("p o t -> p (o t)"), ACT.Square
                      ).then_inc(sq_made, 1)
            std_from(1)
            for k in range(KT):
                act.wait_ge(hn_made, k + 1)
                A(h_hi[:, k, :], hn[k % 2][:, :], ACT.Copy, scale=g_ffn[:, k:k + 1]).then_inc(hn_hi, 1)

            for g, (f0, size) in enumerate(FFN_GROUPS):
                act.preload_act_table_set("gelu_apprx_tanh_and_others")
                with act.Fori(0, size) as j:
                    act.wait_ge(g_made, j + (f0 + 1))
                    for k in range(2):
                        f = bass.ds(j + (f0 + k * FT), 1)
                        act.wait_ge(unit_done, j * 2 + (U_UP[g] + k + 1))
                        A(chunks(up[k][:, :]), ps[k], ACT.Copy)
                        A(tails[:, f, :].rearrange("p o t -> p (o t)"), last_cols(k, TAIL), ACT.Copy)
                        A(chunks(conv[k][:, :]), ps[k], ACT.Identity, bias=conv_par[:, 3, f],
                          scale=conv_par[:, 2, f]).then_inc(ps_free[k], 1)
                    act.wait_ge(conv_step, j * 8 + (8 * f0 + 4))
                    A(conv[0][:, :], conv[0][:, :], ACT.Gelu_apprx_tanh).then_inc(gelu_made, 1)
                    act.wait_ge(gv_made, j + (f0 + 1))
                    A(g_hi[:, bass.ds(j, 1), :].rearrange("p o t -> p (o t)"), conv[0][:, :], ACT.Copy
                      ).then_inc(g_hi_made, 1)
                if g == 0:
                    act.wait_ge(x1_out, 16)
                    with act.Fori(0, KT // 2) as i:
                        for k in range(2):
                            act.wait_ge(unit_done, i * 2 + (U_DOWN[g] + k + 1))
                            A(trunk[:, bass.ds(i * 2 + k, 1), :].rearrange("p o (a b) -> p (o a) b", a=NCH),
                              ps[k], ACT.Copy).then_inc(ps_free[k], 1)
            act.preload_act_table_set("sqrt_and_others")
            with act.Fori(0, KT // 2) as i:
                for k in range(2):
                    act.wait_ge(ps_free[k], i + freed(LAST_DOWN, k, 1))
                    act.wait_ge(ss_added, i * 2 + (2 * KT + k + 1))
                    A(sq, trunk[:, bass.ds(i * 2 + k, 1), :].rearrange("p o t -> p (o t)"), ACT.Square
                      ).then_inc(sq_made, 1)
            std_from(2)
            for n in range(2 * FT // 4):
                act.wait_ge(tail_ps, n + 1)
                if n >= 2:
                    act.wait_ge(tail_out[n % 2], 32 * (n // 2))
                A(up[n % 2][0:TAIL, 0:4 * P], misc[0:TAIL, (n % 2) * 512:(n % 2) * 512 + 4 * P], ACT.Copy
                  ).then_inc(tail_sb, 1)
            for n in range(NT + 1):
                m = P if n < NT else NS
                act.wait_ge(yt_ps, n + 1)
                if n >= 4:
                    act.wait_ge(y_out_done[n % 4], 16 * (n // 4))
                A(y_tok[0:m, n % 4, 0:512], ps_flat[n % 2][0:m, 0:512], ACT.Copy).then_inc(yt_left, 1)

        @block.vector
        def _(dve):
            V = nc.vector

            def split_lo(par, u):
                dve.wait_ge(w_hi_made, u + 1)
                V.tensor_tensor(w_lo[par][:, :, :], stage[par][:, :, :], w_hi[par][:, :, :].bitcast(F32),
                                ALU.subtract).then_inc(w_lo_made, 1)

            dve.wait_ge(gpre_in, 16)
            for b, tiles in enumerate(IN_BATCHES):
                n0_, n1_ = tiles[0], tiles[-1] + 1
                m = P if n0_ < NT else NS
                dve.wait_ge(std_made, b + 1)
                V.reciprocal(rs[0:m, n0_:n1_], std[0:m, n0_:n1_]).then_inc(rs_made, 1)
                dve.wait_ge(rs_made, b + 1)
                for n in tiles:
                    V.scalar_tensor_tensor(x_tok[0:m, n, :], x_tok[0:m, n, :], rs[0:m, n:n + 1], g_pre[0:m, :],
                                           ALU.mult, ALU.mult).then_inc(xn_made, 1)
                for n in tiles:
                    dve.wait_ge(h_hi_made, n + 1)
                    V.tensor_tensor(h_lo[:, :, n * P:n * P + m],
                                    ps_flat[n % 2][:, 0:KT * m].rearrange("p (k t) -> p k t", k=KT),
                                    h_hi[:, :, n * P:n * P + m].bitcast(F32), ALU.subtract
                                    ).then_inc(ps_free[n % 2], 1)
                if b == 0:
                    split_lo(0, 0)
                    split_lo(1, 1)

            dve.wait_ge(params_in, 16 * NPARAMS)
            with dve.Fori(0, HP) as p:
                V.tensor_copy(bias_p[:, :], bias_h[:, bass.ds(p * 2, 2)]).then_inc(biasp_made, 1)
                V.tensor_scalar(nbias_p[:, :], bias_h[:, bass.ds(p * 2, 2)], -1.0, None, ALU.mult).then_inc(biasp_made, 1)
                dve.wait_ge(q_hi_made, p + 1)
                V.scalar_tensor_tensor(chunks(q_lo[:, :]), ps[0], SCALE, chunks(q_hi[:, :]).bitcast(F32),
                                       ALU.mult, ALU.subtract).then_inc(ps_free[0], 1)
                split_lo(0, p * 4 + 2)
                dve.wait_ge(k_hi_made, p + 1)
                V.tensor_tensor(chunks(k_lo[:, :]), ps[1], chunks(k_hi[:, :]).bitcast(F32), ALU.subtract
                                ).then_inc(ps_free[1], 1)
                split_lo(1, p * 4 + 3)
                dve.wait_ge(ktok_ps, p + 1)
                dve.wait_ge(tok_out, p * (16 * TOK_DMAS) + 16)
                V.tensor_copy(k_tok[:, :, :].rearrange("p a b -> p (a b)"), misc).then_inc(ktok_made, 1)
                split_lo(0, p * 4 + 4)
                split_lo(1, p * 4 + 5)
                dve.wait_ge(biasp_made, p * 2 + 2)
                nl = 0
                for c, (hh, kb, q0, W, top, last) in enumerate(CHUNKS):
                    t = zl[c % 4][:, 0:W]
                    dve.wait_ge(l_ready, p * NCK + (c + 1))
                    V.scalar_tensor_tensor(t, z_bank[c % 6][:, 0:W], nbias_p[:, hh:hh + 1], t, ALU.max, ALU.add
                                           ).then_inc(spn_ready, 1)
                    dve.wait_ge(hi_ready, p * NCK + (c + 1))
                    lo = V.scalar_tensor_tensor(sp_lo[c % 3][:, 0:W], t, bias_p[:, hh:hh + 1],
                                                sp_hi[c % 3][:, 0:W].bitcast(F32), ALU.add, ALU.subtract
                                                ).then_inc(sp_ready, 1)
                    if top:
                        V.tensor_scalar(later[c % 4][:, 0:W], t, bias_p[:, hh:hh + 1], None, ALU.add
                                        ).then_inc(later_ready, 1)
                        nl += 1
                    elif not last:
                        Wb = CHUNKS[c - 1][3]
                        dve.wait_ge(later_ready, p * NLATER + nl)
                        V.scalar_tensor_tensor(later[c % 4][:, W - Wb:W], t[:, W - Wb:W], bias_p[:, hh:hh + 1],
                                               later[(c - 1) % 4][:, 0:Wb], ALU.add, ALU.add
                                               ).then_inc(later_ready, 1)
                        if Wb < W:
                            V.tensor_scalar(later[c % 4][:, 0:W - Wb], t[:, 0:W - Wb], bias_p[:, hh:hh + 1], None,
                                            ALU.add).then_inc(later_ready, 1)
                            nl += 1
                        nl += 1
                assert nl == NLATER
                dve.wait_ge(yc_hi_made, p + 1)
                V.tensor_tensor(y_lo[:, bass.ds(p, 1), 0:TP].rearrange("p o t -> p (o t)"), misc,
                                y_hi[:, bass.ds(p, 1), 0:TP].rearrange("p o t -> p (o t)").bitcast(F32),
                                ALU.subtract).then_inc(yc_made, 1)

            dec_scores = 0
            for g in range(SG):
                split_lo(g % 2, U_SG + 2 + g)
                for e in range(g * NE // SG, (g + 1) * NE // SG):
                    b, pg = e // NPG, e % NPG
                    if g == 0 and e == 0:
                        dve.wait_ge(yc_made, HP + 1)
                    dve.wait_ge(page_in[e % 4], 16 * (e // 4 + 1))
                    dve.wait_ge(qbc_in[b % 4], 16 * (b // 4 + 1))
                    if e > 0:
                        dve.wait_ge(zd_made, e)
                    V.tensor_tensor(kq[:, :], kv_pg[:, e % 4, :], q_bc[:, b % 4, :], ALU.mult).then_inc(kq_made, 1)
                    dve.wait_ge(kq_made, e + 1)
                    V.tensor_reduce(z_dec[:, pg, b, :], kq[:, :].rearrange("p (h d) -> p h d", h=H), AX_X, ALU.add
                                    ).then_inc(zd_made, 1)
                dve.wait_ge(vsgtok_ps, g + 1)
                V.tensor_copy(vsg_tok[:, :, :].rearrange("p a b -> p (a b)"), misc).then_inc(vsgtok_made, 1)
                w = WINDOWS[g]
                s, a = win[g % 2][:, PAD:PAD + TP], a_raw[:, g, PAD:PAD + TP]
                dve.wait_ge(win_step, (g + 1) * (g + 2) // 2)
                V.tensor_tensor(edge[:, 0:w - 1], s[:, 0:w - 1], inv_cnt[:, 0:w - 1], ALU.mult).then_inc(pool_edge, 1)
                dve.wait_ge(pool_edge, 2 * g + 1)
                V.tensor_tensor(edge[:, 0:w - 1], edge[:, 0:w - 1], a[:, 0:w - 1], ALU.subtract).then_inc(pool_edge, 1)
                dve.wait_ge(pool_edge, 2 * g + 2)
                V.scalar_tensor_tensor(a, s, 1.0 / w, a, ALU.mult, ALU.subtract).then_inc(pool_d, 1)
                dve.wait_ge(pool_d, 3 * g + 1)
                V.tensor_copy(a[:, 0:w - 1], edge[:, 0:w - 1]).then_inc(pool_d, 1)
                dve.wait_ge(sg_sb, 2)
                ad = a_raw[:, g, PAD + TP:PAD + T]
                V.tensor_reduce(pre[:, :], pool_st[:, g, :].rearrange("p (b j) -> p b j", b=NS)[:, :, PB - (w - 1):PB],
                                AX_X, ALU.add).then_inc(pool_pre, 1)
                dve.wait_ge(pool_pre, 2 * g + 1)
                V.tensor_tensor(pre[:, :], pre[:, :], ad, ALU.add).then_inc(pool_pre, 1)
                dve.wait_ge(pool_pre, 2 * g + 2)
                V.scalar_tensor_tensor(ad, pre[:, :], 1.0 / w, ad, ALU.mult, ALU.subtract).then_inc(pool_d, 1)
            dve.wait_ge(zd_made, NE)
            zv = z_dec[:, :, :, :].rearrange("p g b h -> p (g b) h")
            V.tensor_tensor(zv, zv, bias_h[:, :].unsqueeze(1).to_broadcast([P, NE, H]), ALU.add).then_inc(zb_made, 1)
            dve.wait_ge(dec_l, 1)
            V.scalar_tensor_tensor(t_dec[:], z_dec[:], 0.0, t_dec[:], ALU.max, ALU.add).then_inc(dec_sp, 1)
            dve.wait_ge(dec_cum, 1)
            zf = z_dec[:, :, :, :].rearrange("p g b h -> p (g b h)")
            V.tensor_tensor(zf, misc[:, 0:NE * H], zf, ALU.add).then_inc(dec_arg, 1)
            dve.wait_ge(ydec_hi, 2)
            for hh in range(2):
                r = slice(hh * DH, (hh + 1) * DH)
                V.tensor_tensor(y_lo[r, :, TP:T], dec_o[r, :, :, hh], y_hi[r, :, TP:T].bitcast(F32), ALU.subtract
                                ).then_inc(ydec_made, 1)

            def mix(name, first, adds):
                with dve.Fori(0, KT // 2) as i:
                    for k in range(2):
                        d = bass.ds(i * 2 + k, 1)
                        u = i * 4 + (first + 2 * k)
                        dve.wait_ge(unit_done, u + 2)
                        dve.wait_ge(ps_free[0], i * 2 + freed(name, 0, k + 1))
                        out = trunk[:, d, :].rearrange("p o t -> p (o t)") if adds is None else gate[k][:, :]
                        V.tensor_tensor(chunks(out), ps[1], chunks(gate[k][:, :]), ALU.mult).then_inc(ps_free[1], 1)
                        split_lo(0, u + 2)
                        split_lo(1, u + 3)
                        if adds is not None:
                            dve.wait_ge(ps_free[1], i * 2 + freed(name, 1, k + 1))
                            V.tensor_tensor(trunk[:, d, :], trunk[:, d, :], gate[k][:, :].unsqueeze(1), ALU.add
                                            ).then_inc(mix_made, 1)

            mix("mixc", U_MIXC, None)
            for g in range(SG):
                dve.wait_ge(y_hi_made, g + 1)
                V.scalar_tensor_tensor(chunks(y_lo[:, g, :]), ps[g % 2], a_scale[:, g:g + 1],
                                       chunks(y_hi[:, g, :]).bitcast(F32), ALU.mult, ALU.subtract
                                       ).then_inc(ps_free[g % 2], 1)
            mix("mixa", U_MIXA, 0)
            with dve.Fori(0, SG // 2) as i:
                for k in range(2):
                    g = bass.ds(i * 2 + k, 1)
                    sv = spat[:, g, :].rearrange("p o (a b) -> p (o a) b", a=NCH)
                    dve.wait_ge(unit_done, i * 2 + (U_U + k + 1))
                    V.tensor_tensor(sv, ps[k], sv, ALU.mult).then_inc(ps_free[k], 1)
                    split_lo(k, i * 2 + (U_U + k + 2))
                    dve.wait_ge(y_hi_made, i * 2 + (SG + k + 1))
                    V.tensor_tensor(y_lo[:, g, :], spat[:, g, :], y_hi[:, g, :].bitcast(F32), ALU.subtract
                                    ).then_inc(yb_made, 1)
            mix("mixb", U_MIXB, KT)
            with dve.Fori(0, KT) as k:
                dve.wait_ge(mhi_made, k + 1)
                V.tensor_tensor(h_lo[:, bass.ds(k, 1), :], trunk[:, bass.ds(k, 1), :],
                                h_hi[:, bass.ds(k, 1), :].bitcast(F32), ALU.subtract).then_inc(m_split, 1)

            dve.wait_ge(out_done, 16 * 3)
            V.memset(ss_acc, 0.0).then_inc(ss_zero, 1)
            dve.wait_ge(ss_zero, 1)
            with dve.Fori(0, KT // 2) as i:
                for k in range(2):
                    dve.wait_ge(ps_free[k], i + freed("out", k, 1))
                    dve.wait_ge(ss_added, i * 2 + (k + 1))
                    V.tensor_tensor(ss_acc, ss_acc, sq, ALU.add).then_inc(ss_added, 1)
                    split_lo(k, i * 2 + (U_OUT + k + 2))

            def rstd_from(n):
                dve.wait_ge(ps_free[0], freed(("ss_m", "ss_x", "ss_f")[n], 0, 1))
                V.reciprocal(rstd, rstd).then_inc(rstd_t, 1)
                if n < 2:
                    V.memset(ss_acc, 0.0).then_inc(ss_zero, 1)

            def add_square(k, before):
                dve.wait_ge(sq_made, before + k + 1)
                dve.wait_ge(ss_added, KT + before + k + 1)
                V.tensor_tensor(ss_acc, ss_acc, sq, ALU.add).then_inc(ss_added, 1)

            rstd_from(0)
            dve.wait_ge(rstd_t, 1)
            dve.wait_ge(ss_zero, 2)
            for k in range(KT):
                V.tensor_tensor(trunk[:, k, :], trunk[:, k, :], rstd, ALU.mult).then_inc(mr_made, 1)
                dve.wait_ge(mr_made, k + 1)
                dve.wait_ge(xt_done, k + 1)
                V.scalar_tensor_tensor(trunk[:, k, :], trunk[:, k, :], g_post[:, k:k + 1],
                                       ps_flat[k % 2][:, 0:T], ALU.mult, ALU.add).then_inc(ps_free[k % 2], 1)
                if k > 0:
                    add_square(k - 1, 0)
            add_square(KT - 1, 0)
            rstd_from(1)
            dve.wait_ge(rstd_t, 2)

            def h2_lo(k):
                dve.wait_ge(hn_hi, k + 1)
                V.scalar_tensor_tensor(h_lo[:, k, :], hn[k % 2][:, :], g_ffn[:, k:k + 1],
                                       h_hi[:, k, :].bitcast(F32), ALU.mult, ALU.subtract).then_inc(h2_made, 1)

            for k in range(KT):
                if k >= 2:
                    dve.wait_ge(h2_made, k - 1)
                V.tensor_tensor(hn[k % 2][:, :], trunk[:, k, :], rstd, ALU.mult).then_inc(hn_made, 1)
                if k > 0:
                    h2_lo(k - 1)
            h2_lo(KT - 1)

            for g, (f0, size) in enumerate(FFN_GROUPS):
                with dve.Fori(0, size) as j:
                    for k in range(2):
                        f = bass.ds(j + (f0 + k * FT), 1)
                        c, x = conv[k], up[k]
                        s0 = j * 8 + (8 * f0 + 4 * k)
                        dve.wait_ge(ps_free[k], j + freed(f"up{g}", k, 1))
                        V.scalar_tensor_tensor(c[:, 1:TP], x[:, 0:TP - 1], conv_par[:, 1, f], c[:, 1:TP],
                                               ALU.mult, ALU.add).then_inc(conv_step, 1)
                        V.scalar_tensor_tensor(c[:, TP:T], conv_st[:, f, :, 1].rearrange("p o b -> p (o b)"),
                                               conv_par[:, 1, f], c[:, TP:T], ALU.mult, ALU.add).then_inc(conv_step, 1)
                        dve.wait_ge(conv_step, s0 + 1)
                        V.scalar_tensor_tensor(c[:, 2:TP], x[:, 0:TP - 2], conv_par[:, 0, f], c[:, 2:TP],
                                               ALU.mult, ALU.add).then_inc(conv_step, 1)
                        dve.wait_ge(conv_step, s0 + 2)
                        V.scalar_tensor_tensor(c[:, TP:T], conv_st[:, f, :, 0].rearrange("p o b -> p (o b)"),
                                               conv_par[:, 0, f], c[:, TP:T], ALU.mult, ALU.add).then_inc(conv_step, 1)
                        split_lo(k, j * 2 + (U_UP[g] + k + 2))
                    dve.wait_ge(gelu_made, j + (f0 + 1))
                    dve.wait_ge(conv_step, j * 8 + (8 * f0 + 8))
                    V.tensor_tensor(conv[0][:, :], conv[0][:, :], conv[1][:, :], ALU.mult).then_inc(gv_made, 1)
                    dve.wait_ge(g_hi_made, j + (f0 + 1))
                    V.tensor_tensor(g_lo[:, bass.ds(j, 1), :].rearrange("p o t -> p (o t)"), conv[0][:, :],
                                    g_hi[:, bass.ds(j, 1), :].rearrange("p o t -> p (o t)").bitcast(F32),
                                    ALU.subtract).then_inc(g_made, 1)
                name = f"down{g}"
                if g > 0:
                    for k in range(2):
                        dve.wait_ge(ps_free[k], freed(f"down{g - 1}", k, KT // 2))
                last_group = g == len(FFN_GROUPS) - 1

                def down(i, split):
                    for k in range(2):
                        if g > 0:
                            t = trunk[:, bass.ds(i * 2 + k, 1), :].rearrange("p o (a b) -> p (o a) b", a=NCH)
                            dve.wait_ge(unit_done, i * 2 + (U_DOWN[g] + k + 1))
                            V.tensor_tensor(t, ps[k], t, ALU.add).then_inc(ps_free[k], 1)
                        if split:
                            split_lo(k, i * 2 + (U_DOWN[g] + k + 2))
                        if last_group:
                            dve.wait_ge(sq_made, i * 2 + (KT + k + 1))
                            dve.wait_ge(ss_added, i * 2 + (2 * KT + k + 1))
                            V.tensor_tensor(ss_acc, ss_acc, sq, ALU.add).then_inc(ss_added, 1)

                if last_group:
                    dve.wait_ge(ss_zero, 3)
                with dve.Fori(0, KT // 2 - last_group) as i:
                    down(i, True)
                if last_group:
                    down(KT // 2 - 1, False)
            rstd_from(2)
            dve.wait_ge(rstd_t, 3)
            for k in range(KT):
                V.tensor_tensor(trunk[:, k, :], trunk[:, k, :], rstd, ALU.mult).then_inc(yr_made, 1)
                dve.wait_ge(yr_made, k + 1)
                if k == 0:
                    dve.wait_ge(x1r_in, 16)
                V.scalar_tensor_tensor(trunk[:, k, :], trunk[:, k, :], g_fpost[:, k:k + 1], x1_back[:, k, :],
                                       ALU.mult, ALU.add).then_inc(yf_made, 1)
            for n in range(NT + 1):
                m = P if n < NT else NS
                dve.wait_ge(yt_ps, n + 1)
                if n >= 4:
                    dve.wait_ge(y_out_done[n % 4], 16 * (n // 4))
                V.tensor_copy(y_tok[0:m, n % 4, 512:D], ps_flat[n % 2][0:m, 512:D]).then_inc(yt_right, 1)

        @block.tensor
        def _(pe):
            M = nc.tensor.matmul

            def T_(out, in_):
                m = in_.shape[0]
                return nc.tensor.transpose(out, in_, ident[0:m, 0:m])

            def unit(u, par, use, xs, ready=None):
                pe.wait_ge(w_lo_made, u + 3)
                pe.wait_ge(ps_free[par], use)
                n = len(xs)
                for k, (x_hi, x_lo) in enumerate(xs):
                    if ready:
                        ready(k)
                    for s, (w, x) in enumerate(((w_lo, x_hi), (w_hi, x_lo), (w_hi, x_hi))):
                        for c in range(NCH):
                            last = M(ps[par][:, c, :], w[par][:, k, :], x[:, c * CH:(c + 1) * CH],
                                     start=(k == 0 and s == 0), stop=(k == n - 1 and s == 2))
                last.then_inc(unit_done, 1)

            hs = [(h_hi[:, k, :], h_lo[:, k, :]) for k in range(KT)]
            ys = [(y_hi[:, k, :], y_lo[:, k, :]) for k in range(BT)]

            pe.wait_ge(consts, NCONST + 4)
            pe.wait_ge(params_in, 16 * NPARAMS)
            T_(misc[:, 0:NORM_COLS], norm_rows[:, :])
            for j in range(4):
                T_(misc[:, NORM_COLS + 2 * FT * j:NORM_COLS + 2 * FT * (j + 1)], conv_rows[:, j, :])
            for f in range(2 * FT):
                at = ST_AT + 2 * NS * f if f < ST0 else 512 + 2 * NS * (f - ST0)
                t = T_(misc[:, at:at + 2 * NS], st_rows[:, f * P:(f + 1) * P])
            t.then_inc(par_ps, 1)
            for n in range(NT + 1):
                m = P if n < NT else NS
                pe.wait_ge(xn_made, n + 1)
                pe.wait_ge(ps_free[n % 2], freed("in", n % 2, n // 2))
                for k in range(KT):
                    t = T_(ps_flat[n % 2][:, k * m:(k + 1) * m], x_tok[0:m, n, k * P:(k + 1) * P])
                t.then_inc(xt_ps, 1)
            pe.wait_ge(par_sb, 3)
            pe.wait_ge(ps_free[1], freed("att", 1, 0))

            with pe.Fori(0, HP) as p:
                def tokens(dst, src, m=T):
                    for n in range(NT):
                        t = T_(dst[:, n * P:(n + 1) * P], src[:, n * P:(n + 1) * P])
                    return t

                unit(p * 4, 0, p * 2 + freed("att", 0, 0), hs)
                unit(p * 4 + 1, 1, p * 2 + freed("att", 1, 0), hs)
                unit(p * 4 + 2, 0, p * 2 + freed("att", 0, 1), hs)
                pe.wait_ge(kf_made, p + 1)
                pe.wait_ge(yc_made, p + 1)
                tokens(misc, k_f).then_inc(ktok_ps, 1)
                unit(p * 4 + 3, 1, p * 2 + freed("att", 1, 1), hs)
                pe.wait_ge(ps_free[0], p * 2 + freed("att", 0, 2))
                pe.wait_ge(ktok_made, p + 1)
                tokens(misc, v_f).then_inc(vtok_ps, 1)
                pe.wait_ge(ps_free[1], p * 2 + freed("att", 1, 2))
                pe.wait_ge(vtok_made, p + 1)
                T_(misc[0:NS, 0:P], q_dec[:, :])
                T_(misc[0:NS, P:2 * P], k_f[:, TP:T])
                T_(misc[0:NS, 2 * P:3 * P], v_f[:, TP:T])
                T_(misc[0:PTAIL, 3 * P:4 * P], a_tail[:, :]).then_inc(small_ps, 1)
                pe.wait_ge(small_made, p * 2 + 2)

                def scores(c):
                    hh, kb, q0, W, top, last = CHUNKS[c]
                    r = slice(hh * DH, (hh + 1) * DH)
                    z = z_bank[c % 6][:, 0:W]
                    for s, (k, q) in enumerate(((k_lo, q_hi), (k_hi, q_lo), (k_hi, q_hi))):
                        t = M(z, k[r, kb * P:(kb + 1) * P], q[r, q0:q0 + W], start=(s == 0), stop=(s == 2),
                              skip_group_check=True)
                    if q0 == kb * P:
                        t = M(z[:, 0:P], ident_b[:, :], mask_b[:, :], start=False, stop=True, skip_group_check=True)
                    t.then_inc(z_ready, 1)

                def softplus_sums(c):
                    hh, kb, q0, W, top, last = CHUNKS[c]
                    z = z_bank[c % 6][:, 0:W]
                    pe.wait_ge(sp_ready, p * NCK + (c + 4))
                    M(z, neg_tri[:, :], sp_lo[c % 3][:, 0:W], start=False, stop=False, skip_group_check=True)
                    t = M(z, neg_tri[:, :], sp_hi[c % 3][:, 0:W], start=False, stop=top, skip_group_check=True)
                    if not top:
                        Wb = CHUNKS[c - 1][3]
                        pe.wait_ge(later_ready, p * NLATER + later_upto[c])
                        t = M(z[:, W - Wb:W], neg_ones[:, :], later[(c - 1) % 4][:, 0:Wb], start=False, stop=True,
                              skip_group_check=True)
                    t.then_inc(cum_ready, 1)

                def values(c):
                    hh, kb, q0, W, top, last = CHUNKS[c]
                    r = slice(hh * DH, (hh + 1) * DH)
                    pe.wait_ge(att_ready, p * NCK + (c + 1))
                    M(misc[r, q0:q0 + W], v_tok[:, kb, r], att[c % 2][:, 0:W], start=top, stop=last,
                      skip_group_check=True).then_inc(pv_done, 1)

                for c in range(NCK + LAG_PV):
                    if c < NCK:
                        scores(c)
                    if LAG_CUM <= c < NCK + LAG_CUM:
                        softplus_sums(c - LAG_CUM)
                    if c >= LAG_PV:
                        values(c - LAG_PV)

            def sg_unit(g):
                unit(U_SG + g, g % 2, freed("sg", g % 2, g // 2), hs)

            def sg_tokens(g):
                pe.wait_ge(ps_free[g % 2], freed("sg", g % 2, g // 2 + 1))
                if g > 0:
                    pe.wait_ge(spat_made, g)
                else:
                    pe.wait_ge(sg_sb, 2)
                for n in range(NT):
                    t = T_(misc[:, n * P:(n + 1) * P], vsg_f[g % 2][:, n * P:(n + 1) * P])
                t.then_inc(vsgtok_ps, 1)

            def sg_mix(g):
                pe.wait_ge(vsgtok_made, g + 1)
                for n in range(NT):
                    M(misc[:, n * P:(n + 1) * P], vsg_tok[:, n, :], sgw_t[:, g, :], start=True, stop=False)
                    t = M(misc[:, n * P:(n + 1) * P], ones[0:1, :], sgb_row[0:1, g * P:(g + 1) * P],
                          start=False, stop=True)
                t.then_inc(mixed_ps, 1)

            sg_unit(0)
            sg_unit(1)
            pe.wait_ge(sgw_masked, SG)
            pe.wait_ge(yc_made, HP + 1)
            pe.wait_ge(st_in, 64)
            for g in range(SG):
                T_(misc[:, g * P:(g + 1) * P], sgw_rows[:, g, :])
                t = T_(misc[:, 512 + g * NS * PB:512 + (g + 1) * NS * PB], sp_rows[:, g * P:(g + 1) * P])
            t.then_inc(sg_ps, 1)
            sg_tokens(0)
            sg_unit(2)
            sg_mix(0)
            sg_tokens(1)
            sg_unit(3)
            sg_mix(1)
            for g in range(2, SG):
                sg_tokens(g)
                sg_mix(g)

            pe.wait_ge(spat_made, SG)
            pe.wait_ge(dec_sp, 1)
            half = NS * H
            sp_d = t_dec[:, :, :, :].rearrange("p g b h -> p (g b h)")
            M(misc[:, 0:NE * H], neg_tri[:, :].bitcast(F32), sp_d, start=True, stop=False, skip_group_check=True)
            M(misc[:, 0:half], neg_ones[:, :], sp_d[:, half:], start=False, stop=True, skip_group_check=True
              ).then_inc(dec_cum, 1)
            pe.wait_ge(dec_arg, 1)
            for g in range(SG):
                t = T_(misc[0:NS, g * P:(g + 1) * P], vsg_dec[:, g, :])
            t.then_inc(sgv_ps, 1)
            pe.wait_ge(dec_att, 1)
            for b in range(NS):
                for pg in range(NPG):
                    n = NE + b * NPG + pg
                    pe.wait_ge(page_in[n % 4], 16 * (n // 4 + 1))
                for hp in range(HP):
                    for pg in range(NPG):
                        t = M(dec_o[:, hp, b, :], kv_pg[:, (b * NPG + pg) % 4, hp * P:(hp + 1) * P],
                              a_dec[:, pg, b, 2 * hp:2 * hp + 2], start=(pg == 0), stop=(pg == NPG - 1))
                t.then_inc(dec_pv, NPG)

            def branch(name, first, y_ready):
                with pe.Fori(0, KT) as d:
                    unit(d * 2 + first, 0, d + freed(name, 0, 0), hs)
                    y_ready()
                    unit(d * 2 + (first + 1), 1, d + freed(name, 1, 0), ys)

            branch("mixc", U_MIXC, lambda: pe.wait_ge(ydec_made, 2))
            for g in range(SG):
                pe.wait_ge(pool_d, 3 * SG)
                pe.wait_ge(ps_free[g % 2], freed("pool", g % 2, g // 2))
                for c in range(NCH):
                    t = M(ps[g % 2][:, c, :], poolw[:, g, :], a_raw[:, g, PAD + c * CH:PAD + (c + 1) * CH],
                          start=True, stop=True)
                t.then_inc(ya_ps, 1)
            branch("mixa", U_MIXA, lambda: [pe.wait_ge(ps_free[k], freed("mixa", k, 0)) for k in range(2)])
            with pe.Fori(0, SG // 2) as i:
                for k in range(2):
                    unit(i * 2 + (U_U + k), k, i + freed("u", k, 0), hs)
            branch("mixb", U_MIXB, lambda: pe.wait_ge(yb_made, SG))

            with pe.Fori(0, KT // 2) as i:
                for k in range(2):
                    unit(i * 2 + (U_OUT + k), k, i + freed("out", k, 0), hs,
                         (lambda kt: pe.wait_ge(m_split, kt + 1)) if k == 0 else None)

            def ss_total(name, n):
                pe.wait_ge(ss_added, KT * (n + 1) + 1)
                pe.wait_ge(ps_free[0], freed(name, 0, 0))
                for c in range(NCH):
                    t = M(ps[0][:, c, :], ones[:, :], ss_acc[:, c * CH:(c + 1) * CH], start=True, stop=True)
                t.then_inc(ss_ps, 1)

            ss_total("ss_m", 0)
            pe.wait_ge(xr_in, 32)
            for k in range(KT):
                pe.wait_ge(ps_free[k % 2], freed("xt", k % 2, k // 2))
                for n in range(NT + 1):
                    m = P if n < NT else NS
                    t = T_(ps_flat[k % 2][:, n * P:n * P + m], xr_tok[0:m, n, k * P:(k + 1) * P])
                t.then_inc(xt_done, 1)
            ss_total("ss_x", 1)

            for g, (f0, size) in enumerate(FFN_GROUPS):
                with pe.Fori(0, size) as j:
                    for k in range(2):
                        unit(j * 2 + (U_UP[g] + k), k, j + freed(f"up{g}", k, 0), hs,
                             (lambda kt: pe.wait_ge(h2_made, kt + 1)) if g == 0 and k == 0 else None)
                gs = [(g_hi[:, k, :], g_lo[:, k, :]) for k in range(size)]
                with pe.Fori(0, KT // 2) as i:
                    for k in range(2):
                        unit(i * 2 + (U_DOWN[g] + k), k, i + freed(f"down{g}", k, 0), gs,
                             (lambda kt: pe.wait_ge(g_made, f0 + kt + 2)) if k == 0 else None)
            ss_total("ss_f", 2)
            for n in range(2 * FT // 4):
                if n >= 2:
                    pe.wait_ge(tail_sb, n - 1)
                for j in range(4):
                    t = T_(misc[0:TAIL, (n % 2) * 512 + j * P:(n % 2) * 512 + (j + 1) * P], tails[:, 4 * n + j, :])
                t.then_inc(tail_ps, 1)
            pe.wait_ge(yf_made, KT)
            pe.wait_ge(ps_free[0], freed("yt", 0, 0))
            pe.wait_ge(ps_free[1], freed("yt", 1, 0))
            for n in range(NT + 1):
                m = P if n < NT else NS
                if n >= 2:
                    pe.wait_ge(yt_left, n - 1)
                    pe.wait_ge(yt_right, n - 1)
                for k in range(KT):
                    t = T_(ps_flat[n % 2][0:m, k * P:(k + 1) * P], trunk[:, k, n * P:n * P + m])
                t.then_inc(yt_ps, 1)


_INS = ["x_prompt", "x_sample", "state_pool", "cache_k", "cache_v", "page_table", "state_conv",
        "norm_mix_pre", "norm_mix_post", "norm_ffn_pre", "norm_ffn_post", "w_in", "pool_w",
        "pool_scale", "sg_w", "sg_b", "sb_bias", "w_branch", "w_out", "w_up", "conv_w", "conv_b",
        "w_down"]


def kernel(**inputs):
    import numpy as np
    import concourse.bacc as bacc
    from concourse.bass_utils import run_bass_kernel_spmd

    nc = bacc.Bacc("TRN2", target_bir_lowering=False, num_devices=1, dynamic_dma_scratch_size=1024)
    arrays = {n: np.ascontiguousarray(inputs[n]) for n in _INS}
    args = [nc.dram_tensor(f"in_{n}", a.shape, mybir.dt.from_np(a.dtype), kind="ExternalInput").ap()
            for n, a in arrays.items()]
    s = {n: a.shape for n, a in arrays.items()}
    depth, dec, heads = s["w_in"][0], s["x_sample"][0], s["sb_bias"][1]
    head_dim = s["cache_k"][4]
    shapes = [s["x_prompt"], s["x_sample"],
              (depth, s["x_prompt"][0]) + s["state_pool"][2:], s["state_pool"],
              *[(depth,) + s["x_prompt"][:2] + (heads, head_dim)] * 2,
              *[(depth,) + s["x_sample"][:2] + (heads, head_dim)] * 2,
              (depth, dec, s["x_sample"][1], s["sg_w"][1] * (s["w_branch"][2] // s["sg_w"][1])),
              (depth, s["x_prompt"][0]) + s["state_conv"][2:], s["state_conv"]]
    outs = [nc.dram_tensor(f"out_{i}", shape, F32, kind="ExternalOutput").ap() for i, shape in enumerate(shapes)]
    build(nc, *args, outs)
    r = run_bass_kernel_spmd(nc, [{f"in_{n}": a for n, a in arrays.items()}], core_ids=[0])
    return tuple(r.results[0][f"out_{i}"] for i in range(len(outs)))
```

```python
from contextlib import ExitStack

import concourse.bass as bass
from concourse import mybir

F32 = mybir.dt.float32
F32R = mybir.dt.float32r
BF16 = mybir.dt.bfloat16
I32 = mybir.dt.int32
ALU = mybir.AluOpType
ACT = mybir.ActivationFunctionType
AX_X = mybir.AxisListType.X

P = 128


def build(nc, x_prompt, x_sample, state_pool, cache_k, cache_v, page_table, state_conv,
          norm_mix_pre, norm_mix_post, norm_ffn_pre, norm_ffn_post, w_in, pool_w, pool_scale,
          sg_w, sg_b, sb_bias, w_branch, w_out, w_up, conv_w, conv_b, w_down, outs):
    (y_prompt, y_sample, pool_prompt, pool_sample, k_prompt, v_prompt, k_sample, v_sample,
     sgv_sample, conv_prompt, conv_sample) = outs

    D = x_prompt.shape[2]
    TP = x_prompt.shape[1]
    NS = x_sample.shape[0]
    T = TP + NS
    NCH = 3
    CH = T // NCH
    KT = D // P
    NT = TP // P
    SG = pool_w.shape[1]
    BT = w_branch.shape[2] // P
    H = sb_bias.shape[1]
    DH = k_prompt.shape[4]
    HP = H // 2
    NPOOL = cache_k.shape[1]
    NPG = page_table.shape[1]
    NE = NS * NPG
    F = w_down.shape[1]
    FT = F // P
    PB = state_pool.shape[2]
    WINDOWS = (2, 4, 8, 16)
    PAD = max(WINDOWS)
    SCALE = DH ** -0.5
    HALF = 512
    TAIL = 2 + NS
    PTAIL = PB + NS
    NEG = -1.0e30
    assert T == NCH * CH and CH % 2 == 0 and CH <= 512 and cache_k.shape[2] == P
    assert DH * 2 == P and BT == SG == HP and x_sample.shape[1] == 1 and NPG == 2

    C_A, C_U, C_V, C_Q, C_K, C_VV, C_G = (n * BT for n in range(7))
    FFN_GROUPS = [(0, 8), (8, 7), (15, 7)]
    assert sum(n for _, n in FFN_GROUPS) == FT

    U_ATT = 0
    U_SG = U_ATT + 4 * HP
    U_MIXC = U_SG + SG
    U_MIXA = U_MIXC + 2 * KT
    U_U = U_MIXA + 2 * KT
    U_MIXB = U_U + SG
    U_OUT = U_MIXB + 2 * KT
    U_UP, U_DOWN = [], []
    n = U_OUT + KT
    for _, size in FFN_GROUPS:
        U_UP.append(n)
        U_DOWN.append(n + 2 * size)
        n += 2 * size + KT
    U_END = n

    USES = {}
    n0 = n1 = 0
    for name, a, b in ([("att", 2 * HP, HP), ("sg", 2, 2), ("mixc", KT, KT),
                        ("pool", 2, 2), ("mixa", KT, KT), ("u", 2, 2), ("mixb", KT, KT),
                        ("out", KT // 2, KT // 2), ("ss_m", 1, 0), ("xt", KT // 2, KT // 2),
                        ("ss_x", 1, 0)]
                       + [x for g, (_, size) in enumerate(FFN_GROUPS)
                          for x in ((f"up{g}", size, size), (f"down{g}", KT // 2, KT // 2))]
                       + [("ss_f", 1, 0), ("yt", 5, 4)]):
        USES[name] = (n0, n1)
        n0, n1 = n0 + a, n1 + b

    def freed(stage, par, k):
        return k + (USES[stage][par] + 1)

    CHUNKS = []
    for hh in range(2):
        for half in reversed(range(TP // HALF)):
            top = (half + 1) * HALF // P - 1
            for kb in reversed(range(top + 1)):
                q0 = max(kb * P, half * HALF)
                CHUNKS.append((hh, kb, q0, (half + 1) * HALF - q0, kb == top, kb == 0))
    NCK = len(CHUNKS)
    later_upto = [0]
    for n, (_, _, _, W, top, last) in enumerate(CHUNKS):
        wider = not top and W > CHUNKS[n - 1][3]
        later_upto.append(later_upto[-1] + (0 if last else 1 + wider))
    NLATER = later_upto[NCK]
    assert NCK % 12 == 0
    LAG_CUM, LAG_PV, LAG_EXP = 3, 5, 4
    NEXT_SPLITS = (3, 18)
    A_STEPS = [(0, 2), (4, 9), (11, 16)]
    SMALL_STEP = 18

    ctx = ExitStack()
    with ctx:
        def sb(name, shape, dt=F32, scope=ctx):
            return scope.enter_context(nc.sbuf_tensor(name, shape, dt))

        h_hi = sb("h_hi", [P, KT, T], F32R)
        h_lo = sb("h_lo", [P, KT, T], F32R)
        stage = [sb(f"stage{i}", [P, KT, P]) for i in range(2)]
        w_hi = [sb(f"w_hi{i}", [P, KT, P], F32R) for i in range(2)]
        w_lo = [sb(f"w_lo{i}", [P, KT, P], F32R) for i in range(2)]
        ident = sb("ident", [P, P])
        ones = sb("ones", [P, P])
        neg_ones = sb("neg_ones", [P, P])
        neg_tri = sb("neg_tri", [P, P], F32R)
        ident_b = sb("ident_b", [P, P], BF16)
        mask_b = sb("mask_b", [P, P], BF16)
        NORM_COLS = 3 * KT + SG
        par_t = sb("par_t", [P, NORM_COLS + 4 * 2 * FT])
        g_post, g_ffn, g_fpost = (par_t[:, n * KT:(n + 1) * KT] for n in range(3))
        a_scale = par_t[:, 3 * KT:NORM_COLS]
        conv_par = par_t[:, NORM_COLS:].rearrange("p (j f) -> p j f", j=4)
        bias_h = sb("bias_h", [P, H])
        bias_p = sb("bias_p", [P, 2])
        nbias_p = sb("nbias_p", [P, 2])
        w00 = sb("w00", [P, SG])
        b0 = sb("b0", [P, SG])
        conv_st = sb("conv_st", [P, 2 * FT, NS, 2])
        tails = sb("tails", [P, 2 * FT, TAIL])
        inv_cnt = sb("inv_cnt", [P, PB])
        edge = sb("edge", [P, PB])
        pre = sb("pre", [P, NS])
        eps = sb("eps", [P, 1])
        ss = sb("ss", [P, NT + 1])
        std = sb("std", [P, NT + 1])
        rs = sb("rs", [P, NT + 1])
        work = [sb(f"work{i}", [P, PAD + TP]) for i in range(3)]
        rstd, ss_acc, sq = (w[:, 0:T] for w in work)
        sgv_tok = work[1][0:NS, 0:SG * P]
        win = work[0:2]
        small_tok = work[0][0:PTAIL, 0:4 * P].rearrange("p (a b) -> p a b", a=4)

        s_in = ExitStack()
        x_tok = sb("x_tok", [P, NT + 1, D], F32, s_in)
        g_pre = sb("g_pre", [P, D], F32, s_in)
        st_rows = sb("st_rows", [NS * 2, 2 * F], F32, s_in)
        norm_rows = sb("norm_rows", [NORM_COLS, P], F32, s_in)
        conv_rows = sb("conv_rows", [2 * FT, 4, P], F32, s_in)
        s_in.close()

        s_pair = ExitStack()
        q_hi, q_lo, k_hi, k_lo = (sb(n, [P, T], F32R, s_pair) for n in ("q_hi", "q_lo", "k_hi", "k_lo"))
        k_f, v_f = (sb(n, [P, T], F32, s_pair) for n in ("k_f", "v_f"))
        k_tok, v_tok = (sb(n, [P, NT, P], F32, s_pair) for n in ("k_tok", "v_tok"))
        s_pair.close()
        s_dec = ExitStack()
        q_bc = sb("q_bc", [P, 4, HP * P], F32, s_dec)
        kv_pg = sb("kv_pg", [P, 4, HP * P], F32, s_dec)
        kq = sb("kq", [P, HP * P], F32, s_dec)
        sp_rows = sb("sp_rows", [NS * PB, SG * P], F32, s_dec)
        sgw_rows = sb("sgw_rows", [P, SG, P], F32, s_dec)
        vsg_tok = sb("vsg_tok", [P, NT, P], F32, s_dec)
        z_dec, t_dec = (sb(n, [P, NPG, NS, H], F32, s_dec) for n in ("z_dec", "t_dec"))
        A_STEP = NS * H + 1
        a_pad = q_bc[:, :, :].rearrange("p a b -> p (a b)")[:, 0:NPG * NS * A_STEP]
        a_dec = a_pad.rearrange("p (g b x) -> p g b x", g=NPG, b=NS)[:, :, :, 0:NS * H].rearrange(
            "p g b (h y) -> p g b h y", h=H)[:, :, :, :, 0]
        own = sp_rows[0:NS * H, :]
        own_rows = kq[0:NS * H, :]
        pick = sb("pick", [NS * H, NS], F32, s_dec)
        s_dec.close()
        trunk = sb("trunk", [P, KT, T])

        s_mix = ExitStack()
        y_hi = sb("y_hi", [P, BT, T], F32R, s_mix)
        y_lo = sb("y_lo", [P, BT, T], F32R, s_mix)
        a_raw = sb("a_raw", [P, SG, PAD + T], F32, s_mix)
        s_att = ExitStack()
        zl = [sb(f"zl{i}", [P, HALF], F32, s_att) for i in range(4)]
        sp_hi = [sb(f"sp_hi{i}", [P, HALF], F32R, s_att) for i in range(3)]
        sp_lo = [sb(f"sp_lo{i}", [P, HALF], F32R, s_att) for i in range(3)]
        later = [sb(f"later{i}", [P, HALF], F32, s_att) for i in range(4)]
        att = [sb(f"att{i}", [P, HALF], F32, s_att) for i in range(2)]
        q_dec = sb("q_dec", [P, NS], F32, s_att)
        a_tail = sb("a_tail", [P, PTAIL], F32, s_att)
        s_att.close()
        spat = sb("spat", [P, SG, T], F32, s_mix)
        pool_st = sb("pool_st", [P, SG, NS * PB], F32, s_mix)
        sgw_t = sb("sgw_t", [P, SG, P], F32, s_mix)
        sgb_row = sb("sgb_row", [1, SG * P], F32, s_mix)
        poolw = sb("poolw", [P, SG, P], F32, s_mix)
        s_sg = ExitStack()
        vsg_dec = sb("vsg_dec", [P, SG, NS], F32, s_sg)
        pt_sb = sb("pt_sb", [1, NE], I32, s_sg)
        vsg_f = [work[2][:, 0:T], sb("vsg_f1", [P, T], F32, s_sg)[:, :]]
        s_sg.close()
        s_gate = ExitStack()
        gate = [sb(f"gate{i}", [P, T], F32, s_gate) for i in range(2)]
        s_gate.close()
        s_mix.close()
        s_res = ExitStack()
        xr_tok = sb("xr_tok", [P, NT + 1, D], F32, s_res)
        hn = [sb(f"hn{i}", [P, T], F32, s_res) for i in range(2)]
        s_res.close()
        s_ffn = ExitStack()
        GMAX = max(n for _, n in FFN_GROUPS)
        g_hi = sb("g_hi", [P, GMAX, T], F32R, s_ffn)
        g_lo = sb("g_lo", [P, GMAX, T], F32R, s_ffn)
        up = [sb(f"up{i}", [P, T], F32, s_ffn) for i in range(2)]
        conv = [sb(f"conv{i}", [P, T], F32, s_ffn) for i in range(2)]
        s_ffn.close()
        x1_back = sb("x1_back", [P, KT, T])
        y_tok = sb("y_tok", [P, 4, D])

        ps_all = [ctx.enter_context(nc.psum_tensor(f"ps{i}", [P, NCH, 512], F32)) for i in range(2)]
        misc_t = ctx.enter_context(nc.psum_tensor("misc", [P, 2 * 512], F32))
        ps = [t[:, :, 0:CH] for t in ps_all]
        ps_flat = [t[:, :, :].rearrange("p a b -> p (a b)") for t in ps_all]
        misc = misc_t[:, :]
        banks = [ps_all[i // NCH][:, i % NCH, :] for i in range(2 * NCH)]
        NZ = 5
        in_ps = [misc, ps_flat[1][:, 0:D]]
        z_bank = [banks[(c + (NZ - NCK) % NZ) % NZ] for c in range(NCK)]
        a_bank = banks[NZ]
        DEC0 = TP - (NCH - 1) * CH

        def chunks(ap):
            return ap.rearrange("p (a b) -> p a b", a=NCH)

        def last_cols(par, n):
            return ps_all[par][:, NCH - 1, CH - n:CH]

        x1_dram = nc.dram_tensor("x1_scratch", [P, KT, T], F32, kind="Internal").ap()
        q_dram = nc.dram_tensor("q_scratch", [NS, HP * P], F32, kind="Internal").ap()

        win_v, wout_v, wup_v, wdn_v = (w.rearrange("o (k p) n -> p (o k) n", p=P)
                                       for w in (w_in, w_out, w_up, w_down))
        wbr_v = w_branch.rearrange("o b (k p) n -> p (o b) k n", p=P)

        sems = {}

        def sem(name):
            if name not in sems:
                sems[name] = ctx.enter_context(nc.semaphore(name))
            return sems[name]

        w_landed = [sem("w_landed0"), sem("w_landed1")]
        ps_free = [sem("ps_free0"), sem("ps_free1")]
        tail_out = [sem("tail_out0"), sem("tail_out1")]
        y_out_done = [sem(f"y_out_done{i}") for i in range(4)]
        page_in = [sem(f"page_in{i}") for i in range(4)]
        qbc_in = [sem(f"qbc_in{i}") for i in range(4)]
        x_in = [sem(f"x_in{i}") for i in range(5)]
        in_free = [sem("in_free0"), sem("in_free1")]
        (params_in, gpre_in, consts, par_ps, par_sb, ss_made, std_made, rs_made, xn_made, xt_ps, h_hi_made,
         w_hi_made, w_lo_made, unit_done, biasp_made, q_hi_made, kf_made, k_hi_made, ktok_ps,
         ktok_made, vtok_ps, vtok_made, small_ps, small_made, tok_out, z_ready, abs_made, e_made,
         l_ready, spn_ready, hi_ready, sp_ready, later_ready, cum_ready, att_ready,
         pv_done, yc_hi_made, yc_made) = (sem(n) for n in (
             "params_in", "gpre_in", "consts", "par_ps", "par_sb", "ss_made", "std_made", "rs_made",
             "xn_made", "xt_ps", "h_hi_made", "w_hi_made", "w_lo_made", "unit_done",
             "biasp_made", "q_hi_made", "kf_made", "k_hi_made", "ktok_ps", "ktok_made", "vtok_ps",
             "vtok_made", "small_ps", "small_made", "tok_out", "z_ready", "abs_made", "e_made",
             "l_ready", "spn_ready", "hi_ready", "sp_ready", "later_ready",
             "cum_ready", "att_ready", "pv_done", "yc_hi_made", "yc_made"))
        pad_zero, own_mask, own_made, dec_o_ps = (sem(n) for n in ("pad_zero", "own_mask", "own_made", "dec_o_ps"))
        a_ps, a_out, tail_cols = sem("a_ps"), sem("a_out"), sem("tail_cols")
        (st_in, pt_in, sgw_masked, sg_ps, sg_sb, vsgtok_ps, vsgtok_made, mixed_ps, spat_made,
         kq_made, zd_made, zb_made, dec_abs, dec_e, dec_l, dec_sp, dec_cum, dec_arg, dec_att, dec_pv,
         ydec_hi, ydec_made, sgv_ps, sgv_sb, pads_made, win_step, pool_edge, pool_pre,
         pool_d) = (
             sem(n) for n in (
                 "st_in", "pt_in", "sgw_masked", "sg_ps", "sg_sb", "vsgtok_ps", "vsgtok_made",
                 "mixed_ps", "spat_made", "kq_made", "zd_made", "zb_made", "dec_abs", "dec_e", "dec_l",
                 "dec_sp", "dec_cum", "dec_arg", "dec_att", "dec_pv", "ydec_hi", "ydec_made",
                 "sgv_ps", "sgv_sb", "pads_made", "win_step", "pool_edge", "pool_pre",
                 "pool_d"))
        (ya_ps, y_hi_made, y_made, gated, mix_made, yb_made, mhi_made, m_split, sq_made, ss_added,
         ss_ps, std_t, rstd_t, xr_in, xt_done, mr_made, x1_made, hn_made, hn_hi, h2_made, x1_out,
         conv_step, gelu_made, gv_made, g_hi_made, g_made, acc_made, tail_ps, tail_sb,
         x1r_in, yr_made, yf_made, yt_ps, yt_left, yt_right, hi_begun, out_done, ss_zero) = (
             sem(n) for n in (
                 "ya_ps", "y_hi_made", "y_made", "gated", "mix_made", "yb_made", "mhi_made",
                 "m_split", "sq_made", "ss_added", "ss_ps", "std_t", "rstd_t", "xr_in",
                 "xt_done", "mr_made", "x1_made", "hn_made", "hn_hi", "h2_made", "x1_out",
                 "conv_step", "gelu_made", "gv_made", "g_hi_made", "g_made",
                 "acc_made", "tail_ps", "tail_sb", "x1r_in", "yr_made", "yf_made",
                 "yt_ps", "yt_left", "yt_right", "hi_begun", "out_done", "ss_zero"))
        BEGIN = [(ps_free[0], 1), (ps_free[1], 1), (w_lo_made, 2), (sp_ready, 3), (cum_ready, 3),
                 (pv_done, 2), (tok_out, 16), (yc_made, 1), (small_made, 2), (mix_made, 2), (g_made, 1),
                 (ss_added, 1), (ss_made, 1)]
        TOK_DMAS = 7
        NCONST = 5 + PB
        NPARAMS = 10
        IN_BATCHES = [range(n, min(n + 2, NT + 1)) if n < NT else range(NT, NT + 1) for n in range(0, NT + 1, 2)]
        PAR_COLS = NORM_COLS + 4 * 2 * FT
        ST_AT = 212
        ST0 = (512 - ST_AT) // (2 * NS)
        LAST_DOWN = f"down{len(FFN_GROUPS) - 1}"
        dec_sums = banks[3][:, 0:NE * H]
        dec_rows = misc[0:NS * H, 0:HP * P]
        dec_o = misc[:, 512:512 + HP * NS].rearrange("p (a b) -> p a b", a=HP)

        block = ctx.enter_context(nc.Block())

        @block.sync
        def _(sp):
            for s, n in BEGIN:
                sp.sem_inc(s, n)

            def fetch(u, par, src):
                sp.wait_ge(w_lo_made, u + 1)
                sp.dma_start(stage[par][:, 0:src.shape[1], :], src).then_inc(w_landed[par], 16)

            def col(v, c):
                return v[:, :, bass.ds(c * P, P)]

            def mix_tiles(d, first, branch):
                fetch(d * 2 + first, 0, col(win_v, d + (C_G + branch * KT)))
                fetch(d * 2 + (first + 1), 1, wbr_v[:, branch, :, bass.ds(d * P, P)])

            def fetch_mix(first, branch, begin=0):
                with sp.Fori(begin, KT) as d:
                    mix_tiles(d, first, branch)

            for n in range(NT):
                sp.dma_start(x_tok[:, n, :], x_prompt[0, n * P:(n + 1) * P, :]).then_inc(x_in[n // 2], 16)
                if n == 1:
                    fetch(0, 0, col(win_v, C_Q))
            sp.dma_start(x_tok[0:NS, NT, :], x_sample.rearrange("b t d -> (b t) d")).then_inc(x_in[NT // 2], 16)
            fetch(1, 1, col(win_v, C_K))
            rows = [(norm_rows[n * KT:(n + 1) * KT, :], v.rearrange("o (k p) -> (o k) p", p=P))
                    for n, v in enumerate((norm_mix_post, norm_ffn_pre, norm_ffn_post))]
            rows += [(norm_rows[3 * KT:NORM_COLS, :], pool_scale.rearrange("o (k p) -> (o k) p", p=P)),
                     (conv_rows[:, 0:3, :], conv_w.rearrange("o j (f p) -> f (o j) p", p=P)),
                     (conv_rows[:, 3, :], conv_b.rearrange("o (f p) -> (o f) p", p=P)),
                     (st_rows[:, :], state_conv.rearrange("o b j c -> (o b j) c")),
                     (bias_h[:, :], sb_bias[0, :].partition_broadcast(P))]
            for dst, src in rows:
                sp.dma_start(dst, src).then_inc(params_in, 16)
            with nc.allow_non_contiguous_dma(reason="one element of each group"):
                sp.dma_start(w00[:, :], sg_w[0, :, 0, 0].partition_broadcast(P)).then_inc(params_in, 16)
                sp.dma_start(b0[:, :], sg_b[0, :, 0].partition_broadcast(P)).then_inc(params_in, 16)
            sp.dma_start(pool_sample[0, :, 0:PB - 1, :], state_pool[0, :, 1:PB, :]).then_inc(out_done, 16)
            sp.dma_start(conv_sample[0, :, 0, :], state_conv[0, :, 1, :]).then_inc(out_done, 16)

            def store_pair(p):
                sp.wait_ge(ktok_made, p + 1)
                sp.dma_start(k_prompt[0, 0, :, bass.ds(p * 2, 2), :].rearrange("(n q) h d -> q n (h d)", q=P),
                             k_tok[:, :, :]).then_inc(tok_out, 16)
                sp.wait_ge(vtok_made, p + 1)
                sp.dma_start(v_prompt[0, 0, :, bass.ds(p * 2, 2), :].rearrange("(n q) h d -> q n (h d)", q=P),
                             v_tok[:, :, :]).then_inc(tok_out, 16)
                sp.wait_ge(small_made, p * 2 + 4)
                sp.dma_start(q_dram[:, bass.ds(p * P, P)], small_tok[0:NS, 0, :]).then_inc(tok_out, 16)
                for j, dst in ((1, k_sample), (2, v_sample)):
                    sp.dma_start(dst[0, :, 0, bass.ds(p * 2, 2), :].rearrange("b h d -> b (h d)"),
                                 small_tok[0:NS, j, :]).then_inc(tok_out, 16)
                sp.dma_start(pool_prompt[0, 0, :, bass.ds(p * P, P)], small_tok[0:PB, 3, :]).then_inc(tok_out, 16)
                sp.dma_start(pool_sample[0, :, PB - 1, bass.ds(p * P, P)],
                             small_tok[PB:PTAIL, 3, :]).then_inc(tok_out, 16)

            with sp.Fori(0, HP - 1) as p:
                for j, c in ((2, C_VV), (3, C_A), (4, C_Q + 1), (5, C_K + 1)):
                    fetch(p * 4 + j, j % 2, col(win_v, p + c))
                store_pair(p)
            fetch(U_SG - 2, 0, col(win_v, C_VV + HP - 1))
            fetch(U_SG - 1, 1, col(win_v, C_A + HP - 1))
            for g in range(2):
                fetch(U_SG + g, g, col(win_v, C_V + g))
            store_pair(HP - 1)
            for g in range(2, SG):
                fetch(U_SG + g, g % 2, col(win_v, C_V + g))
            sp.wait_ge(yc_made, HP + 1)
            sp.wait_ge(tok_out, 16 * (TOK_DMAS * HP + 1))
            sp.dma_start(sp_rows[:, :], state_pool.rearrange("o b j c -> (o b j) c")).then_inc(st_in, 16)
            sp.dma_start(sgw_rows[:, :, :], sg_w.rearrange("o g t s -> t (o g) s")).then_inc(st_in, 16)
            sp.dma_start(sgb_row[:, :], sg_b.rearrange("o g t -> o (g t)")).then_inc(st_in, 16)
            sp.dma_start(poolw[:, :, :], pool_w.rearrange("o g c d -> c (o g) d")).then_inc(st_in, 16)
            sp.dma_start(pt_sb[:, :], page_table.rearrange("(o b) j -> o (b j)", o=1)).then_inc(pt_in, 16)
            sp.wait_ge(pt_in, 16)
            for which, cache in enumerate((cache_k, cache_v)):
                for e in range(NE):
                    n = which * NE + e
                    if 4 <= n < NE + 4:
                        sp.wait_ge(kq_made, n - 3)
                    elif n >= NE + 4:
                        sp.wait_ge(dec_pv, n - 3 - NE)
                    if which == 0 and e % NPG == 0:
                        b = e // NPG
                        if b >= 4:
                            sp.wait_ge(kq_made, (b - 3) * NPG)
                        sp.dma_start(q_bc[:, b % 4, :], q_dram[b, :].partition_broadcast(P)
                                     ).then_inc(qbc_in[b % 4], 16)
                    page = sp.value_load(pt_sb[0:1, e:e + 1], min_val=0, max_val=NPOOL - 1)
                    sp.dma_start(kv_pg[:, n % 4, :],
                                 cache[0, bass.ds(page, 1), :, :, :].rearrange("o t h d -> (o t) (h d)")
                                 ).then_inc(page_in[n % 4], 16)
                    if n == NE // 2:
                        mix_tiles(0, U_MIXC, 2)
            fetch_mix(U_MIXC, 2, 1)
            sp.wait_ge(sgv_sb, 1)
            sp.dma_start(sgv_sample[0, :, 0, :], sgv_tok[:, :]).then_inc(out_done, 16)
            fetch_mix(U_MIXA, 0)
            with sp.Fori(0, SG // 2) as i:
                for j in range(2):
                    fetch(i * 2 + (U_U + j), j, col(win_v, i * 2 + (C_U + j)))
            fetch_mix(U_MIXB, 1)
            with sp.Fori(0, KT // 2) as i:
                for j in range(2):
                    fetch(i * 2 + (U_OUT + j), j, col(wout_v, i * 2 + j))
            sp.wait_ge(m_split, KT)
            sp.dma_start(xr_tok[:, 0:NT, :], x_prompt.rearrange("o (n q) d -> q (o n) d", q=P)).then_inc(xr_in, 16)
            sp.dma_start(xr_tok[0:NS, NT, :], x_sample.rearrange("b t d -> (b t) d")).then_inc(xr_in, 16)
            for g, (f0, size) in enumerate(FFN_GROUPS):
                def up_tiles(j):
                    fetch(j * 2 + U_UP[g], 0, col(wup_v, j + f0))
                    fetch(j * 2 + (U_UP[g] + 1), 1, col(wup_v, j + (f0 + FT)))
                if g == 0:
                    up_tiles(0)
                    for par in range(2):
                        sp.wait_ge(ps_free[par], freed("xt", par, KT // 2))
                    sp.dma_start(x1_dram, trunk[:, :, :]).then_inc(x1_out, 16)
                with sp.Fori(1 if g == 0 else 0, size) as j:
                    up_tiles(j)
                with sp.Fori(0, KT // 2) as i:
                    for j in range(2):
                        fetch(i * 2 + (U_DOWN[g] + j), j,
                              wdn_v[:, f0:f0 + size, bass.ds((i * 2 + j) * P, P)])
            sp.wait_ge(unit_done, U_END)
            sp.wait_ge(x1_out, 16)
            sp.dma_start(x1_back[:, :, :], x1_dram).then_inc(x1r_in, 16)
            for n in range(2 * FT // 4):
                sp.wait_ge(tail_sb, n + 1)
                rows = up[n % 2][0:TAIL, 0:4 * P]
                sp.dma_start(conv_prompt[0, 0, :, n * 4 * P:(n + 1) * 4 * P], rows[0:2, :]).then_inc(tail_out[n % 2], 16)
                sp.dma_start(conv_sample[0, :, 1, n * 4 * P:(n + 1) * 4 * P], rows[2:TAIL, :]).then_inc(tail_out[n % 2], 16)
            for n in range(NT):
                sp.wait_ge(yt_left, n + 1)
                sp.wait_ge(yt_right, n + 1)
                sp.dma_start(y_prompt[0, n * P:(n + 1) * P, :], y_tok[:, n % 4, :]).then_inc(y_out_done[n % 4], 16)
            sp.wait_ge(yt_left, NT + 1)
            sp.wait_ge(yt_right, NT + 1)
            sp.dma_start(y_sample.rearrange("b t d -> (b t) d"), y_tok[0:NS, NT % 4, :]).then_inc(y_out_done[NT % 4], 16)
            for k in range(4):
                sp.wait_ge(y_out_done[k], 16 * ((NT + 4 - k) // 4))
            sp.wait_ge(out_done, 16 * 3)
            for k in range(2):
                sp.wait_ge(tail_out[k], 32 * ((2 * FT // 4 + 1 - k) // 2))
            sp.wait_ge(tok_out, 16 * (TOK_DMAS * HP + 1))

        @block.gpsimd
        def _(pool):
            def split_hi(par, n16, u):
                pool.wait_ge(w_landed[par], n16)
                if u is not None:
                    pool.wait_ge(unit_done, u - 1)
                    pool.sem_inc(hi_begun, 1)
                nc.gpsimd.tensor_scalar(w_hi[par][:, :, :], stage[par][:, :, :], 1.0, 0.0,
                                        ALU.mult, ALU.add).then_inc(w_hi_made, 1)

            def split_stage(first, count):
                with pool.Fori(0, count // 2) as i:
                    for j in range(2):
                        split_hi(j, i * 16 + 16 * (first // 2 + 2), i * 2 + (first + 2 + j))

            nc.gpsimd.memset(ident[:, :], 0.0).then_inc(consts, 1)
            nc.gpsimd.memset(ones[:, :], 1.0).then_inc(consts, 1)
            nc.gpsimd.memset(neg_ones[:, :], -1.0).then_inc(consts, 1)
            nc.gpsimd.memset(mask_b[:, :], NEG).then_inc(consts, 1)
            nc.gpsimd.memset(eps[:, :], 1e-6).then_inc(consts, 1)
            for t in range(PB):
                nc.gpsimd.memset(inv_cnt[:, t:t + 1], 1.0 / (t + 1)).then_inc(consts, 1)
            pool.wait_ge(consts, NCONST)
            nc.gpsimd.affine_select(out=ident[:, :], in_=ident[:, :], compare_op=ALU.not_equal, fill=1.0,
                                    base=0, pattern=[[-1, P]], channel_multiplier=1).then_inc(consts, 1)
            nc.gpsimd.affine_select(out=neg_tri[:, :], in_=neg_ones[:, :], compare_op=ALU.is_ge, fill=0.0,
                                    base=0, pattern=[[-1, P]], channel_multiplier=1).then_inc(consts, 1)
            nc.gpsimd.affine_select(out=mask_b[:, :], in_=mask_b[:, :], compare_op=ALU.is_ge, fill=0.0,
                                    base=0, pattern=[[-1, P]], channel_multiplier=1).then_inc(consts, 1)
            pool.wait_ge(consts, NCONST + 1)
            nc.gpsimd.tensor_copy(ident_b[:, :], ident[:, :]).then_inc(consts, 1)
            split_hi(0, 16, None)
            split_hi(1, 16, None)
            with pool.Fori(0, HP) as p:
                for j in range(2):
                    split_hi(j, p * 32 + 32, p * 4 + (2 + j))
                for c, (hh, kb, q0, W, top, last) in enumerate(CHUNKS):
                    if c in NEXT_SPLITS:
                        j = NEXT_SPLITS.index(c)
                        split_hi(j, p * 32 + 48, p * 4 + (4 + j))
                    pool.wait_ge(spn_ready, p * NCK + (c + 1))
                    pool.wait_ge(cum_ready, p * NCK + (c + 1))
                    pool.sem_inc(hi_begun, 1)
                    nc.gpsimd.tensor_scalar(sp_hi[c % 3][:, 0:W], zl[c % 4][:, 0:W], bias_p[:, hh:hh + 1], 1.0,
                                            ALU.add, ALU.mult).then_inc(hi_ready, 1)
            pool.wait_ge(yc_made, HP + 1)
            pool.wait_ge(tok_out, 16 * (TOK_DMAS * HP + 1))
            nc.gpsimd.memset(a_raw[:, :, 0:PAD], 0.0).then_inc(pads_made, 1)
            for w in win:
                nc.gpsimd.memset(w[:, 0:PAD], 0.0).then_inc(pads_made, 1)
            pool.wait_ge(st_in, 64)
            for g in range(SG):
                nc.gpsimd.affine_select(out=sgw_rows[:, g, :], in_=sgw_rows[:, g, :], compare_op=ALU.is_ge,
                                        fill=0.0, base=0, pattern=[[-1, P]], channel_multiplier=1
                                        ).then_inc(sgw_masked, 1)
            pool.wait_ge(pads_made, 3)
            step = 0
            for g in range(SG):
                split_hi(g % 2, 16 * (U_SG // 2 + 2 + g // 2), U_SG + 2 + g)
                src = a_raw[:, g, 0:PAD + TP]
                for m in range(g + 1):
                    if g > 0 and m == 0:
                        pool.wait_ge(pool_d, 3 * g)
                    if m > 0:
                        pool.wait_ge(win_step, step)
                    dst = win[m % 2]
                    nc.gpsimd.tensor_tensor(dst[:, PAD:PAD + TP], src[:, PAD:PAD + TP],
                                            src[:, PAD - 2 ** m:PAD + TP - 2 ** m], ALU.add
                                            ).then_inc(win_step, 1)
                    step += 1
                    src = dst
            pool.wait_ge(sg_ps, 1)
            own3 = own.rearrange("p (h d) -> p h d", h=H)
            nc.gpsimd.memset(own, 1.0).then_inc(own_mask, 1)
            for i, (row, head, base) in enumerate(((1, -NS, 0), (-1, NS, NS - 1))):
                pool.wait_ge(own_mask, i + 1)
                nc.gpsimd.affine_select(out=own3, in_=own3, compare_op=ALU.is_ge, fill=0.0, base=base,
                                        pattern=[[head, H], [0, DH]], channel_multiplier=row).then_inc(own_mask, 1)
            pool.wait_ge(zd_made, NE)
            nc.gpsimd.memset(a_pad, 0.0).then_inc(pad_zero, 1)
            split_stage(U_MIXC, U_END - 2 - U_MIXC)

        @block.scalar
        def _(act):
            A = nc.scalar.activation

            act.preload_act_table_set("sqrt_and_others")
            act.dma_start(g_pre[:, :], norm_mix_pre[0, :].partition_broadcast(P)).then_inc(gpre_in, 16)

            act.wait_ge(consts, NCONST + 4)
            for b in range(len(IN_BATCHES) + 1):
                if b < len(IN_BATCHES):
                    tiles = IN_BATCHES[b]
                    n0_, n1_ = tiles[0], tiles[-1] + 1
                    m = P if n0_ < NT else NS
                    act.wait_ge(x_in[b], 16 * len(tiles))
                    for n in tiles:
                        act.wait_ge(ss_made, n + 1)
                        A(sq[0:m, 0:D], x_tok[0:m, n, :], ACT.Square, accum_out=ss[0:m, n:n + 1]).then_inc(ss_made, 1)
                    act.wait_ge(ss_made, n1_ + 1)
                    A(std[0:m, n0_:n1_], ss[0:m, n0_:n1_], ACT.Sqrt, bias=eps[0:m, :], scale=1.0 / D
                      ).then_inc(std_made, 1)
                for n in (IN_BATCHES[b - 1] if b > 0 else []):
                    m = P if n < NT else NS
                    act.wait_ge(xt_ps, n + 1)
                    A(h_hi[:, :, n * P:n * P + m],
                      in_ps[n % 2][:, 0:KT * m].rearrange("p (k t) -> p k t", k=KT), ACT.Copy).then_inc(h_hi_made, 1)
            act.wait_ge(par_ps, 1)
            A(par_t[:, :], misc[:, 0:PAR_COLS], ACT.Copy).then_inc(par_sb, 1)
            A(conv_st[:, 0:ST0, :, :].rearrange("p f b j -> p (f b j)"),
              misc[:, ST_AT:ST_AT + ST0 * 2 * NS], ACT.Copy).then_inc(par_sb, 1)
            A(conv_st[:, ST0:, :, :].rearrange("p f b j -> p (f b j)"),
              misc[:, 512:512 + (2 * FT - ST0) * 2 * NS], ACT.Copy).then_inc(par_sb, 1)

            act.preload_act_table_set("natural_log_exp_and_others")
            with act.Fori(0, HP) as p:
                act.wait_ge(unit_done, p * 4 + 1)
                A(q_dec[:, :], last_cols(0, NS), ACT.Copy, scale=SCALE)
                A(chunks(q_hi[:, :]), ps[0], ACT.Copy, scale=SCALE).then_inc(q_hi_made, 1)
                act.wait_ge(unit_done, p * 4 + 2)
                A(chunks(k_f[:, :]), ps[1], ACT.Copy).then_inc(kf_made, 1)
                A(chunks(k_hi[:, :]), ps[1], ACT.Copy).then_inc(k_hi_made, 1)
                act.wait_ge(unit_done, p * 4 + 3)
                A(chunks(v_f[:, :]), ps[0], ACT.Copy).then_inc(ps_free[0], 1)
                act.wait_ge(biasp_made, p * 2 + 2)

                def soft_abs(c):
                    hh, kb, q0, W, top, last = CHUNKS[c]
                    act.wait_ge(z_ready, p * NCK + (c + 1))
                    act.wait_ge(sp_ready, p * NCK + (c + 1))
                    A(zl[c % 4][:, 0:W], z_bank[c][:, 0:W], ACT.Abs, bias=bias_p[:, hh:hh + 1]).then_inc(abs_made, 1)

                def soft_exp(c):
                    t = zl[c % 4][:, 0:CHUNKS[c][3]]
                    act.wait_ge(abs_made, p * NCK + (c + 1))
                    A(t, t, ACT.Exp, scale=-1.0).then_inc(e_made, 1)

                def soft_ln(c):
                    t = zl[c % 4][:, 0:CHUNKS[c][3]]
                    act.wait_ge(e_made, p * NCK + (c + 1))
                    A(t, t, ACT.Ln, bias=ones[:, 0:1]).then_inc(l_ready, 1)

                def weights(c):
                    hh, kb, q0, W, top, last = CHUNKS[c]
                    act.wait_ge(cum_ready, p * NCK + (c + 4))
                    act.wait_ge(pv_done, p * NCK + (c + 1))
                    A(att[c % 2][:, 0:W], z_bank[c][:, 0:W], ACT.Exp, bias=bias_p[:, hh:hh + 1]
                      ).then_inc(att_ready, 1)

                def value_rows():
                    act.wait_ge(vtok_ps, p + 1)
                    act.wait_ge(tok_out, p * (16 * TOK_DMAS) + 16)
                    A(v_tok[:, :, :].rearrange("p a b -> p (a b)"), misc, ACT.Copy).then_inc(vtok_made, 1)

                def small_rows():
                    act.wait_ge(small_ps, p + 1)
                    A(small_tok[0:NS, 0:3, :].rearrange("p a b -> p (a b)"), a_bank[0:NS, 0:3 * P],
                      ACT.Copy).then_inc(small_made, 1)
                    A(small_tok[:, 3, :], a_bank[0:PTAIL, 3 * P:4 * P], ACT.Copy).then_inc(small_made, 1)

                for c in range(NCK + LAG_EXP):
                    if c >= LAG_EXP:
                        weights(c - LAG_EXP)
                    if c < NCK:
                        soft_abs(c)
                    if 0 < c <= NCK:
                        soft_ln(c - 1)
                    if c < NCK:
                        soft_exp(c)
                    if c == 0:
                        value_rows()
                    if c == SMALL_STEP + 1:
                        small_rows()
                act.wait_ge(pv_done, p * NCK + (NCK + 2))
                A(y_hi[:, bass.ds(p, 1), 0:TP].rearrange("p o t -> p (o t)"), misc, ACT.Copy).then_inc(yc_hi_made, 1)

            def vsg_out(g):
                par = g % 2
                act.wait_ge(unit_done, U_SG + g + 1)
                if g == 0:
                    act.wait_ge(yc_made, HP + 1)
                    act.wait_ge(tok_out, 16 * (TOK_DMAS * HP + 1))
                A(chunks(vsg_f[par]), ps[par], ACT.Copy)
                A(vsg_dec[:, g, :], last_cols(par, NS), ACT.Copy)
                A(spat[:, g, TP:T], last_cols(par, NS), ACT.Identity, bias=b0[:, g:g + 1],
                  scale=w00[:, g:g + 1]).then_inc(ps_free[par], 1)

            def mix_out(g):
                act.wait_ge(mixed_ps, g + 1)
                A(spat[:, g, 0:TP], misc, ACT.Copy).then_inc(spat_made, 1)

            vsg_out(0)
            vsg_out(1)
            act.wait_ge(sg_ps, 1)
            A(sgw_t[:, :, :].rearrange("p g t -> p (g t)"), misc[:, 0:SG * P], ACT.Copy).then_inc(sg_sb, 1)
            A(pool_st[:, :, :].rearrange("p g t -> p (g t)"), misc[:, 512:512 + SG * NS * PB], ACT.Copy
              ).then_inc(sg_sb, 1)
            mix_out(0)
            vsg_out(2)
            mix_out(1)
            vsg_out(3)
            mix_out(2)
            act.wait_ge(zb_made, 1)
            A(t_dec[:], z_dec[:], ACT.Abs).then_inc(dec_abs, 1)
            act.wait_ge(dec_abs, 1)
            A(t_dec[:], t_dec[:], ACT.Exp, scale=-1.0).then_inc(dec_e, 1)
            act.wait_ge(dec_e, 1)
            A(t_dec[:], t_dec[:], ACT.Ln, bias=ones[:, 0:1]).then_inc(dec_l, 1)
            act.wait_ge(dec_arg, 1)
            act.wait_ge(pad_zero, 1)
            A(a_dec, z_dec[:], ACT.Exp).then_inc(dec_att, 1)
            act.wait_ge(sgv_ps, 1)
            A(sgv_tok[:, :], banks[4][0:NS, 0:SG * P], ACT.Copy).then_inc(sgv_sb, 1)
            mix_out(3)
            act.wait_ge(dec_o_ps, 1)
            A(y_hi[:, :, TP:T], dec_o, ACT.Copy).then_inc(ydec_hi, 1)

            act.preload_act_table_set("sigmoid_and_others")

            def gates(name, first, adds):
                with act.Fori(0, KT // 2) as i:
                    for k in range(2):
                        act.wait_ge(unit_done, i * 4 + (first + 2 * k + 1))
                        if adds is None:
                            act.wait_ge(ps_free[1], i * 2 + freed(name, 1, k - 1))
                        else:
                            act.wait_ge(mix_made, i * 2 + (adds + k + 1))
                        A(chunks(gate[k][:, :]), ps[0], ACT.Sigmoid).then_inc(ps_free[0], 1)

            gates("mixc", U_MIXC, None)
            for g in range(SG):
                act.wait_ge(ya_ps, g + 1)
                A(chunks(y_hi[:, g, :]), ps[g % 2], ACT.Copy, scale=a_scale[:, g:g + 1]).then_inc(y_hi_made, 1)
            gates("mixa", U_MIXA, 0)
            with act.Fori(0, SG // 2) as i:
                for k in range(2):
                    act.wait_ge(ps_free[k], i + freed("u", k, 1))
                    A(y_hi[:, bass.ds(i * 2 + k, 1), :], spat[:, bass.ds(i * 2 + k, 1), :], ACT.Copy
                      ).then_inc(y_hi_made, 1)
            gates("mixb", U_MIXB, KT)
            act.preload_act_table_set("sqrt_and_others")
            act.wait_ge(unit_done, U_OUT)
            with act.Fori(0, KT) as k:
                act.wait_ge(mix_made, k + (2 + KT + 1))
                A(h_hi[:, bass.ds(k, 1), :], trunk[:, bass.ds(k, 1), :], ACT.Copy).then_inc(mhi_made, 1)

            act.wait_ge(m_split, KT)
            with act.Fori(0, KT // 2) as i:
                for k in range(2):
                    act.wait_ge(unit_done, i * 2 + (U_OUT + k + 1))
                    A(trunk[:, bass.ds(i * 2 + k, 1), :].rearrange("p o (a b) -> p (o a) b", a=NCH), ps[k], ACT.Copy)
                    act.wait_ge(ss_added, i * 2 + (k + 1))
                    A(chunks(sq), ps[k], ACT.Square).then_inc(ps_free[k], 1)

            def std_from(n):
                act.wait_ge(ss_ps, n + 1)
                A(chunks(rstd), ps[0], ACT.Sqrt, bias=eps[:, :], scale=1.0 / D).then_inc(ps_free[0], 1)

            std_from(0)
            with act.Fori(0, KT // 2) as i:
                for k in range(2):
                    act.wait_ge(ps_free[k], i + freed("xt", k, 1))
                    act.wait_ge(ss_added, i * 2 + (KT + k + 1))
                    A(sq, trunk[:, bass.ds(i * 2 + k, 1), :].rearrange("p o t -> p (o t)"), ACT.Square
                      ).then_inc(sq_made, 1)
            std_from(1)
            for k in range(KT):
                act.wait_ge(hn_made, k + 1)
                A(h_hi[:, k, :], hn[k % 2][:, :], ACT.Copy, scale=g_ffn[:, k:k + 1]).then_inc(hn_hi, 1)

            for g, (f0, size) in enumerate(FFN_GROUPS):
                act.preload_act_table_set("gelu_apprx_tanh_and_others")
                with act.Fori(0, size) as j:
                    act.wait_ge(g_made, j + (f0 + 1))
                    for k in range(2):
                        f = bass.ds(j + (f0 + k * FT), 1)
                        act.wait_ge(unit_done, j * 2 + (U_UP[g] + k + 1))
                        A(chunks(up[k][:, :]), ps[k], ACT.Copy)
                        A(tails[:, f, :].rearrange("p o t -> p (o t)"), last_cols(k, TAIL), ACT.Copy)
                        A(chunks(conv[k][:, :]), ps[k], ACT.Identity, bias=conv_par[:, 3, f],
                          scale=conv_par[:, 2, f]).then_inc(ps_free[k], 1)
                    act.wait_ge(conv_step, j * 8 + (8 * f0 + 4))
                    A(conv[0][:, :], conv[0][:, :], ACT.Gelu_apprx_tanh).then_inc(gelu_made, 1)
                    act.wait_ge(gv_made, j + (f0 + 1))
                    A(g_hi[:, bass.ds(j, 1), :].rearrange("p o t -> p (o t)"), conv[0][:, :], ACT.Copy
                      ).then_inc(g_hi_made, 1)
                if g == 0:
                    act.wait_ge(x1_out, 16)
                    with act.Fori(0, KT // 2) as i:
                        for k in range(2):
                            act.wait_ge(unit_done, i * 2 + (U_DOWN[g] + k + 1))
                            A(trunk[:, bass.ds(i * 2 + k, 1), :].rearrange("p o (a b) -> p (o a) b", a=NCH),
                              ps[k], ACT.Copy).then_inc(ps_free[k], 1)
            act.preload_act_table_set("sqrt_and_others")
            with act.Fori(0, KT // 2) as i:
                for k in range(2):
                    act.wait_ge(ps_free[k], i + freed(LAST_DOWN, k, 1))
                    act.wait_ge(ss_added, i * 2 + (2 * KT + k + 1))
                    A(sq, trunk[:, bass.ds(i * 2 + k, 1), :].rearrange("p o t -> p (o t)"), ACT.Square
                      ).then_inc(sq_made, 1)
            std_from(2)
            for n in range(2 * FT // 4):
                act.wait_ge(tail_ps, n + 1)
                if n >= 2:
                    act.wait_ge(tail_out[n % 2], 32 * (n // 2))
                A(up[n % 2][0:TAIL, 0:4 * P], misc[0:TAIL, (n % 2) * 512:(n % 2) * 512 + 4 * P], ACT.Copy
                  ).then_inc(tail_sb, 1)
            for n in range(NT + 1):
                m = P if n < NT else NS
                act.wait_ge(yt_ps, n + 1)
                if n >= 4:
                    act.wait_ge(y_out_done[n % 4], 16 * (n // 4))
                A(y_tok[0:m, n % 4, 0:512], ps_flat[n % 2][0:m, 0:512], ACT.Copy).then_inc(yt_left, 1)

        @block.vector
        def _(dve):
            V = nc.vector

            def split_lo(par, u):
                dve.wait_ge(w_hi_made, u + 1)
                V.tensor_tensor(w_lo[par][:, :, :], stage[par][:, :, :], w_hi[par][:, :, :].bitcast(F32),
                                ALU.subtract).then_inc(w_lo_made, 1)

            dve.wait_ge(gpre_in, 16)
            for b in range(len(IN_BATCHES) + 1):
                if b < len(IN_BATCHES):
                    tiles = IN_BATCHES[b]
                    n0_, n1_ = tiles[0], tiles[-1] + 1
                    m = P if n0_ < NT else NS
                    dve.wait_ge(std_made, b + 1)
                    V.reciprocal(rs[0:m, n0_:n1_], std[0:m, n0_:n1_]).then_inc(rs_made, 1)
                    dve.wait_ge(rs_made, b + 1)
                    for n in tiles:
                        V.scalar_tensor_tensor(x_tok[0:m, n, :], x_tok[0:m, n, :], rs[0:m, n:n + 1], g_pre[0:m, :],
                                               ALU.mult, ALU.mult).then_inc(xn_made, 1)
                for n in (IN_BATCHES[b - 1] if b > 0 else []):
                    m = P if n < NT else NS
                    dve.wait_ge(h_hi_made, n + 1)
                    V.tensor_tensor(h_lo[:, :, n * P:n * P + m],
                                    in_ps[n % 2][:, 0:KT * m].rearrange("p (k t) -> p k t", k=KT),
                                    h_hi[:, :, n * P:n * P + m].bitcast(F32), ALU.subtract
                                    ).then_inc(in_free[n % 2], 1)
                if b == 1:
                    split_lo(0, 0)
            split_lo(1, 1)

            dve.wait_ge(params_in, 16 * NPARAMS)
            with dve.Fori(0, HP) as p:
                V.tensor_copy(bias_p[:, :], bias_h[:, bass.ds(p * 2, 2)]).then_inc(biasp_made, 1)
                V.tensor_scalar(nbias_p[:, :], bias_h[:, bass.ds(p * 2, 2)], -1.0, None, ALU.mult).then_inc(biasp_made, 1)
                dve.wait_ge(q_hi_made, p + 1)
                V.scalar_tensor_tensor(chunks(q_lo[:, :]), ps[0], SCALE, chunks(q_hi[:, :]).bitcast(F32),
                                       ALU.mult, ALU.subtract).then_inc(ps_free[0], 1)
                split_lo(0, p * 4 + 2)
                dve.wait_ge(k_hi_made, p + 1)
                V.tensor_tensor(chunks(k_lo[:, :]), ps[1], chunks(k_hi[:, :]).bitcast(F32), ALU.subtract
                                ).then_inc(ps_free[1], 1)
                split_lo(1, p * 4 + 3)
                dve.wait_ge(ktok_ps, p + 1)
                dve.wait_ge(tok_out, p * (16 * TOK_DMAS) + 16)
                V.tensor_copy(k_tok[:, :, :].rearrange("p a b -> p (a b)"), misc).then_inc(ktok_made, 1)
                dve.wait_ge(biasp_made, p * 2 + 2)
                nl = 0
                for c, (hh, kb, q0, W, top, last) in enumerate(CHUNKS):
                    if c in NEXT_SPLITS:
                        j = NEXT_SPLITS.index(c)
                        split_lo(j, p * 4 + (4 + j))
                    for j, (_, end) in enumerate(A_STEPS):
                        if c == end - 1:
                            dve.wait_ge(a_ps, p * NCH + (j + 1))
                            V.tensor_copy(a_raw[:, bass.ds(p, 1), PAD + j * CH:PAD + (j + 1) * CH].rearrange(
                                "p o t -> p (o t)"), a_bank[:, 0:CH]).then_inc(a_out, 1)
                            if j == NCH - 1:
                                V.tensor_copy(a_tail[:, :], last_cols(1, PTAIL)).then_inc(tail_cols, 1)
                    t = zl[c % 4][:, 0:W]
                    dve.wait_ge(l_ready, p * NCK + (c + 1))
                    V.scalar_tensor_tensor(t, z_bank[c][:, 0:W], nbias_p[:, hh:hh + 1], t, ALU.max, ALU.add
                                           ).then_inc(spn_ready, 1)
                    if not last:
                        dve.wait_ge(spn_ready, p * NCK + (c + 1))
                        dve.wait_ge(cum_ready, p * NCK + (c + 1))
                    if top:
                        V.tensor_scalar(later[c % 4][:, 0:W], t, bias_p[:, hh:hh + 1], None, ALU.add
                                        ).then_inc(later_ready, 1)
                        nl += 1
                    elif not last:
                        Wb = CHUNKS[c - 1][3]
                        dve.wait_ge(later_ready, p * NLATER + nl)
                        V.scalar_tensor_tensor(later[c % 4][:, W - Wb:W], t[:, W - Wb:W], bias_p[:, hh:hh + 1],
                                               later[(c - 1) % 4][:, 0:Wb], ALU.add, ALU.add
                                               ).then_inc(later_ready, 1)
                        if Wb < W:
                            V.tensor_scalar(later[c % 4][:, 0:W - Wb], t[:, 0:W - Wb], bias_p[:, hh:hh + 1], None,
                                            ALU.add).then_inc(later_ready, 1)
                            nl += 1
                        nl += 1
                    dve.wait_ge(hi_ready, p * NCK + (c + 1))
                    V.scalar_tensor_tensor(sp_lo[c % 3][:, 0:W], t, bias_p[:, hh:hh + 1],
                                                sp_hi[c % 3][:, 0:W].bitcast(F32), ALU.add, ALU.subtract
                                                ).then_inc(sp_ready, 1)
                assert nl == NLATER
                dve.wait_ge(yc_hi_made, p + 1)
                V.tensor_tensor(y_lo[:, bass.ds(p, 1), 0:TP].rearrange("p o t -> p (o t)"), misc,
                                y_hi[:, bass.ds(p, 1), 0:TP].rearrange("p o t -> p (o t)").bitcast(F32),
                                ALU.subtract).then_inc(yc_made, 1)

            dec_scores = 0
            for g in range(SG):
                split_lo(g % 2, U_SG + 2 + g)
                for e in range(g * NE // SG, (g + 1) * NE // SG):
                    b, pg = e // NPG, e % NPG
                    if g == 0 and e == 0:
                        dve.wait_ge(yc_made, HP + 1)
                    dve.wait_ge(page_in[e % 4], 16 * (e // 4 + 1))
                    dve.wait_ge(qbc_in[b % 4], 16 * (b // 4 + 1))
                    if e > 0:
                        dve.wait_ge(zd_made, e)
                    V.tensor_tensor(kq[:, :], kv_pg[:, e % 4, :], q_bc[:, b % 4, :], ALU.mult).then_inc(kq_made, 1)
                    dve.wait_ge(kq_made, e + 1)
                    V.tensor_reduce(z_dec[:, pg, b, :], kq[:, :].rearrange("p (h d) -> p h d", h=H), AX_X, ALU.add
                                    ).then_inc(zd_made, 1)
                dve.wait_ge(vsgtok_ps, g + 1)
                V.tensor_copy(vsg_tok[:, :, :].rearrange("p a b -> p (a b)"), misc).then_inc(vsgtok_made, 1)
                w = WINDOWS[g]
                s, a = win[g % 2][:, PAD:PAD + TP], a_raw[:, g, PAD:PAD + TP]
                dve.wait_ge(win_step, (g + 1) * (g + 2) // 2)
                V.tensor_tensor(edge[:, 0:w - 1], s[:, 0:w - 1], inv_cnt[:, 0:w - 1], ALU.mult).then_inc(pool_edge, 1)
                dve.wait_ge(pool_edge, 2 * g + 1)
                V.tensor_tensor(edge[:, 0:w - 1], edge[:, 0:w - 1], a[:, 0:w - 1], ALU.subtract).then_inc(pool_edge, 1)
                dve.wait_ge(pool_edge, 2 * g + 2)
                V.scalar_tensor_tensor(a, s, 1.0 / w, a, ALU.mult, ALU.subtract).then_inc(pool_d, 1)
                dve.wait_ge(pool_d, 3 * g + 1)
                V.tensor_copy(a[:, 0:w - 1], edge[:, 0:w - 1]).then_inc(pool_d, 1)
                dve.wait_ge(sg_sb, 2)
                ad = a_raw[:, g, PAD + TP:PAD + T]
                V.tensor_reduce(pre[:, :], pool_st[:, g, :].rearrange("p (b j) -> p b j", b=NS)[:, :, PB - (w - 1):PB],
                                AX_X, ALU.add).then_inc(pool_pre, 1)
                dve.wait_ge(pool_pre, 2 * g + 1)
                V.tensor_tensor(pre[:, :], pre[:, :], ad, ALU.add).then_inc(pool_pre, 1)
                dve.wait_ge(pool_pre, 2 * g + 2)
                V.scalar_tensor_tensor(ad, pre[:, :], 1.0 / w, ad, ALU.mult, ALU.subtract).then_inc(pool_d, 1)
            dve.wait_ge(zd_made, NE)
            zv = z_dec[:, :, :, :].rearrange("p g b h -> p (g b) h")
            V.tensor_tensor(zv, zv, bias_h[:, :].unsqueeze(1).to_broadcast([P, NE, H]), ALU.add).then_inc(zb_made, 1)
            dve.wait_ge(dec_l, 1)
            V.scalar_tensor_tensor(t_dec[:], z_dec[:], 0.0, t_dec[:], ALU.max, ALU.add).then_inc(dec_sp, 1)
            dve.wait_ge(dec_cum, 1)
            zf = z_dec[:, :, :, :].rearrange("p g b h -> p (g b h)")
            V.tensor_tensor(zf, dec_sums, zf, ALU.add).then_inc(dec_arg, 1)
            dve.wait_ge(consts, NCONST + 4)
            V.tensor_reduce(pick[:, :], ident[0:NS * H, 0:NS * H].rearrange("p (h b) -> p b h", h=H), AX_X, ALU.add
                            ).then_inc(own_made, 1)
            dve.wait_ge(own_mask, 3)
            dve.wait_ge(dec_pv, NE)
            V.tensor_tensor(own_rows, dec_rows, own, ALU.mult).then_inc(own_made, 1)
            dve.wait_ge(ydec_hi, 1)
            V.tensor_tensor(y_lo[:, :, TP:T], dec_o, y_hi[:, :, TP:T].bitcast(F32), ALU.subtract).then_inc(ydec_made, 1)

            def mix(name, first, adds):
                with dve.Fori(0, KT // 2) as i:
                    for k in range(2):
                        d = bass.ds(i * 2 + k, 1)
                        u = i * 4 + (first + 2 * k)
                        split_lo(0, u + 2)
                        dve.wait_ge(unit_done, u + 2)
                        dve.wait_ge(ps_free[0], i * 2 + freed(name, 0, k + 1))
                        out = trunk[:, d, :].rearrange("p o t -> p (o t)") if adds is None else gate[k][:, :]
                        V.tensor_tensor(chunks(out), ps[1], chunks(gate[k][:, :]), ALU.mult).then_inc(ps_free[1], 1)
                        split_lo(1, u + 3)
                        if adds is not None:
                            dve.wait_ge(ps_free[1], i * 2 + freed(name, 1, k + 1))
                            V.tensor_tensor(trunk[:, d, :], trunk[:, d, :], gate[k][:, :].unsqueeze(1), ALU.add
                                            ).then_inc(mix_made, 1)

            mix("mixc", U_MIXC, None)
            for g in range(SG):
                dve.wait_ge(y_hi_made, g + 1)
                V.scalar_tensor_tensor(chunks(y_lo[:, g, :]), ps[g % 2], a_scale[:, g:g + 1],
                                       chunks(y_hi[:, g, :]).bitcast(F32), ALU.mult, ALU.subtract
                                       ).then_inc(ps_free[g % 2], 1)
            mix("mixa", U_MIXA, 0)
            with dve.Fori(0, SG // 2) as i:
                for k in range(2):
                    g = bass.ds(i * 2 + k, 1)
                    sv = spat[:, g, :].rearrange("p o (a b) -> p (o a) b", a=NCH)
                    dve.wait_ge(unit_done, i * 2 + (U_U + k + 1))
                    V.tensor_tensor(sv, ps[k], sv, ALU.mult).then_inc(ps_free[k], 1)
                    split_lo(k, i * 2 + (U_U + k + 2))
                    dve.wait_ge(y_hi_made, i * 2 + (SG + k + 1))
                    V.tensor_tensor(y_lo[:, g, :], spat[:, g, :], y_hi[:, g, :].bitcast(F32), ALU.subtract
                                    ).then_inc(yb_made, 1)
            mix("mixb", U_MIXB, KT)
            with dve.Fori(0, KT) as k:
                dve.wait_ge(mhi_made, k + 1)
                V.tensor_tensor(h_lo[:, bass.ds(k, 1), :], trunk[:, bass.ds(k, 1), :],
                                h_hi[:, bass.ds(k, 1), :].bitcast(F32), ALU.subtract).then_inc(m_split, 1)

            dve.wait_ge(out_done, 16 * 3)
            V.memset(ss_acc, 0.0).then_inc(ss_zero, 1)
            dve.wait_ge(ss_zero, 1)
            with dve.Fori(0, KT // 2) as i:
                for k in range(2):
                    dve.wait_ge(ps_free[k], i + freed("out", k, 1))
                    dve.wait_ge(ss_added, i * 2 + (k + 1))
                    V.tensor_tensor(ss_acc, ss_acc, sq, ALU.add).then_inc(ss_added, 1)
                    split_lo(k, i * 2 + (U_OUT + k + 2))

            def rstd_from(n):
                dve.wait_ge(ps_free[0], freed(("ss_m", "ss_x", "ss_f")[n], 0, 1))
                V.reciprocal(rstd, rstd).then_inc(rstd_t, 1)
                if n < 2:
                    V.memset(ss_acc, 0.0).then_inc(ss_zero, 1)

            def add_square(k, before):
                dve.wait_ge(sq_made, before + k + 1)
                dve.wait_ge(ss_added, KT + before + k + 1)
                V.tensor_tensor(ss_acc, ss_acc, sq, ALU.add).then_inc(ss_added, 1)

            rstd_from(0)
            dve.wait_ge(rstd_t, 1)
            dve.wait_ge(ss_zero, 2)
            for k in range(KT):
                V.tensor_tensor(trunk[:, k, :], trunk[:, k, :], rstd, ALU.mult).then_inc(mr_made, 1)
                dve.wait_ge(mr_made, k + 1)
                dve.wait_ge(xt_done, k + 1)
                V.scalar_tensor_tensor(trunk[:, k, :], trunk[:, k, :], g_post[:, k:k + 1],
                                       ps_flat[k % 2][:, 0:T], ALU.mult, ALU.add).then_inc(ps_free[k % 2], 1)
                if k > 0:
                    add_square(k - 1, 0)
            add_square(KT - 1, 0)
            rstd_from(1)
            dve.wait_ge(rstd_t, 2)

            def h2_lo(k):
                dve.wait_ge(hn_hi, k + 1)
                V.scalar_tensor_tensor(h_lo[:, k, :], hn[k % 2][:, :], g_ffn[:, k:k + 1],
                                       h_hi[:, k, :].bitcast(F32), ALU.mult, ALU.subtract).then_inc(h2_made, 1)

            for k in range(KT):
                if k >= 2:
                    dve.wait_ge(h2_made, k - 1)
                V.tensor_tensor(hn[k % 2][:, :], trunk[:, k, :], rstd, ALU.mult).then_inc(hn_made, 1)
                if k > 0:
                    h2_lo(k - 1)
            h2_lo(KT - 1)

            for g, (f0, size) in enumerate(FFN_GROUPS):
                with dve.Fori(0, size) as j:
                    for k in range(2):
                        f = bass.ds(j + (f0 + k * FT), 1)
                        c, x = conv[k], up[k]
                        s0 = j * 8 + (8 * f0 + 4 * k)
                        dve.wait_ge(ps_free[k], j + freed(f"up{g}", k, 1))
                        V.scalar_tensor_tensor(c[:, 1:TP], x[:, 0:TP - 1], conv_par[:, 1, f], c[:, 1:TP],
                                               ALU.mult, ALU.add).then_inc(conv_step, 1)
                        V.scalar_tensor_tensor(c[:, TP:T], conv_st[:, f, :, 1].rearrange("p o b -> p (o b)"),
                                               conv_par[:, 1, f], c[:, TP:T], ALU.mult, ALU.add).then_inc(conv_step, 1)
                        dve.wait_ge(conv_step, s0 + 1)
                        V.scalar_tensor_tensor(c[:, 2:TP], x[:, 0:TP - 2], conv_par[:, 0, f], c[:, 2:TP],
                                               ALU.mult, ALU.add).then_inc(conv_step, 1)
                        dve.wait_ge(conv_step, s0 + 2)
                        V.scalar_tensor_tensor(c[:, TP:T], conv_st[:, f, :, 0].rearrange("p o b -> p (o b)"),
                                               conv_par[:, 0, f], c[:, TP:T], ALU.mult, ALU.add).then_inc(conv_step, 1)
                        split_lo(k, j * 2 + (U_UP[g] + k + 2))
                    dve.wait_ge(gelu_made, j + (f0 + 1))
                    dve.wait_ge(conv_step, j * 8 + (8 * f0 + 8))
                    V.tensor_tensor(conv[0][:, :], conv[0][:, :], conv[1][:, :], ALU.mult).then_inc(gv_made, 1)
                    dve.wait_ge(g_hi_made, j + (f0 + 1))
                    V.tensor_tensor(g_lo[:, bass.ds(j, 1), :].rearrange("p o t -> p (o t)"), conv[0][:, :],
                                    g_hi[:, bass.ds(j, 1), :].rearrange("p o t -> p (o t)").bitcast(F32),
                                    ALU.subtract).then_inc(g_made, 1)
                name = f"down{g}"
                if g > 0:
                    for k in range(2):
                        dve.wait_ge(ps_free[k], freed(f"down{g - 1}", k, KT // 2))
                last_group = g == len(FFN_GROUPS) - 1

                def down(i, split):
                    for k in range(2):
                        if g > 0:
                            t = trunk[:, bass.ds(i * 2 + k, 1), :].rearrange("p o (a b) -> p (o a) b", a=NCH)
                            dve.wait_ge(unit_done, i * 2 + (U_DOWN[g] + k + 1))
                            V.tensor_tensor(t, ps[k], t, ALU.add).then_inc(ps_free[k], 1)
                        if split:
                            split_lo(k, i * 2 + (U_DOWN[g] + k + 2))
                        if last_group:
                            dve.wait_ge(sq_made, i * 2 + (KT + k + 1))
                            dve.wait_ge(ss_added, i * 2 + (2 * KT + k + 1))
                            V.tensor_tensor(ss_acc, ss_acc, sq, ALU.add).then_inc(ss_added, 1)

                if last_group:
                    dve.wait_ge(ss_zero, 3)
                with dve.Fori(0, KT // 2 - last_group) as i:
                    down(i, True)
                if last_group:
                    down(KT // 2 - 1, False)
            rstd_from(2)
            dve.wait_ge(rstd_t, 3)
            for k in range(KT):
                V.tensor_tensor(trunk[:, k, :], trunk[:, k, :], rstd, ALU.mult).then_inc(yr_made, 1)
                dve.wait_ge(yr_made, k + 1)
                if k == 0:
                    dve.wait_ge(x1r_in, 16)
                V.scalar_tensor_tensor(trunk[:, k, :], trunk[:, k, :], g_fpost[:, k:k + 1], x1_back[:, k, :],
                                       ALU.mult, ALU.add).then_inc(yf_made, 1)
            for n in range(NT + 1):
                m = P if n < NT else NS
                dve.wait_ge(yt_ps, n + 1)
                if n >= 4:
                    dve.wait_ge(y_out_done[n % 4], 16 * (n // 4))
                V.tensor_copy(y_tok[0:m, n % 4, 512:D], ps_flat[n % 2][0:m, 512:D]).then_inc(yt_right, 1)

        @block.tensor
        def _(pe):
            M = nc.tensor.matmul

            def T_(out, in_):
                m = in_.shape[0]
                return nc.tensor.transpose(out, in_, ident[0:m, 0:m])

            def unit(u, par, use, xs, ready=None):
                pe.wait_ge(w_lo_made, u + 3)
                pe.wait_ge(ps_free[par], use)
                n = len(xs)
                for k, (x_hi, x_lo) in enumerate(xs):
                    if ready:
                        ready(k)
                    for s, (w, x) in enumerate(((w_lo, x_hi), (w_hi, x_lo), (w_hi, x_hi))):
                        for c in range(NCH):
                            last = M(ps[par][:, c, :], w[par][:, k, :], x[:, c * CH:(c + 1) * CH],
                                     start=(k == 0 and s == 0), stop=(k == n - 1 and s == 2))
                last.then_inc(unit_done, 1)

            def column_products(out, par, c, xs, first, count):
                n = 3 * len(xs)
                for i in range(first, first + count):
                    x_hi, x_lo = xs[i // 3]
                    w, x = ((w_lo, x_hi), (w_hi, x_lo), (w_hi, x_hi))[i % 3]
                    t = M(out, w[par][:, i // 3, :], x[:, c * CH:(c + 1) * CH], start=(i == 0), stop=(i == n - 1),
                          skip_group_check=True)
                return t

            hs = [(h_hi[:, k, :], h_lo[:, k, :]) for k in range(KT)]
            ys = [(y_hi[:, k, :], y_lo[:, k, :]) for k in range(BT)]

            pe.wait_ge(consts, NCONST + 4)
            for n in range(NT + 1):
                m = P if n < NT else NS
                pe.wait_ge(xn_made, n + 1)
                if n >= 2:
                    pe.wait_ge(in_free[n % 2], n // 2)
                for k in range(KT):
                    t = T_(in_ps[n % 2][:, k * m:(k + 1) * m], x_tok[0:m, n, k * P:(k + 1) * P])
                t.then_inc(xt_ps, 1)
                for c in range(NCH - 1):
                    tiles = -(-(c + 1) * CH // P)
                    if n == tiles + (c > 0):
                        if c == 0:
                            pe.wait_ge(w_lo_made, 3)
                        for k in range(2):
                            pe.wait_ge(in_free[k], (tiles + 1 - k) // 2)
                        column_products(ps[0][:, c, :], 0, c, hs, 0, 3 * KT)
            pe.wait_ge(in_free[0], NT // 2 + 1)
            pe.wait_ge(in_free[1], NT // 2)
            column_products(ps[0][:, NCH - 1, :], 0, NCH - 1, hs, 0, 3 * KT).then_inc(unit_done, 1)
            pe.wait_ge(params_in, 16 * NPARAMS)
            T_(misc[:, 0:NORM_COLS], norm_rows[:, :])
            for j in range(4):
                T_(misc[:, NORM_COLS + 2 * FT * j:NORM_COLS + 2 * FT * (j + 1)], conv_rows[:, j, :])
            for f in range(2 * FT):
                at = ST_AT + 2 * NS * f if f < ST0 else 512 + 2 * NS * (f - ST0)
                t = T_(misc[:, at:at + 2 * NS], st_rows[:, f * P:(f + 1) * P])
            t.then_inc(par_ps, 1)

            with pe.Fori(0, HP) as p:
                def tokens(dst, src, m=T):
                    for n in range(NT):
                        t = T_(dst[:, n * P:(n + 1) * P], src[:, n * P:(n + 1) * P])
                    return t

                def scores(c):
                    hh, kb, q0, W, top, last = CHUNKS[c]
                    r = slice(hh * DH, (hh + 1) * DH)
                    z = z_bank[c][:, 0:W]
                    for s, (k, q) in enumerate(((k_lo, q_hi), (k_hi, q_lo), (k_hi, q_hi))):
                        t = M(z, k[r, kb * P:(kb + 1) * P], q[r, q0:q0 + W], start=(s == 0), stop=(s == 2),
                              skip_group_check=True)
                    if q0 == kb * P:
                        t = M(z[:, 0:P], ident_b[:, :], mask_b[:, :], start=False, stop=True, skip_group_check=True)
                    t.then_inc(z_ready, 1)

                def softplus_sums(c):
                    hh, kb, q0, W, top, last = CHUNKS[c]
                    z = z_bank[c][:, 0:W]
                    pe.wait_ge(sp_ready, p * NCK + (c + 4))
                    M(z, neg_tri[:, :], sp_lo[c % 3][:, 0:W], start=False, stop=False, skip_group_check=True)
                    t = M(z, neg_tri[:, :], sp_hi[c % 3][:, 0:W], start=False, stop=top, skip_group_check=True)
                    if not top:
                        Wb = CHUNKS[c - 1][3]
                        pe.wait_ge(later_ready, p * NLATER + later_upto[c])
                        t = M(z[:, W - Wb:W], neg_ones[:, :], later[(c - 1) % 4][:, 0:Wb], start=False, stop=True,
                              skip_group_check=True)
                    t.then_inc(cum_ready, 1)

                def values(c):
                    hh, kb, q0, W, top, last = CHUNKS[c]
                    r = slice(hh * DH, (hh + 1) * DH)
                    pe.wait_ge(att_ready, p * NCK + (c + 1))
                    M(misc[r, q0:q0 + W], v_tok[:, kb, r], att[c % 2][:, 0:W], start=top, stop=last,
                      skip_group_check=True).then_inc(pv_done, 1)

                def pooling_tile(step):
                    for j, (begin, end) in enumerate(A_STEPS):
                        if not begin <= step <= end:
                            continue
                        if step == begin and j == 0:
                            pe.wait_ge(w_lo_made, p * 4 + 6)
                        if step == begin and j > 0:
                            pe.wait_ge(a_out, p * NCH + j)
                        per_step = 3 * KT // (end + 1 - begin)
                        t = column_products(a_bank[:, 0:CH], 1, j, hs, (step - begin) * per_step, per_step)
                        if step == end and j == NCH - 1:
                            t.then_inc(a_ps, 1)
                            pe.sem_inc(unit_done, 1)
                        elif step == end:
                            t.then_inc(a_ps, 1)

                pe.wait_ge(small_made, p * 2 + 2)
                unit(p * 4 + 1, 1, p + freed("att", 1, 0), hs)
                unit(p * 4 + 2, 0, p * 2 + freed("att", 0, 1), hs)
                pe.wait_ge(kf_made, p + 1)
                pe.wait_ge(yc_made, p + 1)
                pe.wait_ge(par_sb, 3)
                tokens(misc, k_f).then_inc(ktok_ps, 1)
                pe.wait_ge(ps_free[0], p * 2 + freed("att", 0, 2))
                pe.wait_ge(ps_free[1], p + freed("att", 1, 1))
                for c in range(NCK + LAG_PV):
                    if c < NCK:
                        scores(c)
                    if 0 <= c - LAG_CUM < NCK:
                        softplus_sums(c - LAG_CUM)
                    pooling_tile(c)
                    if c == 0:
                        pe.wait_ge(ktok_made, p + 1)
                        tokens(misc, v_f).then_inc(vtok_ps, 1)
                    if c == LAG_PV - 1:
                        pe.wait_ge(vtok_made, p + 1)
                    if c >= LAG_PV - 1:
                        if c - LAG_PV + 1 < NCK: values(c - LAG_PV + 1)
                    if c == SMALL_STEP:
                        pe.wait_ge(tail_cols, p + 1)
                        T_(a_bank[0:NS, 0:P], q_dec[:, :])
                        T_(a_bank[0:NS, P:2 * P], k_f[:, TP:T])
                        T_(a_bank[0:NS, 2 * P:3 * P], v_f[:, TP:T])
                        T_(a_bank[0:PTAIL, 3 * P:4 * P], a_tail[:, :]).then_inc(small_ps, 1)
                    if NCK <= c < NCK + NCH:
                        if c == NCK:
                            pe.wait_ge(w_lo_made, p * 4 + 7)
                        t = column_products(ps[0][:, c - NCK, :], 0, c - NCK, hs, 0, 3 * KT)
                t.then_inc(unit_done, 1)

            def sg_part(u, c):
                name, i = ("sg", (u - U_SG) // 2) if u < U_MIXC else ("mixc", 0)
                if c == 0:
                    pe.wait_ge(w_lo_made, u + 3)
                    pe.wait_ge(ps_free[u % 2], freed(name, u % 2, i))
                xs = ys if u == U_MIXC + 1 else hs
                t = column_products(ps[u % 2][:, c, :], u % 2, c, xs, 0, 3 * len(xs))
                if c == NCH - 1:
                    t.then_inc(unit_done, 1)

            def sg_tokens(g):
                pe.wait_ge(ps_free[g % 2], freed("sg", g % 2, g // 2 + 1))
                if g > 0:
                    pe.wait_ge(spat_made, g)
                else:
                    pe.wait_ge(sg_sb, 2)
                for n in range(NT):
                    t = T_(misc[:, n * P:(n + 1) * P], vsg_f[g % 2][:, n * P:(n + 1) * P])
                t.then_inc(vsgtok_ps, 1)

            def sg_mix(g):
                pe.wait_ge(vsgtok_made, g + 1)
                for n in range(NT):
                    M(misc[:, n * P:(n + 1) * P], vsg_tok[:, n, :], sgw_t[:, g, :], start=True, stop=False)
                    t = M(misc[:, n * P:(n + 1) * P], ones[0:1, :], sgb_row[0:1, g * P:(g + 1) * P],
                          start=False, stop=True)
                t.then_inc(mixed_ps, 1)

            pe.wait_ge(small_made, 2 * HP + 2)
            for c in range(NCH):
                sg_part(U_SG + 1, c)
            pe.wait_ge(sgw_masked, SG)
            pe.wait_ge(yc_made, HP + 1)
            pe.wait_ge(st_in, 64)
            for g in range(SG):
                T_(misc[:, g * P:(g + 1) * P], sgw_rows[:, g, :])
                t = T_(misc[:, 512 + g * NS * PB:512 + (g + 1) * NS * PB], sp_rows[:, g * P:(g + 1) * P])
            t.then_inc(sg_ps, 1)
            sg_part(U_SG + 2, 0)
            sg_tokens(0)
            sg_part(U_SG + 2, 1)
            sg_mix(0)
            sg_part(U_SG + 2, 2)
            sg_tokens(1)
            sg_part(U_SG + 3, 0)
            sg_mix(1)
            sg_part(U_SG + 3, 1)
            sg_tokens(2)
            sg_part(U_SG + 3, 2)
            sg_mix(2)
            sg_part(U_MIXC, 0)
            sg_tokens(3)
            pe.wait_ge(ps_free[1], freed("mixc", 1, 0))
            pe.wait_ge(dec_sp, 1)
            half = NS * H
            sp_d = t_dec[:, :, :, :].rearrange("p g b h -> p (g b h)")
            M(dec_sums, neg_tri[:, :].bitcast(F32), sp_d, start=True, stop=False, skip_group_check=True)
            M(dec_sums[:, 0:half], neg_ones[:, :], sp_d[:, half:], start=False, stop=True, skip_group_check=True
              ).then_inc(dec_cum, 1)
            sg_part(U_MIXC, 1)
            sg_mix(3)
            pe.wait_ge(dec_arg, 1)
            for g in range(SG):
                t = T_(banks[4][0:NS, g * P:(g + 1) * P], vsg_dec[:, g, :])
            t.then_inc(sgv_ps, 1)
            sg_part(U_MIXC, 2)
            pe.wait_ge(dec_att, 1)
            pe.wait_ge(spat_made, SG)
            for e in range(NE):
                b, pg = e // NPG, e % NPG
                pe.wait_ge(page_in[e % 4], 16 * ((NE + e) // 4 + 1))
                M(dec_rows, a_pad[:, pg * NS * A_STEP + b * NS * H:pg * NS * A_STEP + (b + 1) * NS * H],
                  kv_pg[:, e % 4, :], start=(e == 0), stop=(e == NE - 1)).then_inc(dec_pv, 1)
            pe.wait_ge(sgv_sb, 1)
            sg_part(U_MIXC + 1, 0)
            pe.wait_ge(own_made, 2)
            for hp in range(HP):
                t = M(dec_o[:, hp, :], own_rows[:, hp * P:(hp + 1) * P], pick[:, :], start=True, stop=True)
            t.then_inc(dec_o_ps, 1)
            sg_part(U_MIXC + 1, 1)
            pe.wait_ge(ydec_made, 1)
            sg_part(U_MIXC + 1, 2)

            def branch(name, first, y_ready, begin=0):
                with pe.Fori(begin, KT) as d:
                    unit(d * 2 + first, 0, d + freed(name, 0, 0), hs)
                    y_ready()
                    unit(d * 2 + (first + 1), 1, d + freed(name, 1, 0), ys)

            branch("mixc", U_MIXC, lambda: pe.wait_ge(ydec_made, 1), 1)
            for g in range(SG):
                pe.wait_ge(pool_d, 3 * SG)
                pe.wait_ge(ps_free[g % 2], freed("pool", g % 2, g // 2))
                for c in range(NCH):
                    t = M(ps[g % 2][:, c, :], poolw[:, g, :], a_raw[:, g, PAD + c * CH:PAD + (c + 1) * CH],
                          start=True, stop=True)
                t.then_inc(ya_ps, 1)
            branch("mixa", U_MIXA, lambda: [pe.wait_ge(ps_free[k], freed("mixa", k, 0)) for k in range(2)])
            with pe.Fori(0, SG // 2) as i:
                for k in range(2):
                    unit(i * 2 + (U_U + k), k, i + freed("u", k, 0), hs)
            branch("mixb", U_MIXB, lambda: pe.wait_ge(yb_made, SG))

            with pe.Fori(0, KT // 2) as i:
                for k in range(2):
                    unit(i * 2 + (U_OUT + k), k, i + freed("out", k, 0), hs,
                         (lambda kt: pe.wait_ge(m_split, kt + 1)) if k == 0 else None)

            def ss_total(name, n):
                pe.wait_ge(ss_added, KT * (n + 1) + 1)
                pe.wait_ge(ps_free[0], freed(name, 0, 0))
                for c in range(NCH):
                    t = M(ps[0][:, c, :], ones[:, :], ss_acc[:, c * CH:(c + 1) * CH], start=True, stop=True)
                t.then_inc(ss_ps, 1)

            ss_total("ss_m", 0)
            pe.wait_ge(xr_in, 32)
            for k in range(KT):
                pe.wait_ge(ps_free[k % 2], freed("xt", k % 2, k // 2))
                for n in range(NT + 1):
                    m = P if n < NT else NS
                    t = T_(ps_flat[k % 2][:, n * P:n * P + m], xr_tok[0:m, n, k * P:(k + 1) * P])
                t.then_inc(xt_done, 1)
            ss_total("ss_x", 1)

            for g, (f0, size) in enumerate(FFN_GROUPS):
                with pe.Fori(0, size) as j:
                    for k in range(2):
                        unit(j * 2 + (U_UP[g] + k), k, j + freed(f"up{g}", k, 0), hs,
                             (lambda kt: pe.wait_ge(h2_made, kt + 1)) if g == 0 and k == 0 else None)
                gs = [(g_hi[:, k, :], g_lo[:, k, :]) for k in range(size)]
                with pe.Fori(0, KT // 2) as i:
                    for k in range(2):
                        unit(i * 2 + (U_DOWN[g] + k), k, i + freed(f"down{g}", k, 0), gs,
                             (lambda kt: pe.wait_ge(g_made, f0 + kt + 2)) if k == 0 else None)
            ss_total("ss_f", 2)
            for n in range(2 * FT // 4):
                if n >= 2:
                    pe.wait_ge(tail_sb, n - 1)
                for j in range(4):
                    t = T_(misc[0:TAIL, (n % 2) * 512 + j * P:(n % 2) * 512 + (j + 1) * P], tails[:, 4 * n + j, :])
                t.then_inc(tail_ps, 1)
            pe.wait_ge(yf_made, KT)
            pe.wait_ge(ps_free[0], freed("yt", 0, 0))
            pe.wait_ge(ps_free[1], freed("yt", 1, 0))
            for n in range(NT + 1):
                m = P if n < NT else NS
                if n >= 2:
                    pe.wait_ge(yt_left, n - 1)
                    pe.wait_ge(yt_right, n - 1)
                for k in range(KT):
                    t = T_(ps_flat[n % 2][0:m, k * P:(k + 1) * P], trunk[:, k, n * P:n * P + m])
                t.then_inc(yt_ps, 1)


_INS = ["x_prompt", "x_sample", "state_pool", "cache_k", "cache_v", "page_table", "state_conv",
        "norm_mix_pre", "norm_mix_post", "norm_ffn_pre", "norm_ffn_post", "w_in", "pool_w",
        "pool_scale", "sg_w", "sg_b", "sb_bias", "w_branch", "w_out", "w_up", "conv_w", "conv_b",
        "w_down"]


def kernel(**inputs):
    import numpy as np
    import concourse.bacc as bacc
    from concourse.bass_utils import run_bass_kernel_spmd

    nc = bacc.Bacc("TRN2", target_bir_lowering=False, num_devices=1, dynamic_dma_scratch_size=1024)
    arrays = {n: np.ascontiguousarray(inputs[n]) for n in _INS}
    args = [nc.dram_tensor(f"in_{n}", a.shape, mybir.dt.from_np(a.dtype), kind="ExternalInput").ap()
            for n, a in arrays.items()]
    s = {n: a.shape for n, a in arrays.items()}
    depth, dec, heads = s["w_in"][0], s["x_sample"][0], s["sb_bias"][1]
    head_dim = s["cache_k"][4]
    shapes = [s["x_prompt"], s["x_sample"],
              (depth, s["x_prompt"][0]) + s["state_pool"][2:], s["state_pool"],
              *[(depth,) + s["x_prompt"][:2] + (heads, head_dim)] * 2,
              *[(depth,) + s["x_sample"][:2] + (heads, head_dim)] * 2,
              (depth, dec, s["x_sample"][1], s["sg_w"][1] * (s["w_branch"][2] // s["sg_w"][1])),
              (depth, s["x_prompt"][0]) + s["state_conv"][2:], s["state_conv"]]
    outs = [nc.dram_tensor(f"out_{i}", shape, F32, kind="ExternalOutput").ap() for i, shape in enumerate(shapes)]
    build(nc, *args, outs)
    r = run_bass_kernel_spmd(nc, [{f"in_{n}": a for n, a in arrays.items()}], core_ids=[0])
    return tuple(r.results[0][f"out_{i}"] for i in range(len(outs)))
```

```python
from contextlib import ExitStack

import concourse.bass as bass
from concourse import mybir

F32 = mybir.dt.float32
F32R = mybir.dt.float32r
BF16 = mybir.dt.bfloat16
I32 = mybir.dt.int32
ALU = mybir.AluOpType
ACT = mybir.ActivationFunctionType
AX_X = mybir.AxisListType.X

P = 128


def build(nc, x_prompt, x_sample, state_pool, cache_k, cache_v, page_table, state_conv,
          norm_mix_pre, norm_mix_post, norm_ffn_pre, norm_ffn_post, w_in, pool_w, pool_scale,
          sg_w, sg_b, sb_bias, w_branch, w_out, w_up, conv_w, conv_b, w_down, outs):
    (y_prompt, y_sample, pool_prompt, pool_sample, k_prompt, v_prompt, k_sample, v_sample,
     sgv_sample, conv_prompt, conv_sample) = outs

    D = x_prompt.shape[2]
    TP = x_prompt.shape[1]
    NS = x_sample.shape[0]
    T = TP + NS
    NCH = 3
    CH = T // NCH
    KT = D // P
    NT = TP // P
    SG = pool_w.shape[1]
    BT = w_branch.shape[2] // P
    H = sb_bias.shape[1]
    DH = k_prompt.shape[4]
    HP = H // 2
    NPOOL = cache_k.shape[1]
    NPG = page_table.shape[1]
    NE = NS * NPG
    F = w_down.shape[1]
    FT = F // P
    PB = state_pool.shape[2]
    WINDOWS = (2, 4, 8, 16)
    PAD = max(WINDOWS)
    SCALE = DH ** -0.5
    HALF = 512
    TAIL = 2 + NS
    PTAIL = PB + NS
    NEG = -1.0e30
    assert T == NCH * CH and CH % 2 == 0 and CH <= 512 and cache_k.shape[2] == P
    assert DH * 2 == P and BT == SG == HP and x_sample.shape[1] == 1 and NPG == 2

    C_A, C_U, C_V, C_Q, C_K, C_VV, C_G = (n * BT for n in range(7))
    FFN_GROUPS = [(0, 8), (8, 7), (15, 7)]
    assert sum(n for _, n in FFN_GROUPS) == FT

    U_ATT = 0
    U_SG = U_ATT + 4 * HP
    U_MIXC = U_SG + SG
    U_MIXA = U_MIXC + 2 * KT
    U_U = U_MIXA + 2 * KT
    U_MIXB = U_U + SG
    U_OUT = U_MIXB + 2 * KT
    U_UP, U_DOWN = [], []
    n = U_OUT + KT
    for _, size in FFN_GROUPS:
        U_UP.append(n)
        U_DOWN.append(n + 2 * size)
        n += 2 * size + KT
    U_END = n

    USES = {}
    n0 = n1 = 0
    for name, a, b in ([("att", 2 * HP, HP), ("sg", 2, 2), ("mixc", KT, KT),
                        ("pool", 2, 2), ("mixa", KT, KT), ("u", 2, 2), ("mixb", KT, KT),
                        ("out", KT // 2 - 1, KT // 2 - 1)]
                       + [x for g, (_, size) in enumerate(FFN_GROUPS)
                          for x in ((f"up{g}", size, size), (f"down{g}", KT // 2, KT // 2))]):
        USES[name] = (n0, n1)
        n0, n1 = n0 + a, n1 + b

    def freed(stage, par, k):
        return k + (USES[stage][par] + 1)

    CHUNKS = []
    for hh in range(2):
        for half in reversed(range(TP // HALF)):
            top = (half + 1) * HALF // P - 1
            for kb in reversed(range(top + 1)):
                q0 = max(kb * P, half * HALF)
                CHUNKS.append((hh, kb, q0, (half + 1) * HALF - q0, kb == top, kb == 0))
    NCK = len(CHUNKS)
    later_upto = [0]
    for n, (_, _, _, W, top, last) in enumerate(CHUNKS):
        wider = not top and W > CHUNKS[n - 1][3]
        later_upto.append(later_upto[-1] + (0 if last else 1 + wider))
    NLATER = later_upto[NCK]
    assert NCK % 12 == 0
    LAG_CUM, LAG_EXP, LAG_VALUES = 3, 4, 4
    NEXT_SPLITS = (7, 23)
    A_STEPS = [(0, 5), (8, 13), (15, 22)]
    SMALL_STEP = 23

    ctx = ExitStack()
    with ctx:
        def sb(name, shape, dt=F32, scope=ctx):
            return scope.enter_context(nc.sbuf_tensor(name, shape, dt))

        s_end = ExitStack()
        x1_back = sb("x1_back", [P, KT, T], F32, s_end)
        y_tok = sb("y_tok", [P, 4, D], F32, s_end)
        s_end.close()
        h_hi = sb("h_hi", [P, KT, T], F32R)
        h_lo = sb("h_lo", [P, KT, T], F32R)
        stage = [sb(f"stage{i}", [P, KT, P]) for i in range(2)]
        w_hi = [sb(f"w_hi{i}", [P, KT, P], F32R) for i in range(2)]
        w_lo = [sb(f"w_lo{i}", [P, KT, P], F32R) for i in range(2)]
        ident = sb("ident", [P, P])
        ones = sb("ones", [P, P])
        neg_ones = sb("neg_ones", [P, P])
        neg_tri = sb("neg_tri", [P, P], F32R)
        ident_b = sb("ident_b", [P, P], BF16)
        mask_b = sb("mask_b", [P, P], BF16)
        NORM_COLS = 3 * KT + SG
        par_t = sb("par_t", [P, NORM_COLS + 4 * 2 * FT])
        g_post, g_ffn, g_fpost = (par_t[:, n * KT:(n + 1) * KT] for n in range(3))
        a_scale = par_t[:, 3 * KT:NORM_COLS]
        conv_par = par_t[:, NORM_COLS:].rearrange("p (j f) -> p j f", j=4)
        bias_h = sb("bias_h", [P, H])
        bias_p = sb("bias_p", [P, 2])
        nbias_p = sb("nbias_p", [P, 2])
        w00 = sb("w00", [P, SG])
        b0 = sb("b0", [P, SG])
        conv_st = sb("conv_st", [P, 2 * FT, NS, 2])
        tails = sb("tails", [P, 2 * FT, TAIL])
        inv_cnt = sb("inv_cnt", [P, PB])
        edge = sb("edge", [P, PB])
        pre = sb("pre", [P, NS])
        eps = sb("eps", [P, 1])
        ss = sb("ss", [P, NT + 1])
        std = sb("std", [P, NT + 1])
        rs = sb("rs", [P, NT + 1])
        work = [sb("work0", [P, PAD + TP])]
        s_head = ExitStack()
        q_st1, k_st1 = (sb(n, [P, T], F32R, s_head) for n in ("q_st1", "k_st1"))
        s_head.close()
        work += [sb(f"work{i}", [P, PAD + TP]) for i in (1, 2)]
        rstd, ss_acc, sq = (w[:, 0:T] for w in work)
        sgv_tok = work[1][0:NS, 0:SG * P]
        win = work[0:2]
        small_tok = work[0][0:PTAIL, 0:4 * P].rearrange("p (a b) -> p a b", a=4)

        s_in = ExitStack()
        x_tok = sb("x_tok", [P, NT + 1, D], F32, s_in)
        g_pre = sb("g_pre", [P, D], F32, s_in)
        st_rows = sb("st_rows", [NS * 2, 2 * F], F32, s_in)
        norm_rows = sb("norm_rows", [NORM_COLS, P], F32, s_in)
        conv_rows = sb("conv_rows", [2 * FT, 4, P], F32, s_in)
        s_in.close()

        s_pair = ExitStack()
        q_st0, q_lo, k_st0, k_lo = (sb(n, [P, T], F32R, s_pair) for n in ("q_st0", "q_lo", "k_st0", "k_lo"))
        q_st, k_st = [q_st0, q_st1], [k_st0, k_st1]
        k_f, v_f = (sb(n, [P, T], F32, s_pair) for n in ("k_f", "v_f"))
        k_tok, v_tok = (sb(n, [P, NT, P], F32, s_pair) for n in ("k_tok", "v_tok"))
        s_pair.close()
        s_dec = ExitStack()
        q_bc = sb("q_bc", [P, 4, HP * P], F32, s_dec)
        kv_pg = sb("kv_pg", [P, 4, HP * P], F32, s_dec)
        kq = sb("kq", [P, HP * P], F32, s_dec)
        sp_rows = sb("sp_rows", [NS * PB, SG * P], F32, s_dec)
        sgw_rows = sb("sgw_rows", [P, SG, P], F32, s_dec)
        vsg_tok = sb("vsg_tok", [P, NT, P], F32, s_dec)
        z_dec, t_dec = (sb(n, [P, NPG, NS, H], F32, s_dec) for n in ("z_dec", "t_dec"))
        A_STEP = NS * H + 1
        a_pad = q_bc[:, :, :].rearrange("p a b -> p (a b)")[:, 0:NPG * NS * A_STEP]
        a_dec = a_pad.rearrange("p (g b x) -> p g b x", g=NPG, b=NS)[:, :, :, 0:NS * H].rearrange(
            "p g b (h y) -> p g b h y", h=H)[:, :, :, :, 0]
        own = sp_rows[0:NS * H, :]
        own_rows = kq[0:NS * H, :]
        pick = sb("pick", [NS * H, NS], F32, s_dec)
        s_dec.close()
        trunk = sb("trunk", [P, KT, T])

        s_mix = ExitStack()
        y_hi = sb("y_hi", [P, BT, T], F32R, s_mix)
        y_lo = sb("y_lo", [P, BT, T], F32R, s_mix)
        a_raw = sb("a_raw", [P, SG, PAD + T], F32, s_mix)
        s_att = ExitStack()
        zl = [sb(f"zl{i}", [P, HALF], F32, s_att) for i in range(4)]
        sp_hi = [sb(f"sp_hi{i}", [P, HALF], F32R, s_att) for i in range(3)]
        sp_lo = [sb(f"sp_lo{i}", [P, HALF], F32R, s_att) for i in range(3)]
        later = [sb(f"later{i}", [P, HALF], F32, s_att) for i in range(4)]
        att = [sb(f"att{i}", [P, HALF], F32, s_att) for i in range(2)]
        q_dec = sb("q_dec", [P, NS], F32, s_att)
        a_tail = sb("a_tail", [P, PTAIL], F32, s_att)
        s_att.close()
        spat = sb("spat", [P, SG, T], F32, s_mix)
        pool_st = sb("pool_st", [P, SG, NS * PB], F32, s_mix)
        sgw_t = sb("sgw_t", [P, SG, P], F32, s_mix)
        sgb_row = sb("sgb_row", [1, SG * P], F32, s_mix)
        poolw = sb("poolw", [P, SG, P], F32, s_mix)
        s_sg = ExitStack()
        vsg_dec = sb("vsg_dec", [P, SG, NS], F32, s_sg)
        pt_sb = sb("pt_sb", [1, NE], I32, s_sg)
        vsg_f = [work[2][:, 0:T], sb("vsg_f1", [P, T], F32, s_sg)[:, :]]
        s_sg.close()
        s_gate = ExitStack()
        gate = [sb(f"gate{i}", [P, T], F32, s_gate) for i in range(2)]
        s_gate.close()
        s_mix.close()
        s_res = ExitStack()
        xr_tok = sb("xr_tok", [P, NT + 1, D], F32, s_res)
        x_t = sb("x_t", [P, KT, T], F32, s_res)
        hn = [sb(f"hn{i}", [P, CH], F32, s_res) for i in range(3)]
        x_sq = [sb(f"x_sq{i}", [P, CH], F32, s_res)[:, :] for i in range(3)]
        x_sq += [work[2][:, i * CH:(i + 1) * CH] for i in range(NCH)]
        m_sq = [sb(f"m_sq{i}", [P, CH], F32, s_res) for i in range(3)]
        s_res.close()
        s_ffn = ExitStack()
        GMAX = max(n for _, n in FFN_GROUPS)
        g_hi = sb("g_hi", [P, GMAX, T], F32R, s_ffn)
        g_lo = sb("g_lo", [P, GMAX, T], F32R, s_ffn)
        up = [sb(f"up{i}", [P, T], F32, s_ffn) for i in range(2)]
        conv = [sb(f"conv{i}", [P, T], F32, s_ffn) for i in range(2)]
        s_ffn.close()

        ps_all = [ctx.enter_context(nc.psum_tensor(f"ps{i}", [P, NCH, 512], F32)) for i in range(2)]
        misc_t = ctx.enter_context(nc.psum_tensor("misc", [P, 2 * 512], F32))
        ps = [t[:, :, 0:CH] for t in ps_all]
        ps_flat = [t[:, :, :].rearrange("p a b -> p (a b)") for t in ps_all]
        misc = misc_t[:, :]
        banks = [ps_all[i // NCH][:, i % NCH, :] for i in range(2 * NCH)]
        NZ = 5
        in_ps = [misc, ps_flat[1][:, 0:D]]
        z_bank = [banks[(c + (NZ - NCK) % NZ) % NZ] for c in range(NCK)]
        a_bank = banks[NZ]
        HEAD_ROWS = (slice(0, DH), slice(DH, 2 * DH))

        def chunks(ap):
            return ap.rearrange("p (a b) -> p a b", a=NCH)

        def last_cols(par, n):
            return ps_all[par][:, NCH - 1, CH - n:CH]

        cols = [slice(c * CH, (c + 1) * CH) for c in range(NCH)]
        XT_HALF = NT // 2
        XT_GROUPS = [(half, k) for half in range(2) for k in range(KT)] + [(2, 0)]
        M_PARTS = [(u, c) for u in (KT - 4, KT - 3) for c in range(NCH)]
        M_PARTS += [(u, c) for c in range(NCH) for u in (KT - 2, KT - 1)]
        XT_AFTER = [range(min(2 * n, len(XT_GROUPS)), min(2 * n + 2, len(XT_GROUPS))) for n in range(len(M_PARTS))]
        SUMS0 = KT - 1
        SUMS1 = 2 * KT + 2 * (NCH - 1) - 1
        F_PARTS = [(u, c) for c in range(NCH) for u in (KT - 2, KT - 1)]
        ROW_GROUPS = 2 * FT // 4
        ROWS_AFTER = [range(min(2 * n, ROW_GROUPS), min(2 * n + 2, ROW_GROUPS)) for n in range(len(F_PARTS))]
        Y_WHOLE = 5

        x1_dram = nc.dram_tensor("x1_scratch", [P, KT, T], F32, kind="Internal").ap()
        q_dram = nc.dram_tensor("q_scratch", [NS, HP * P], F32, kind="Internal").ap()

        win_v, wout_v, wup_v, wdn_v = (w.rearrange("o (k p) n -> p (o k) n", p=P)
                                       for w in (w_in, w_out, w_up, w_down))
        wbr_v = w_branch.rearrange("o b (k p) n -> p (o b) k n", p=P)

        sems = {}

        def sem(name):
            if name not in sems:
                sems[name] = ctx.enter_context(nc.semaphore(name))
            return sems[name]

        w_landed = [sem("w_landed0"), sem("w_landed1")]
        ps_free = [sem("ps_free0"), sem("ps_free1")]
        tail_out = [sem("tail_out0"), sem("tail_out1")]
        y_out_done = [sem(f"y_out_done{i}") for i in range(4)]
        page_in = [sem(f"page_in{i}") for i in range(4)]
        qbc_in = [sem(f"qbc_in{i}") for i in range(4)]
        x_in = [sem(f"x_in{i}") for i in range(NT // 2 + 2)]
        in_free = [sem("in_free0"), sem("in_free1")]
        (
            params_in, gpre_in, consts, par_ps, par_sb, ss_made, std_made, rs_made, xn_made, xt_ps,
            h_hi_made, w_hi_made, w_lo_made, unit_done, biasp_made, q_hi_made, kf_made, k_hi_made,
            ktok_ps, ktok_made, vtok_ps, vtok_made, small_ps, small_made, tok_out, z_ready,
            abs_made, e_made, l_ready, spn_ready, hi_ready, sp_ready, later_ready, cum_ready,
            att_ready, pv_done, yc_hi_made, yc_made, pad_zero, own_mask, own_made, dec_o_ps, xg_ps,
            xg_sb, part_ps, msq_made, ssm_ps, ln_made, rm_made, rx_made, x1_even, x1_odd, xsq_made,
            sx_used, fpart_ps, f_summed, fsq_made, ssf_ps, rf_made, y_even, y_odd, stack_in, a_ps,
            a_out, tail_cols, st_in, pt_in, sgw_masked, sg_ps, sg_sb, vsgtok_ps, vsgtok_made,
            mixed_ps, spat_made, kq_made, zd_made, zb_made, dec_abs, dec_e, dec_l, dec_sp, dec_cum,
            dec_arg, dec_att, dec_pv, ydec_hi, ydec_made, sgv_ps, sgv_sb, pads_made, win_step,
            pool_edge, pool_pre, pool_d, ya_ps, y_hi_made, mix_made, yb_made, mhi_made, m_split,
            sq_made, ss_added, xr_in, mr_made, hn_made, hn_hi, h2_made, x1_out, conv_step,
            gelu_made, gv_made, g_hi_made, g_made, tail_ps, tail_sb, x1r_in, yr_made, yt_ps,
            yt_left, yt_right, hi_begun, out_done, ss_zero
        ) = (sem(n) for n in (
            "params_in", "gpre_in", "consts", "par_ps", "par_sb", "ss_made", "std_made", "rs_made",
            "xn_made", "xt_ps", "h_hi_made", "w_hi_made", "w_lo_made", "unit_done", "biasp_made",
            "q_hi_made", "kf_made", "k_hi_made", "ktok_ps", "ktok_made", "vtok_ps", "vtok_made",
            "small_ps", "small_made", "tok_out", "z_ready", "abs_made", "e_made", "l_ready",
            "spn_ready", "hi_ready", "sp_ready", "later_ready", "cum_ready", "att_ready", "pv_done",
            "yc_hi_made", "yc_made", "pad_zero", "own_mask", "own_made", "dec_o_ps", "xg_ps",
            "xg_sb", "part_ps", "msq_made", "ssm_ps", "ln_made", "rm_made", "rx_made", "x1_even",
            "x1_odd", "xsq_made", "sx_used", "fpart_ps", "f_summed", "fsq_made", "ssf_ps",
            "rf_made", "y_even", "y_odd", "stack_in", "a_ps", "a_out", "tail_cols", "st_in",
            "pt_in", "sgw_masked", "sg_ps", "sg_sb", "vsgtok_ps", "vsgtok_made", "mixed_ps",
            "spat_made", "kq_made", "zd_made", "zb_made", "dec_abs", "dec_e", "dec_l", "dec_sp",
            "dec_cum", "dec_arg", "dec_att", "dec_pv", "ydec_hi", "ydec_made", "sgv_ps", "sgv_sb",
            "pads_made", "win_step", "pool_edge", "pool_pre", "pool_d", "ya_ps", "y_hi_made",
            "mix_made", "yb_made", "mhi_made", "m_split", "sq_made", "ss_added", "xr_in", "mr_made",
            "hn_made", "hn_hi", "h2_made", "x1_out", "conv_step", "gelu_made", "gv_made",
            "g_hi_made", "g_made", "tail_ps", "tail_sb", "x1r_in", "yr_made", "yt_ps", "yt_left",
            "yt_right", "hi_begun", "out_done", "ss_zero"))
        BEGIN = [(ps_free[0], 1), (ps_free[1], 1), (w_lo_made, 2), (sp_ready, 3), (cum_ready, 3),
                 (pv_done, 2), (tok_out, 16), (yc_made, 1), (small_made, 2), (mix_made, 2), (g_made, 1),
                 (ss_added, 1), (ss_made, 1)]
        TOK_DMAS = 7
        NCONST = 5 + PB
        NPARAMS = 10
        IN_BATCHES = [range(0, 1)] + [range(n, min(n + 2, NT)) for n in range(1, NT, 2)] + [range(NT, NT + 1)]
        PAR_COLS = NORM_COLS + 4 * 2 * FT
        ST_AT = 212
        ST0 = (512 - ST_AT) // (2 * NS)
        LAST_DOWN = f"down{len(FFN_GROUPS) - 1}"
        yt_buf = [ps_flat[1], misc]
        dec_sums = banks[3][:, 0:NE * H]
        dec_rows = misc[0:NS * H, 0:HP * P]
        dec_o = misc[:, 512:512 + HP * NS].rearrange("p (a b) -> p a b", a=HP)

        block = ctx.enter_context(nc.Block())

        @block.sync
        def _(sp):
            for s, n in BEGIN:
                sp.sem_inc(s, n)

            def fetch(u, par, src):
                sp.wait_ge(w_lo_made, u + 1)
                sp.dma_start(stage[par][:, 0:src.shape[1], :], src).then_inc(w_landed[par], 16)

            def col(v, c):
                return v[:, :, bass.ds(c * P, P)]

            def mix_tiles(d, first, branch):
                fetch(d * 2 + first, 0, col(win_v, d + (C_G + branch * KT)))
                fetch(d * 2 + (first + 1), 1, wbr_v[:, branch, :, bass.ds(d * P, P)])

            def fetch_mix(first, branch, begin=0):
                with sp.Fori(begin, KT) as d:
                    mix_tiles(d, first, branch)

            for n in range(NT):
                sp.dma_start(x_tok[:, n, :], x_prompt[0, n * P:(n + 1) * P, :]).then_inc(x_in[(n + 1) // 2], 16)
                if n == 2:
                    fetch(0, 0, col(win_v, C_Q))
            sp.dma_start(x_tok[0:NS, NT, :], x_sample.rearrange("b t d -> (b t) d")).then_inc(x_in[NT // 2 + 1], 16)
            fetch(1, 1, col(win_v, C_K))
            rows = [(norm_rows[n * KT:(n + 1) * KT, :], v.rearrange("o (k p) -> (o k) p", p=P))
                    for n, v in enumerate((norm_mix_post, norm_ffn_pre, norm_ffn_post))]
            rows += [(norm_rows[3 * KT:NORM_COLS, :], pool_scale.rearrange("o (k p) -> (o k) p", p=P)),
                     (conv_rows[:, 0:3, :], conv_w.rearrange("o j (f p) -> f (o j) p", p=P)),
                     (conv_rows[:, 3, :], conv_b.rearrange("o (f p) -> (o f) p", p=P)),
                     (st_rows[:, :], state_conv.rearrange("o b j c -> (o b j) c")),
                     (bias_h[:, :], sb_bias[0, :].partition_broadcast(P))]
            for dst, src in rows:
                sp.dma_start(dst, src).then_inc(params_in, 16)
            with nc.allow_non_contiguous_dma(reason="one element of each group"):
                sp.dma_start(w00[:, :], sg_w[0, :, 0, 0].partition_broadcast(P)).then_inc(params_in, 16)
                sp.dma_start(b0[:, :], sg_b[0, :, 0].partition_broadcast(P)).then_inc(params_in, 16)
            sp.dma_start(pool_sample[0, :, 0:PB - 1, :], state_pool[0, :, 1:PB, :]).then_inc(out_done, 16)
            sp.dma_start(conv_sample[0, :, 0, :], state_conv[0, :, 1, :]).then_inc(out_done, 16)

            def stack_pair(p):
                sp.wait_ge(q_hi_made, p * 2 + 2)
                for hh in range(2):
                    sp.dma_start(q_st[hh][HEAD_ROWS[1 - hh], :].bitcast(F32), q_st[hh][HEAD_ROWS[hh], :].bitcast(F32)).then_inc(stack_in, 16)
                sp.wait_ge(ps_free[1], p + freed("att", 1, 1))
                for hh in range(2):
                    sp.dma_start(k_st[hh][HEAD_ROWS[1 - hh], :].bitcast(F32), k_lo[HEAD_ROWS[hh], :].bitcast(F32)).then_inc(stack_in, 16)

            def store_pair(p):
                sp.wait_ge(ktok_made, p + 1)
                sp.dma_start(k_prompt[0, 0, :, bass.ds(p * 2, 2), :].rearrange("(n q) h d -> q n (h d)", q=P),
                             k_tok[:, :, :]).then_inc(tok_out, 16)
                sp.wait_ge(vtok_made, p + 1)
                sp.dma_start(v_prompt[0, 0, :, bass.ds(p * 2, 2), :].rearrange("(n q) h d -> q n (h d)", q=P),
                             v_tok[:, :, :]).then_inc(tok_out, 16)
                sp.wait_ge(small_made, p * 2 + 4)
                sp.dma_start(q_dram[:, bass.ds(p * P, P)], small_tok[0:NS, 0, :]).then_inc(tok_out, 16)
                for j, dst in ((1, k_sample), (2, v_sample)):
                    sp.dma_start(dst[0, :, 0, bass.ds(p * 2, 2), :].rearrange("b h d -> b (h d)"),
                                 small_tok[0:NS, j, :]).then_inc(tok_out, 16)
                sp.dma_start(pool_prompt[0, 0, :, bass.ds(p * P, P)], small_tok[0:PB, 3, :]).then_inc(tok_out, 16)
                sp.dma_start(pool_sample[0, :, PB - 1, bass.ds(p * P, P)],
                             small_tok[PB:PTAIL, 3, :]).then_inc(tok_out, 16)

            with sp.Fori(0, HP - 1) as p:
                for j, c in ((2, C_VV), (3, C_A), (4, C_Q + 1), (5, C_K + 1)):
                    fetch(p * 4 + j, j % 2, col(win_v, p + c))
                    if j == 3:
                        stack_pair(p)
                store_pair(p)
            fetch(U_SG - 2, 0, col(win_v, C_VV + HP - 1))
            fetch(U_SG - 1, 1, col(win_v, C_A + HP - 1))
            stack_pair(HP - 1)
            for g in range(2):
                fetch(U_SG + g, g, col(win_v, C_V + g))
            store_pair(HP - 1)
            for g in range(2, SG):
                fetch(U_SG + g, g % 2, col(win_v, C_V + g))
            sp.wait_ge(yc_made, HP + 1)
            sp.wait_ge(tok_out, 16 * (TOK_DMAS * HP + 1))
            sp.dma_start(sp_rows[:, :], state_pool.rearrange("o b j c -> (o b j) c")).then_inc(st_in, 16)
            sp.dma_start(sgw_rows[:, :, :], sg_w.rearrange("o g t s -> t (o g) s")).then_inc(st_in, 16)
            sp.dma_start(sgb_row[:, :], sg_b.rearrange("o g t -> o (g t)")).then_inc(st_in, 16)
            sp.dma_start(poolw[:, :, :], pool_w.rearrange("o g c d -> c (o g) d")).then_inc(st_in, 16)
            sp.dma_start(pt_sb[:, :], page_table.rearrange("(o b) j -> o (b j)", o=1)).then_inc(pt_in, 16)
            sp.wait_ge(pt_in, 16)
            for which, cache in enumerate((cache_k, cache_v)):
                for e in range(NE):
                    n = which * NE + e
                    if 4 <= n < NE + 4:
                        sp.wait_ge(kq_made, n - 3)
                    elif n >= NE + 4:
                        sp.wait_ge(dec_pv, n - 3 - NE)
                    if which == 0 and e % NPG == 0:
                        b = e // NPG
                        if b >= 4:
                            sp.wait_ge(kq_made, (b - 3) * NPG)
                        sp.dma_start(q_bc[:, b % 4, :], q_dram[b, :].partition_broadcast(P)
                                     ).then_inc(qbc_in[b % 4], 16)
                    page = sp.value_load(pt_sb[0:1, e:e + 1], min_val=0, max_val=NPOOL - 1)
                    sp.dma_start(kv_pg[:, n % 4, :],
                                 cache[0, bass.ds(page, 1), :, :, :].rearrange("o t h d -> (o t) (h d)")
                                 ).then_inc(page_in[n % 4], 16)
                    if n == NE // 2:
                        mix_tiles(0, U_MIXC, 2)
            fetch_mix(U_MIXC, 2, 1)
            sp.wait_ge(sgv_sb, 1)
            sp.dma_start(sgv_sample[0, :, 0, :], sgv_tok[:, :]).then_inc(out_done, 16)
            fetch_mix(U_MIXA, 0)
            with sp.Fori(0, SG // 2) as i:
                for j in range(2):
                    fetch(i * 2 + (U_U + j), j, col(win_v, i * 2 + (C_U + j)))
            fetch_mix(U_MIXB, 1)
            with sp.Fori(0, KT // 2) as i:
                for j in range(2):
                    fetch(i * 2 + (U_OUT + j), j, col(wout_v, i * 2 + j))
            for g, (f0, size) in enumerate(FFN_GROUPS):
                def up_tiles(j):
                    fetch(j * 2 + U_UP[g], 0, col(wup_v, j + f0))
                    fetch(j * 2 + (U_UP[g] + 1), 1, col(wup_v, j + (f0 + FT)))
                if g == 0:
                    up_tiles(0)
                    sp.wait_ge(x1_even, NCH * KT // 2)
                    sp.wait_ge(x1_odd, NCH * KT // 2)
                    sp.dma_start(x1_dram, trunk[:, :, :]).then_inc(x1_out, 16)
                with sp.Fori(1 if g == 0 else 0, size) as j:
                    up_tiles(j)
                def down_tiles(i):
                    for j in range(2):
                        fetch(i * 2 + (U_DOWN[g] + j), j,
                              wdn_v[:, f0:f0 + size, bass.ds((i * 2 + j) * P, P)])
                last_group = g == len(FFN_GROUPS) - 1
                if last_group:
                    for i in range(2):
                        down_tiles(i)
                    sp.wait_ge(unit_done, U_DOWN[g])
                    sp.wait_ge(x1_out, 16)
                    sp.dma_start(x1_back[:, :, :], x1_dram).then_inc(x1r_in, 16)
                with sp.Fori(2 if last_group else 0, KT // 2) as i:
                    down_tiles(i)
            for n in range(2 * FT // 4):
                sp.wait_ge(tail_sb, n + 1)
                rows = up[n % 2][0:TAIL, 0:4 * P]
                sp.dma_start(conv_prompt[0, 0, :, n * 4 * P:(n + 1) * 4 * P], rows[0:2, :]).then_inc(tail_out[n % 2], 16)
                sp.dma_start(conv_sample[0, :, 1, n * 4 * P:(n + 1) * 4 * P], rows[2:TAIL, :]).then_inc(tail_out[n % 2], 16)
            for n in range(NT):
                sp.wait_ge(yt_left, n + 1)
                if n >= Y_WHOLE:
                    sp.wait_ge(yt_right, n - Y_WHOLE + 1)
                sp.dma_start(y_prompt[0, n * P:(n + 1) * P, :], y_tok[:, n % 4, :]).then_inc(y_out_done[n % 4], 16)
            sp.wait_ge(yt_left, NT + 1)
            sp.wait_ge(yt_right, NT + 1 - Y_WHOLE)
            sp.dma_start(y_sample.rearrange("b t d -> (b t) d"), y_tok[0:NS, NT % 4, :]).then_inc(y_out_done[NT % 4], 16)
            for k in range(4):
                sp.wait_ge(y_out_done[k], 16 * ((NT + 4 - k) // 4))
            sp.wait_ge(out_done, 16 * 3)
            for k in range(2):
                sp.wait_ge(tail_out[k], 32 * ((2 * FT // 4 + 1 - k) // 2))
            sp.wait_ge(tok_out, 16 * (TOK_DMAS * HP + 1))

        @block.gpsimd
        def _(pool):
            def split_hi(par, n16, u):
                pool.wait_ge(w_landed[par], n16)
                if u is not None:
                    pool.wait_ge(unit_done, u - 1)
                    pool.sem_inc(hi_begun, 1)
                nc.gpsimd.tensor_scalar(w_hi[par][:, :, :], stage[par][:, :, :], 1.0, 0.0,
                                        ALU.mult, ALU.add).then_inc(w_hi_made, 1)

            def split_stage(first, count):
                with pool.Fori(0, count // 2) as i:
                    for j in range(2):
                        split_hi(j, i * 16 + 16 * (first // 2 + 2), i * 2 + (first + 2 + j))

            nc.gpsimd.memset(ident[:, :], 0.0).then_inc(consts, 1)
            nc.gpsimd.memset(ones[:, :], 1.0).then_inc(consts, 1)
            nc.gpsimd.memset(neg_ones[:, :], -1.0).then_inc(consts, 1)
            nc.gpsimd.memset(mask_b[:, :], NEG).then_inc(consts, 1)
            nc.gpsimd.memset(eps[:, :], 1e-6).then_inc(consts, 1)
            for t in range(PB):
                nc.gpsimd.memset(inv_cnt[:, t:t + 1], 1.0 / (t + 1)).then_inc(consts, 1)
            pool.wait_ge(consts, NCONST)
            nc.gpsimd.affine_select(out=ident[:, :], in_=ident[:, :], compare_op=ALU.not_equal, fill=1.0,
                                    base=0, pattern=[[-1, P]], channel_multiplier=1).then_inc(consts, 1)
            nc.gpsimd.affine_select(out=neg_tri[:, :], in_=neg_ones[:, :], compare_op=ALU.is_ge, fill=0.0,
                                    base=0, pattern=[[-1, P]], channel_multiplier=1).then_inc(consts, 1)
            nc.gpsimd.affine_select(out=mask_b[:, :], in_=mask_b[:, :], compare_op=ALU.is_ge, fill=0.0,
                                    base=0, pattern=[[-1, P]], channel_multiplier=1).then_inc(consts, 1)
            pool.wait_ge(consts, NCONST + 1)
            nc.gpsimd.tensor_copy(ident_b[:, :], ident[:, :]).then_inc(consts, 1)
            split_hi(0, 16, None)
            split_hi(1, 16, None)
            with pool.Fori(0, HP) as p:
                for j in range(2):
                    split_hi(j, p * 32 + 32, p * 4 + (2 + j))
                for c, (hh, kb, q0, W, top, last) in enumerate(CHUNKS):
                    if c in NEXT_SPLITS:
                        j = NEXT_SPLITS.index(c)
                        split_hi(j, p * 32 + 48, p * 4 + (4 + j))
                    pool.wait_ge(spn_ready, p * NCK + (c + 1))
                    pool.wait_ge(cum_ready, p * NCK + (c + 1))
                    pool.sem_inc(hi_begun, 1)
                    nc.gpsimd.tensor_scalar(sp_hi[c % 3][:, 0:W], zl[c % 4][:, 0:W], bias_p[:, hh:hh + 1], 1.0,
                                            ALU.add, ALU.mult).then_inc(hi_ready, 1)
            pool.wait_ge(yc_made, HP + 1)
            pool.wait_ge(tok_out, 16 * (TOK_DMAS * HP + 1))
            nc.gpsimd.memset(a_raw[:, :, 0:PAD], 0.0).then_inc(pads_made, 1)
            for w in win:
                nc.gpsimd.memset(w[:, 0:PAD], 0.0).then_inc(pads_made, 1)
            pool.wait_ge(st_in, 64)
            for g in range(SG):
                nc.gpsimd.affine_select(out=sgw_rows[:, g, :], in_=sgw_rows[:, g, :], compare_op=ALU.is_ge,
                                        fill=0.0, base=0, pattern=[[-1, P]], channel_multiplier=1
                                        ).then_inc(sgw_masked, 1)
            pool.wait_ge(pads_made, 3)
            step = 0
            for g in range(SG):
                split_hi(g % 2, 16 * (U_SG // 2 + 2 + g // 2), U_SG + 2 + g)
                src = a_raw[:, g, 0:PAD + TP]
                for m in range(g + 1):
                    if g > 0 and m == 0:
                        pool.wait_ge(pool_d, 3 * g)
                    if m > 0:
                        pool.wait_ge(win_step, step)
                    dst = win[m % 2]
                    nc.gpsimd.tensor_tensor(dst[:, PAD:PAD + TP], src[:, PAD:PAD + TP],
                                            src[:, PAD - 2 ** m:PAD + TP - 2 ** m], ALU.add
                                            ).then_inc(win_step, 1)
                    step += 1
                    src = dst
            pool.wait_ge(sg_ps, 1)
            own3 = own.rearrange("p (h d) -> p h d", h=H)
            nc.gpsimd.memset(own, 1.0).then_inc(own_mask, 1)
            for i, (row, head, base) in enumerate(((1, -NS, 0), (-1, NS, NS - 1))):
                pool.wait_ge(own_mask, i + 1)
                nc.gpsimd.affine_select(out=own3, in_=own3, compare_op=ALU.is_ge, fill=0.0, base=base,
                                        pattern=[[head, H], [0, DH]], channel_multiplier=row).then_inc(own_mask, 1)
            pool.wait_ge(zd_made, NE)
            nc.gpsimd.memset(a_pad, 0.0).then_inc(pad_zero, 1)
            split_stage(U_MIXC, U_UP[0] - 2 - U_MIXC)
            for c in range(NCH):
                for k in range(0, KT, 2):
                    pool.wait_ge(mr_made, c * KT + k + 1)
                    if c == 0 and k == 0:
                        pool.wait_ge(xg_sb, len(XT_GROUPS))
                    nc.gpsimd.tensor_tensor(trunk[:, k, cols[c]], trunk[:, k, cols[c]], x_t[:, k, cols[c]], ALU.add
                                            ).then_inc(x1_even, 1)
                if c == 0:
                    for j in range(2):
                        split_hi(j, 16 * (U_UP[0] // 2 + 1), U_UP[0] + j)
            split_stage(U_UP[0], U_END - 2 - U_UP[0])
            for c in range(NCH):
                for k in range(0, KT, 2):
                    pool.wait_ge(yr_made, c * KT + k + 1)
                    if c == 0 and k == 0:
                        pool.wait_ge(x1r_in, 16)
                    nc.gpsimd.tensor_tensor(trunk[:, k, cols[c]], trunk[:, k, cols[c]], x1_back[:, k, cols[c]], ALU.add
                                            ).then_inc(y_even, 1)

        @block.scalar
        def _(act):
            A = nc.scalar.activation

            act.preload_act_table_set("sqrt_and_others")
            act.dma_start(g_pre[:, :], norm_mix_pre[0, :].partition_broadcast(P)).then_inc(gpre_in, 16)

            act.wait_ge(consts, NCONST + 4)
            for b in range(len(IN_BATCHES) + 1):
                if b < len(IN_BATCHES):
                    tiles = IN_BATCHES[b]
                    n0_, n1_ = tiles[0], tiles[-1] + 1
                    m = P if n0_ < NT else NS
                    act.wait_ge(x_in[b], 16 * len(tiles))
                    for n in tiles:
                        act.wait_ge(ss_made, n + 1)
                        A(sq[0:m, 0:D], x_tok[0:m, n, :], ACT.Square, accum_out=ss[0:m, n:n + 1]).then_inc(ss_made, 1)
                    act.wait_ge(ss_made, n1_ + 1)
                    A(std[0:m, n0_:n1_], ss[0:m, n0_:n1_], ACT.Sqrt, bias=eps[0:m, :], scale=1.0 / D
                      ).then_inc(std_made, 1)
                for n in (IN_BATCHES[b - 1] if b > 0 else []):
                    m = P if n < NT else NS
                    act.wait_ge(xt_ps, n + 1)
                    A(h_hi[:, :, n * P:n * P + m],
                      in_ps[n % 2][:, 0:KT * m].rearrange("p (k t) -> p k t", k=KT), ACT.Copy).then_inc(h_hi_made, 1)
            act.wait_ge(par_ps, 1)
            A(par_t[:, :], misc[:, 0:PAR_COLS], ACT.Copy).then_inc(par_sb, 1)
            A(conv_st[:, 0:ST0, :, :].rearrange("p f b j -> p (f b j)"),
              misc[:, ST_AT:ST_AT + ST0 * 2 * NS], ACT.Copy).then_inc(par_sb, 1)
            A(conv_st[:, ST0:, :, :].rearrange("p f b j -> p (f b j)"),
              misc[:, 512:512 + (2 * FT - ST0) * 2 * NS], ACT.Copy).then_inc(par_sb, 1)

            act.preload_act_table_set("natural_log_exp_and_others")
            with act.Fori(0, HP) as p:
                act.wait_ge(unit_done, p * 4 + 1)
                A(q_dec[:, :], last_cols(0, NS), ACT.Copy, scale=SCALE)
                for hh, r in enumerate(HEAD_ROWS):
                    A(chunks(q_st[hh][r, :]), ps[0][r], ACT.Copy, scale=SCALE).then_inc(q_hi_made, 1)
                act.wait_ge(unit_done, p * 4 + 2)
                A(chunks(k_f[:, :]), ps[1], ACT.Copy).then_inc(kf_made, 1)
                for hh, r in enumerate(HEAD_ROWS):
                    A(chunks(k_st[hh][r, :]), ps[1][r], ACT.Copy).then_inc(k_hi_made, 1)
                act.wait_ge(unit_done, p * 4 + 3)
                A(chunks(v_f[:, :]), ps[0], ACT.Copy).then_inc(ps_free[0], 1)
                act.wait_ge(biasp_made, p * 2 + 2)

                def soft_abs(c):
                    hh, kb, q0, W, top, last = CHUNKS[c]
                    act.wait_ge(z_ready, p * NCK + (c + 1))
                    act.wait_ge(sp_ready, p * NCK + (c + 1))
                    A(zl[c % 4][:, 0:W], z_bank[c][:, 0:W], ACT.Abs, bias=bias_p[:, hh:hh + 1]).then_inc(abs_made, 1)

                def soft_exp(c):
                    t = zl[c % 4][:, 0:CHUNKS[c][3]]
                    act.wait_ge(abs_made, p * NCK + (c + 1))
                    A(t, t, ACT.Exp, scale=-1.0).then_inc(e_made, 1)

                def soft_ln(c):
                    t = zl[c % 4][:, 0:CHUNKS[c][3]]
                    act.wait_ge(e_made, p * NCK + (c + 1))
                    A(t, t, ACT.Ln, bias=ones[:, 0:1]).then_inc(l_ready, 1)

                def weights(c):
                    hh, kb, q0, W, top, last = CHUNKS[c]
                    act.wait_ge(cum_ready, p * NCK + (c + 4))
                    act.wait_ge(pv_done, p * NCK + (c + 1))
                    A(att[c % 2][:, 0:W], z_bank[c][:, 0:W], ACT.Exp, bias=bias_p[:, hh:hh + 1]
                      ).then_inc(att_ready, 1)

                def value_rows():
                    act.wait_ge(vtok_ps, p + 1)
                    act.wait_ge(tok_out, p * (16 * TOK_DMAS) + 16)
                    A(v_tok[:, :, :].rearrange("p a b -> p (a b)"), misc, ACT.Copy).then_inc(vtok_made, 1)

                def small_rows():
                    act.wait_ge(small_ps, p + 1)
                    A(small_tok[0:NS, 0:3, :].rearrange("p a b -> p (a b)"), a_bank[0:NS, 0:3 * P],
                      ACT.Copy).then_inc(small_made, 1)
                    A(small_tok[:, 3, :], a_bank[0:PTAIL, 3 * P:4 * P], ACT.Copy).then_inc(small_made, 1)

                for c in range(NCK + LAG_EXP):
                    if c >= LAG_EXP:
                        weights(c - LAG_EXP)
                    if c < NCK:
                        soft_abs(c)
                    if 0 < c <= NCK:
                        soft_ln(c - 1)
                    if c < NCK:
                        soft_exp(c)
                    if c == 0:
                        value_rows()
                    if c == SMALL_STEP + 1:
                        small_rows()
                act.wait_ge(pv_done, p * NCK + (NCK + 2))
                A(y_hi[:, bass.ds(p, 1), 0:TP].rearrange("p o t -> p (o t)"), misc, ACT.Copy).then_inc(yc_hi_made, 1)

            def vsg_out(g):
                par = g % 2
                act.wait_ge(unit_done, U_SG + g + 1)
                if g == 0:
                    act.wait_ge(yc_made, HP + 1)
                    act.wait_ge(tok_out, 16 * (TOK_DMAS * HP + 1))
                A(chunks(vsg_f[par]), ps[par], ACT.Copy)
                A(vsg_dec[:, g, :], last_cols(par, NS), ACT.Copy)
                A(spat[:, g, TP:T], last_cols(par, NS), ACT.Identity, bias=b0[:, g:g + 1],
                  scale=w00[:, g:g + 1]).then_inc(ps_free[par], 1)

            def mix_out(g):
                act.wait_ge(mixed_ps, g + 1)
                A(spat[:, g, 0:TP], misc, ACT.Copy).then_inc(spat_made, 1)

            vsg_out(0)
            vsg_out(1)
            act.wait_ge(sg_ps, 1)
            A(sgw_t[:, :, :].rearrange("p g t -> p (g t)"), misc[:, 0:SG * P], ACT.Copy).then_inc(sg_sb, 1)
            A(pool_st[:, :, :].rearrange("p g t -> p (g t)"), misc[:, 512:512 + SG * NS * PB], ACT.Copy
              ).then_inc(sg_sb, 1)
            mix_out(0)
            vsg_out(2)
            mix_out(1)
            vsg_out(3)
            mix_out(2)
            act.wait_ge(zb_made, 1)
            A(t_dec[:], z_dec[:], ACT.Abs).then_inc(dec_abs, 1)
            act.wait_ge(dec_abs, 1)
            A(t_dec[:], t_dec[:], ACT.Exp, scale=-1.0).then_inc(dec_e, 1)
            act.wait_ge(dec_e, 1)
            A(t_dec[:], t_dec[:], ACT.Ln, bias=ones[:, 0:1]).then_inc(dec_l, 1)
            act.wait_ge(dec_arg, 1)
            act.wait_ge(pad_zero, 1)
            A(a_dec, z_dec[:], ACT.Exp).then_inc(dec_att, 1)
            act.wait_ge(sgv_ps, 1)
            A(sgv_tok[:, :], banks[4][0:NS, 0:SG * P], ACT.Copy).then_inc(sgv_sb, 1)
            mix_out(3)
            act.wait_ge(dec_o_ps, 1)
            A(y_hi[:, :, TP:T], dec_o, ACT.Copy).then_inc(ydec_hi, 1)

            act.preload_act_table_set("sigmoid_and_others")

            def gates(name, first, adds):
                with act.Fori(0, KT // 2) as i:
                    for k in range(2):
                        act.wait_ge(unit_done, i * 4 + (first + 2 * k + 1))
                        if adds is None:
                            act.wait_ge(ps_free[1], i * 2 + freed(name, 1, k - 1))
                        else:
                            act.wait_ge(mix_made, i * 2 + (adds + k + 1))
                        A(chunks(gate[k][:, :]), ps[0], ACT.Sigmoid).then_inc(ps_free[0], 1)

            gates("mixc", U_MIXC, None)
            for g in range(SG):
                act.wait_ge(ya_ps, g + 1)
                A(chunks(y_hi[:, g, :]), ps[g % 2], ACT.Copy, scale=a_scale[:, g:g + 1]).then_inc(y_hi_made, 1)
            gates("mixa", U_MIXA, 0)
            with act.Fori(0, SG // 2) as i:
                for k in range(2):
                    act.wait_ge(ps_free[k], i + freed("u", k, 1))
                    A(y_hi[:, bass.ds(i * 2 + k, 1), :], spat[:, bass.ds(i * 2 + k, 1), :], ACT.Copy
                      ).then_inc(y_hi_made, 1)
            gates("mixb", U_MIXB, KT)
            act.wait_ge(unit_done, U_OUT - 1)
            with act.Fori(0, KT) as k:
                act.wait_ge(mix_made, k + (2 + KT + 1))
                A(h_hi[:, bass.ds(k, 1), :], trunk[:, bass.ds(k, 1), :], ACT.Copy).then_inc(mhi_made, 1)
            act.preload_act_table_set("natural_log_exp_and_others")

            act.wait_ge(m_split, KT)
            act.dma_start(xr_tok[:, 0:NT, :], x_prompt.rearrange("o (n q) d -> q (o n) d", q=P)).then_inc(xr_in, 16)
            act.dma_start(xr_tok[0:NS, NT, :], x_sample.rearrange("b t d -> (b t) d")).then_inc(xr_in, 16)

            def m_out(i, k):
                t = bass.ds(i * 2 + k, 1)
                act.wait_ge(unit_done, i * 2 + (U_OUT + k + 1))
                A(trunk[:, t, :].rearrange("p o (a b) -> p (o a) b", a=NCH), ps[k], ACT.Copy, scale=g_post[:, t])
                act.wait_ge(ss_added, i * 2 + (k + 1))
                A(chunks(sq), ps[k], ACT.Square).then_inc(ps_free[k], 1)

            def x_out(first, end):
                for n in range(first, min(end, len(XT_GROUPS))):
                    half, k = XT_GROUPS[n]
                    src = misc[:, (n % 2) * 512:(n % 2 + 1) * 512]
                    act.wait_ge(xg_ps, n + 1)
                    if half < 2:
                        A(x_t[:, k, half * 512:(half + 1) * 512], src, ACT.Copy).then_inc(xg_sb, 1)
                    else:
                        A(x_t[:, :, TP:T], src[:, 0:KT * NS].rearrange("p (k b) -> p k b", k=KT), ACT.Copy
                          ).then_inc(xg_sb, 1)

            def m_part_out(n):
                u, c = M_PARTS[6 + n]
                if c < NCH - 1:
                    act.wait_ge(part_ps, n + 1)
                else:
                    act.wait_ge(unit_done, U_OUT + u + 1)
                A(trunk[:, u, cols[c]], ps[u % 2][:, c, :], ACT.Copy, scale=g_post[:, u:u + 1])
                if n >= 3:
                    act.wait_ge(ss_added, SUMS0 + (n - 2))
                A(m_sq[n % 3][:, :], ps[u % 2][:, c, :], ACT.Square).then_inc(msq_made, 1)

            def rstd_of(c, made, step, psum):
                A(rstd[:, cols[c]], psum, ACT.Ln, bias=eps[:, :], scale=1.0 / D).then_inc(ln_made, 1)
                act.wait_ge(ln_made, step)
                A(rstd[:, cols[c]], rstd[:, cols[c]], ACT.Exp, scale=-0.5).then_inc(made, 1)

            LN_ORDER = [("m", 0), ("x1", 0), ("m", 1), ("m", 2), ("x1", 1), ("x1", 2)]

            def rstd_m(c):
                act.wait_ge(ssm_ps, c + 1)
                rstd_of(c, rm_made, LN_ORDER.index(("m", c)) + 1, ps[0][:, c, :])

            def rstd_x(c):
                act.wait_ge(sx_used, (c + 1) * KT)
                rstd_of(c, rx_made, LN_ORDER.index(("x1", c)) + 1, ps[1][:, c, :])

            def x1_squares(c, first, end):
                for k in range(first, end):
                    j = c * KT + k
                    act.wait_ge(x1_odd if k % 2 else x1_even, c * (KT // 2) + k // 2 + 1)
                    if j >= len(x_sq):
                        act.wait_ge(sx_used, j + 1 - len(x_sq))
                    else:
                        act.wait_ge(ss_added, SUMS0)
                    A(x_sq[j % len(x_sq)], trunk[:, k, cols[c]], ACT.Square).then_inc(xsq_made, 1)

            def h_out(c):
                for k in range(KT):
                    act.wait_ge(hn_made, c * KT + k + 1)
                    A(h_hi[:, k, cols[c]], hn[(c * KT + k) % 3][:, :], ACT.Copy).then_inc(hn_hi, 1)

            with act.Fori(0, KT // 2 - 2) as i:
                for k in range(2):
                    m_out(i, k)
            x_out(0, 6)
            m_out(KT // 2 - 2, 0)
            x_out(6, 10)
            x_out(10, 12)
            m_out(KT // 2 - 2, 1)
            m_part_out(0)
            x_out(12, 14)
            m_part_out(1)
            x_out(14, 16)
            m_part_out(2)
            x_out(16, 18)
            rstd_m(0)
            x1_squares(0, 0, KT // 2)
            m_part_out(3)
            x1_squares(0, KT // 2, KT)
            rstd_x(0)
            rstd_m(1)
            m_part_out(4)
            h_out(0)
            m_part_out(5)
            x1_squares(1, 0, len(x_sq))
            rstd_m(2)
            x1_squares(1, len(x_sq), KT)
            x1_squares(2, 0, len(x_sq) - 1)
            rstd_x(1)
            x1_squares(2, len(x_sq) - 1, KT)
            h_out(1)
            rstd_x(2)
            h_out(2)

            for g, (f0, size) in enumerate(FFN_GROUPS):
                act.preload_act_table_set("gelu_apprx_tanh_and_others")
                with act.Fori(0, size) as j:
                    act.wait_ge(g_made, j + (f0 + 1))
                    for k in range(2):
                        f = bass.ds(j + (f0 + k * FT), 1)
                        act.wait_ge(unit_done, j * 2 + (U_UP[g] + k + 1))
                        A(chunks(up[k][:, :]), ps[k], ACT.Copy)
                        A(tails[:, f, :].rearrange("p o t -> p (o t)"), last_cols(k, TAIL), ACT.Copy)
                        A(chunks(conv[k][:, :]), ps[k], ACT.Identity, bias=conv_par[:, 3, f],
                          scale=conv_par[:, 2, f]).then_inc(ps_free[k], 1)
                    act.wait_ge(conv_step, j * 8 + (8 * f0 + 4))
                    A(conv[0][:, :], conv[0][:, :], ACT.Gelu_apprx_tanh).then_inc(gelu_made, 1)
                    act.wait_ge(gv_made, j + (f0 + 1))
                    A(g_hi[:, bass.ds(j, 1), :].rearrange("p o t -> p (o t)"), conv[0][:, :], ACT.Copy
                      ).then_inc(g_hi_made, 1)
                if g == 0:
                    act.wait_ge(x1_out, 16)
                    with act.Fori(0, KT // 2) as i:
                        for k in range(2):
                            act.wait_ge(unit_done, i * 2 + (U_DOWN[g] + k + 1))
                            A(trunk[:, bass.ds(i * 2 + k, 1), :].rearrange("p o (a b) -> p (o a) b", a=NCH),
                              ps[k], ACT.Copy).then_inc(ps_free[k], 1)
            act.preload_act_table_set("natural_log_exp_and_others")
            with act.Fori(0, KT // 2 - 1) as i:
                for k in range(2):
                    act.wait_ge(ps_free[k], i + freed(LAST_DOWN, k, 1))
                    act.wait_ge(ss_added, i * 2 + (SUMS0 + 6 + k))
                    A(sq, trunk[:, bass.ds(i * 2 + k, 1), :].rearrange("p o t -> p (o t)"), ACT.Square
                      ).then_inc(sq_made, 1)

            def conv_rows_out(first, end):
                for n in range(first, min(end, ROW_GROUPS)):
                    act.wait_ge(tail_ps, n + 1)
                    if n >= 2:
                        act.wait_ge(tail_out[n % 2], 32 * (n // 2))
                    A(up[n % 2][0:TAIL, 0:4 * P], misc[0:TAIL, (n % 2) * 512:(n % 2) * 512 + 4 * P], ACT.Copy
                      ).then_inc(tail_sb, 1)

            def f_square(n):
                u, c = F_PARTS[n]
                act.wait_ge(f_summed, n + 1)
                if n >= 3:
                    act.wait_ge(ss_added, SUMS1 + (n - 2))
                A(m_sq[n % 3][:, :], trunk[:, u, cols[c]], ACT.Square).then_inc(fsq_made, 1)

            def rstd_f(c):
                act.wait_ge(ssf_ps, c + 1)
                rstd_of(c, rf_made, len(LN_ORDER) + c + 1, ps[0][:, c, :])

            def y_out(first, end):
                for n in range(first, end):
                    m = P if n < NT else NS
                    act.wait_ge(yt_ps, n + 1)
                    if n >= 4:
                        act.wait_ge(y_out_done[n % 4], 16 * (n // 4))
                    w = D if n < Y_WHOLE else 512
                    A(y_tok[0:m, n % 4, 0:w], yt_buf[n % 2][0:m, 0:w], ACT.Copy).then_inc(yt_left, 1)

            f_square(0)
            conv_rows_out(0, 2)
            f_square(1)
            conv_rows_out(2, 4)
            f_square(2)
            rstd_f(0)
            conv_rows_out(4, 8)
            f_square(3)
            conv_rows_out(8, 10)
            f_square(4)
            rstd_f(1)
            conv_rows_out(10, 12)
            f_square(5)
            rstd_f(2)
            y_out(0, NT + 1)

        @block.vector
        def _(dve):
            V = nc.vector

            def split_lo(par, u):
                dve.wait_ge(w_hi_made, u + 1)
                V.tensor_tensor(w_lo[par][:, :, :], stage[par][:, :, :], w_hi[par][:, :, :].bitcast(F32),
                                ALU.subtract).then_inc(w_lo_made, 1)

            dve.wait_ge(gpre_in, 16)
            for b in range(len(IN_BATCHES) + 1):
                if b < len(IN_BATCHES):
                    tiles = IN_BATCHES[b]
                    n0_, n1_ = tiles[0], tiles[-1] + 1
                    m = P if n0_ < NT else NS
                    dve.wait_ge(std_made, b + 1)
                    V.reciprocal(rs[0:m, n0_:n1_], std[0:m, n0_:n1_]).then_inc(rs_made, 1)
                    dve.wait_ge(rs_made, b + 1)
                    for n in tiles:
                        V.scalar_tensor_tensor(x_tok[0:m, n, :], x_tok[0:m, n, :], rs[0:m, n:n + 1], g_pre[0:m, :],
                                               ALU.mult, ALU.mult).then_inc(xn_made, 1)
                for n in (IN_BATCHES[b - 1] if b > 0 else []):
                    m = P if n < NT else NS
                    dve.wait_ge(h_hi_made, n + 1)
                    V.tensor_tensor(h_lo[:, :, n * P:n * P + m],
                                    in_ps[n % 2][:, 0:KT * m].rearrange("p (k t) -> p k t", k=KT),
                                    h_hi[:, :, n * P:n * P + m].bitcast(F32), ALU.subtract
                                    ).then_inc(in_free[n % 2], 1)
                if b == 2:
                    split_lo(0, 0)
            split_lo(1, 1)

            dve.wait_ge(params_in, 16 * NPARAMS)
            with dve.Fori(0, HP) as p:
                V.tensor_copy(bias_p[:, :], bias_h[:, bass.ds(p * 2, 2)]).then_inc(biasp_made, 1)
                V.tensor_scalar(nbias_p[:, :], bias_h[:, bass.ds(p * 2, 2)], -1.0, None, ALU.mult).then_inc(biasp_made, 1)
                for hh, r in enumerate(HEAD_ROWS):
                    dve.wait_ge(q_hi_made, p * 2 + (hh + 1))
                    lo = V.scalar_tensor_tensor(chunks(q_lo[r, :]), ps[0][r], SCALE,
                                                chunks(q_st[hh][r, :]).bitcast(F32), ALU.mult, ALU.subtract)
                lo.then_inc(ps_free[0], 1)
                split_lo(0, p * 4 + 2)
                for hh, r in enumerate(HEAD_ROWS):
                    dve.wait_ge(k_hi_made, p * 2 + (hh + 1))
                    lo = V.tensor_tensor(chunks(k_lo[r, :]), ps[1][r], chunks(k_st[hh][r, :]).bitcast(F32),
                                         ALU.subtract)
                lo.then_inc(ps_free[1], 1)
                split_lo(1, p * 4 + 3)
                dve.wait_ge(ktok_ps, p + 1)
                dve.wait_ge(tok_out, p * (16 * TOK_DMAS) + 16)
                V.tensor_copy(k_tok[:, :, :].rearrange("p a b -> p (a b)"), misc).then_inc(ktok_made, 1)
                dve.wait_ge(biasp_made, p * 2 + 2)
                nl = 0
                for c, (hh, kb, q0, W, top, last) in enumerate(CHUNKS):
                    if c in NEXT_SPLITS:
                        j = NEXT_SPLITS.index(c)
                        split_lo(j, p * 4 + (4 + j))
                    for j, (_, end) in enumerate(A_STEPS):
                        if c == end - 1:
                            if j < NCH - 1:
                                dve.wait_ge(a_ps, p * (NCH - 1) + (j + 1))
                            else:
                                dve.wait_ge(unit_done, p * 4 + 4)
                            V.tensor_copy(a_raw[:, bass.ds(p, 1), PAD + j * CH:PAD + (j + 1) * CH].rearrange(
                                "p o t -> p (o t)"), a_bank[:, 0:CH]).then_inc(a_out, 1)
                            if j == NCH - 1:
                                V.tensor_copy(a_tail[:, :], last_cols(1, PTAIL)).then_inc(tail_cols, 1)
                    t = zl[c % 4][:, 0:W]
                    dve.wait_ge(l_ready, p * NCK + (c + 1))
                    V.scalar_tensor_tensor(t, z_bank[c][:, 0:W], nbias_p[:, hh:hh + 1], t, ALU.max, ALU.add
                                           ).then_inc(spn_ready, 1)
                    if not last:
                        dve.wait_ge(spn_ready, p * NCK + (c + 1))
                        dve.wait_ge(cum_ready, p * NCK + (c + 1))
                    if top:
                        V.tensor_scalar(later[c % 4][:, 0:W], t, bias_p[:, hh:hh + 1], None, ALU.add
                                        ).then_inc(later_ready, 1)
                        nl += 1
                    elif not last:
                        Wb = CHUNKS[c - 1][3]
                        dve.wait_ge(later_ready, p * NLATER + nl)
                        V.scalar_tensor_tensor(later[c % 4][:, W - Wb:W], t[:, W - Wb:W], bias_p[:, hh:hh + 1],
                                               later[(c - 1) % 4][:, 0:Wb], ALU.add, ALU.add
                                               ).then_inc(later_ready, 1)
                        if Wb < W:
                            V.tensor_scalar(later[c % 4][:, 0:W - Wb], t[:, 0:W - Wb], bias_p[:, hh:hh + 1], None,
                                            ALU.add).then_inc(later_ready, 1)
                            nl += 1
                        nl += 1
                    dve.wait_ge(hi_ready, p * NCK + (c + 1))
                    V.scalar_tensor_tensor(sp_lo[c % 3][:, 0:W], t, bias_p[:, hh:hh + 1],
                                                sp_hi[c % 3][:, 0:W].bitcast(F32), ALU.add, ALU.subtract
                                                ).then_inc(sp_ready, 1)
                assert nl == NLATER
                dve.wait_ge(yc_hi_made, p + 1)
                V.tensor_tensor(y_lo[:, bass.ds(p, 1), 0:TP].rearrange("p o t -> p (o t)"), misc,
                                y_hi[:, bass.ds(p, 1), 0:TP].rearrange("p o t -> p (o t)").bitcast(F32),
                                ALU.subtract).then_inc(yc_made, 1)

            for g in range(SG):
                split_lo(g % 2, U_SG + 2 + g)
                for e in range(g * NE // SG, (g + 1) * NE // SG):
                    b, pg = e // NPG, e % NPG
                    if g == 0 and e == 0:
                        dve.wait_ge(yc_made, HP + 1)
                    dve.wait_ge(page_in[e % 4], 16 * (e // 4 + 1))
                    dve.wait_ge(qbc_in[b % 4], 16 * (b // 4 + 1))
                    if e > 0:
                        dve.wait_ge(zd_made, e)
                    V.tensor_tensor(kq[:, :], kv_pg[:, e % 4, :], q_bc[:, b % 4, :], ALU.mult).then_inc(kq_made, 1)
                    dve.wait_ge(kq_made, e + 1)
                    V.tensor_reduce(z_dec[:, pg, b, :], kq[:, :].rearrange("p (h d) -> p h d", h=H), AX_X, ALU.add
                                    ).then_inc(zd_made, 1)
                dve.wait_ge(vsgtok_ps, g + 1)
                V.tensor_copy(vsg_tok[:, :, :].rearrange("p a b -> p (a b)"), misc).then_inc(vsgtok_made, 1)
                w = WINDOWS[g]
                s, a = win[g % 2][:, PAD:PAD + TP], a_raw[:, g, PAD:PAD + TP]
                dve.wait_ge(win_step, (g + 1) * (g + 2) // 2)
                V.tensor_tensor(edge[:, 0:w - 1], s[:, 0:w - 1], inv_cnt[:, 0:w - 1], ALU.mult).then_inc(pool_edge, 1)
                dve.wait_ge(pool_edge, 2 * g + 1)
                V.tensor_tensor(edge[:, 0:w - 1], edge[:, 0:w - 1], a[:, 0:w - 1], ALU.subtract).then_inc(pool_edge, 1)
                dve.wait_ge(pool_edge, 2 * g + 2)
                V.scalar_tensor_tensor(a, s, 1.0 / w, a, ALU.mult, ALU.subtract).then_inc(pool_d, 1)
                dve.wait_ge(pool_d, 3 * g + 1)
                V.tensor_copy(a[:, 0:w - 1], edge[:, 0:w - 1]).then_inc(pool_d, 1)
                dve.wait_ge(sg_sb, 2)
                ad = a_raw[:, g, PAD + TP:PAD + T]
                V.tensor_reduce(pre[:, :], pool_st[:, g, :].rearrange("p (b j) -> p b j", b=NS)[:, :, PB - (w - 1):PB],
                                AX_X, ALU.add).then_inc(pool_pre, 1)
                dve.wait_ge(pool_pre, 2 * g + 1)
                V.tensor_tensor(pre[:, :], pre[:, :], ad, ALU.add).then_inc(pool_pre, 1)
                dve.wait_ge(pool_pre, 2 * g + 2)
                V.scalar_tensor_tensor(ad, pre[:, :], 1.0 / w, ad, ALU.mult, ALU.subtract).then_inc(pool_d, 1)
            dve.wait_ge(zd_made, NE)
            zv = z_dec[:, :, :, :].rearrange("p g b h -> p (g b) h")
            V.tensor_tensor(zv, zv, bias_h[:, :].unsqueeze(1).to_broadcast([P, NE, H]), ALU.add).then_inc(zb_made, 1)
            dve.wait_ge(dec_l, 1)
            V.scalar_tensor_tensor(t_dec[:], z_dec[:], 0.0, t_dec[:], ALU.max, ALU.add).then_inc(dec_sp, 1)
            dve.wait_ge(dec_cum, 1)
            zf = z_dec[:, :, :, :].rearrange("p g b h -> p (g b h)")
            V.tensor_tensor(zf, dec_sums, zf, ALU.add).then_inc(dec_arg, 1)
            dve.wait_ge(consts, NCONST + 4)
            V.tensor_reduce(pick[:, :], ident[0:NS * H, 0:NS * H].rearrange("p (h b) -> p b h", h=H), AX_X, ALU.add
                            ).then_inc(own_made, 1)
            dve.wait_ge(own_mask, 3)
            dve.wait_ge(dec_pv, NE)
            V.tensor_tensor(own_rows, dec_rows, own, ALU.mult).then_inc(own_made, 1)
            dve.wait_ge(ydec_hi, 1)
            V.tensor_tensor(y_lo[:, :, TP:T], dec_o, y_hi[:, :, TP:T].bitcast(F32), ALU.subtract).then_inc(ydec_made, 1)

            def mix_tile(name, first, adds, i, k, split_mixed=False):
                d = bass.ds(i * 2 + k, 1)
                u = i * 4 + (first + 2 * k)
                split_lo(0, u + 2)
                if split_mixed:
                    for n in range(3):
                        mixed_lo(n)
                dve.wait_ge(unit_done, u + 2)
                dve.wait_ge(ps_free[0], i * 2 + freed(name, 0, k + 1))
                out = trunk[:, d, :].rearrange("p o t -> p (o t)") if adds is None else gate[k][:, :]
                V.tensor_tensor(chunks(out), ps[1], chunks(gate[k][:, :]), ALU.mult).then_inc(ps_free[1], 1)
                split_lo(1, u + 3)
                if adds is not None:
                    dve.wait_ge(ps_free[1], i * 2 + freed(name, 1, k + 1))
                    V.tensor_tensor(trunk[:, d, :], trunk[:, d, :], gate[k][:, :].unsqueeze(1), ALU.add
                                    ).then_inc(mix_made, 1)

            def mix(name, first, adds, end=KT // 2):
                with dve.Fori(0, end) as i:
                    for k in range(2):
                        mix_tile(name, first, adds, i, k)

            def mixed_lo(k):
                dve.wait_ge(mhi_made, k + 1)
                V.tensor_tensor(h_lo[:, k, :], trunk[:, k, :], h_hi[:, k, :].bitcast(F32), ALU.subtract
                                ).then_inc(m_split, 1)

            mix("mixc", U_MIXC, None)
            for g in range(SG):
                dve.wait_ge(y_hi_made, g + 1)
                V.scalar_tensor_tensor(chunks(y_lo[:, g, :]), ps[g % 2], a_scale[:, g:g + 1],
                                       chunks(y_hi[:, g, :]).bitcast(F32), ALU.mult, ALU.subtract
                                       ).then_inc(ps_free[g % 2], 1)
            mix("mixa", U_MIXA, 0)
            with dve.Fori(0, SG // 2) as i:
                for k in range(2):
                    g = bass.ds(i * 2 + k, 1)
                    sv = spat[:, g, :].rearrange("p o (a b) -> p (o a) b", a=NCH)
                    dve.wait_ge(unit_done, i * 2 + (U_U + k + 1))
                    V.tensor_tensor(sv, ps[k], sv, ALU.mult).then_inc(ps_free[k], 1)
                    split_lo(k, i * 2 + (U_U + k + 2))
                    dve.wait_ge(y_hi_made, i * 2 + (SG + k + 1))
                    V.tensor_tensor(y_lo[:, g, :], spat[:, g, :], y_hi[:, g, :].bitcast(F32), ALU.subtract
                                    ).then_inc(yb_made, 1)
            mix("mixb", U_MIXB, KT, KT // 2 - 1)
            mix_tile("mixb", U_MIXB, KT, KT // 2 - 1, 0)
            mix_tile("mixb", U_MIXB, KT, KT // 2 - 1, 1, True)
            for k in range(3, KT):
                mixed_lo(k)

            dve.wait_ge(out_done, 16 * 3)
            V.memset(ss_acc, 0.0).then_inc(ss_zero, 1)
            dve.wait_ge(ss_zero, 1)
            with dve.Fori(0, KT // 2 - 1) as i:
                for k in range(2):
                    split_lo(k, i * 2 + (U_OUT + k + 2))
                    dve.wait_ge(ps_free[k], i + freed("out", k, 1))
                    dve.wait_ge(ss_added, i * 2 + (k + 1))
                    V.tensor_tensor(ss_acc, ss_acc, sq, ALU.add).then_inc(ss_added, 1)

            def add_part_squares(c):
                for n in (2 * c, 2 * c + 1):
                    dve.wait_ge(msq_made, n + 1)
                    dve.wait_ge(ss_added, SUMS0 + n)
                    V.tensor_tensor(ss_acc[:, cols[c]], ss_acc[:, cols[c]], m_sq[n % 3][:, :], ALU.add
                                    ).then_inc(ss_added, 1)

            def residual(c):
                dve.wait_ge(rm_made, c + 1)
                for k in range(KT):
                    V.tensor_tensor(trunk[:, k, cols[c]], trunk[:, k, cols[c]], rstd[:, cols[c]], ALU.mult
                                    ).then_inc(mr_made, 1)
                    if c == 0 and k == 1:
                        dve.wait_ge(xg_sb, len(XT_GROUPS))
                    if k % 2:
                        dve.wait_ge(mr_made, c * KT + k + 1)
                        V.tensor_tensor(trunk[:, k, cols[c]], trunk[:, k, cols[c]], x_t[:, k, cols[c]], ALU.add
                                        ).then_inc(x1_odd, 1)

            def ffn_h(c):
                dve.wait_ge(rx_made, c + 1)
                for k in range(KT + 1):
                    j = c * KT + k
                    if c == 0 and k == KT // 2:
                        split_lo(1, U_UP[0] + 1)
                    if k < KT:
                        if j >= 3:
                            dve.wait_ge(h2_made, j - 2)
                        V.scalar_tensor_tensor(hn[j % 3][:, :], trunk[:, k, cols[c]], g_ffn[:, k:k + 1],
                                               rstd[:, cols[c]], ALU.mult, ALU.mult).then_inc(hn_made, 1)
                    if k > 0:
                        dve.wait_ge(hn_hi, j)
                        V.tensor_tensor(h_lo[:, k - 1, cols[c]], hn[(j - 1) % 3][:, :],
                                        h_hi[:, k - 1, cols[c]].bitcast(F32), ALU.subtract).then_inc(h2_made, 1)

            add_part_squares(0)
            residual(0)
            add_part_squares(1)
            split_lo(0, U_UP[0])
            ffn_h(0)
            add_part_squares(2)
            residual(1)
            residual(2)
            ffn_h(1)
            ffn_h(2)
            dve.wait_ge(ssm_ps, NCH)
            V.memset(ss_acc, 0.0).then_inc(ss_zero, 1)

            for g, (f0, size) in enumerate(FFN_GROUPS):
                with dve.Fori(0, size) as j:
                    for k in range(2):
                        f = bass.ds(j + (f0 + k * FT), 1)
                        c, x = conv[k], up[k]
                        s0 = j * 8 + (8 * f0 + 4 * k)
                        split_lo(k, j * 2 + (U_UP[g] + k + 2))
                        dve.wait_ge(ps_free[k], j + freed(f"up{g}", k, 1))
                        V.scalar_tensor_tensor(c[:, 1:TP], x[:, 0:TP - 1], conv_par[:, 1, f], c[:, 1:TP],
                                               ALU.mult, ALU.add).then_inc(conv_step, 1)
                        V.scalar_tensor_tensor(c[:, TP:T], conv_st[:, f, :, 1].rearrange("p o b -> p (o b)"),
                                               conv_par[:, 1, f], c[:, TP:T], ALU.mult, ALU.add).then_inc(conv_step, 1)
                        dve.wait_ge(conv_step, s0 + 1)
                        V.scalar_tensor_tensor(c[:, 2:TP], x[:, 0:TP - 2], conv_par[:, 0, f], c[:, 2:TP],
                                               ALU.mult, ALU.add).then_inc(conv_step, 1)
                        dve.wait_ge(conv_step, s0 + 2)
                        V.scalar_tensor_tensor(c[:, TP:T], conv_st[:, f, :, 0].rearrange("p o b -> p (o b)"),
                                               conv_par[:, 0, f], c[:, TP:T], ALU.mult, ALU.add).then_inc(conv_step, 1)
                    dve.wait_ge(gelu_made, j + (f0 + 1))
                    dve.wait_ge(conv_step, j * 8 + (8 * f0 + 8))
                    V.tensor_tensor(conv[0][:, :], conv[0][:, :], conv[1][:, :], ALU.mult).then_inc(gv_made, 1)
                    dve.wait_ge(g_hi_made, j + (f0 + 1))
                    V.tensor_tensor(g_lo[:, bass.ds(j, 1), :].rearrange("p o t -> p (o t)"), conv[0][:, :],
                                    g_hi[:, bass.ds(j, 1), :].rearrange("p o t -> p (o t)").bitcast(F32),
                                    ALU.subtract).then_inc(g_made, 1)
                name = f"down{g}"
                if g > 0:
                    for k in range(2):
                        dve.wait_ge(ps_free[k], freed(f"down{g - 1}", k, KT // 2))
                last_group = g == len(FFN_GROUPS) - 1

                if last_group:
                    dve.wait_ge(ss_zero, 2)
                with dve.Fori(0, KT // 2 - last_group) as i:
                    for k in range(2):
                        if g > 0:
                            t = trunk[:, bass.ds(i * 2 + k, 1), :].rearrange("p o (a b) -> p (o a) b", a=NCH)
                            dve.wait_ge(unit_done, i * 2 + (U_DOWN[g] + k + 1))
                            V.tensor_tensor(t, ps[k], t, ALU.add).then_inc(ps_free[k], 1)
                        split_lo(k, i * 2 + (U_DOWN[g] + k + 2))
                        if last_group:
                            dve.wait_ge(sq_made, i * 2 + (k + 1))
                            dve.wait_ge(ss_added, i * 2 + (SUMS0 + 6 + k))
                            V.tensor_tensor(ss_acc, ss_acc, sq, ALU.add).then_inc(ss_added, 1)

            def sum_part(n):
                u, c = F_PARTS[n]
                if c < NCH - 1:
                    dve.wait_ge(fpart_ps, n + 1)
                else:
                    dve.wait_ge(unit_done, U_DOWN[-1] + u + 1)
                V.tensor_tensor(trunk[:, u, cols[c]], ps[u % 2][:, c, :], trunk[:, u, cols[c]], ALU.add
                                ).then_inc(f_summed, 1)

            def add_f_square(n):
                c = F_PARTS[n][1]
                dve.wait_ge(fsq_made, n + 1)
                dve.wait_ge(ss_added, SUMS1 + n)
                V.tensor_tensor(ss_acc[:, cols[c]], ss_acc[:, cols[c]], m_sq[n % 3][:, :], ALU.add
                                ).then_inc(ss_added, 1)

            def last_residual(c, first, end):
                dve.wait_ge(rf_made, c + 1)
                dve.wait_ge(x1r_in, 16)
                for k in range(first, end):
                    V.scalar_tensor_tensor(trunk[:, k, cols[c]], trunk[:, k, cols[c]], g_fpost[:, k:k + 1],
                                           rstd[:, cols[c]], ALU.mult, ALU.mult).then_inc(yr_made, 1)
                    if k % 2:
                        dve.wait_ge(yr_made, c * KT + k + 1)
                        V.tensor_tensor(trunk[:, k, cols[c]], trunk[:, k, cols[c]], x1_back[:, k, cols[c]], ALU.add
                                        ).then_inc(y_odd, 1)

            sum_part(0)
            sum_part(1)
            add_f_square(0)
            add_f_square(1)
            sum_part(2)
            add_f_square(2)
            last_residual(0, 0, 4)
            sum_part(3)
            last_residual(0, 4, 6)
            add_f_square(3)
            last_residual(0, 6, KT)
            sum_part(4)
            add_f_square(4)
            last_residual(1, 0, 4)
            sum_part(5)
            last_residual(1, 4, 6)
            add_f_square(5)
            last_residual(1, 6, KT)
            last_residual(2, 0, KT)
            for n in range(Y_WHOLE, NT + 1):
                m = P if n < NT else NS
                dve.wait_ge(yt_ps, n + 1)
                if n >= 4:
                    dve.wait_ge(y_out_done[n % 4], 16 * (n // 4))
                V.tensor_copy(y_tok[0:m, n % 4, 512:D], yt_buf[n % 2][0:m, 512:D]).then_inc(yt_right, 1)

        @block.tensor
        def _(pe):
            M = nc.tensor.matmul

            def T_(out, in_):
                m = in_.shape[0]
                return nc.tensor.transpose(out, in_, ident[0:m, 0:m])

            def unit(u, par, use, xs, ready=None):
                pe.wait_ge(w_lo_made, u + 3)
                pe.wait_ge(ps_free[par], use)
                n = len(xs)
                for k, (x_hi, x_lo) in enumerate(xs):
                    if ready:
                        ready(k)
                    for s, (w, x) in enumerate(((w_lo, x_hi), (w_hi, x_lo), (w_hi, x_hi))):
                        for c in range(NCH):
                            last = M(ps[par][:, c, :], w[par][:, k, :], x[:, c * CH:(c + 1) * CH],
                                     start=(k == 0 and s == 0), stop=(k == n - 1 and s == 2))
                last.then_inc(unit_done, 1)

            def column_products(out, par, c, xs, first, count):
                n = 3 * len(xs)
                for i in range(first, first + count):
                    x_hi, x_lo = xs[i // 3]
                    w, x = ((w_lo, x_hi), (w_hi, x_lo), (w_hi, x_hi))[i % 3]
                    t = M(out, w[par][:, i // 3, :], x[:, c * CH:(c + 1) * CH], start=(i == 0), stop=(i == n - 1),
                          skip_group_check=True)
                return t

            hs = [(h_hi[:, k, :], h_lo[:, k, :]) for k in range(KT)]
            ys = [(y_hi[:, k, :], y_lo[:, k, :]) for k in range(BT)]

            pe.wait_ge(consts, NCONST + 4)
            FIRST_Q = {4: (0, 0, KT), 5: (0, KT, KT), 6: (0, 2 * KT, KT),
                       7: (1, 0, 3 * KT // 2), 8: (1, 3 * KT // 2, 3 * KT // 2)}
            for n in range(NT + 1):
                m = P if n < NT else NS
                pe.wait_ge(xn_made, n + 1)
                if n >= 2:
                    pe.wait_ge(in_free[n % 2], n // 2)
                for k in range(KT):
                    t = T_(in_ps[n % 2][:, k * m:(k + 1) * m], x_tok[0:m, n, k * P:(k + 1) * P])
                t.then_inc(xt_ps, 1)
                if n in FIRST_Q:
                    c, first, count = FIRST_Q[n]
                    if n == 4:
                        pe.wait_ge(w_lo_made, 3)
                    if first == 0:
                        tiles = -(-(c + 1) * CH // P)
                        for k in range(2):
                            pe.wait_ge(in_free[k], (tiles + 1 - k) // 2)
                    column_products(ps[0][:, c, :], 0, c, hs, first, count)
            pe.wait_ge(in_free[0], NT // 2 + 1)
            pe.wait_ge(in_free[1], NT // 2)
            column_products(ps[0][:, NCH - 1, :], 0, NCH - 1, hs, 0, 3 * KT).then_inc(unit_done, 1)
            pe.wait_ge(params_in, 16 * NPARAMS)
            T_(misc[:, 0:NORM_COLS], norm_rows[:, :])
            for j in range(4):
                T_(misc[:, NORM_COLS + 2 * FT * j:NORM_COLS + 2 * FT * (j + 1)], conv_rows[:, j, :])
            for f in range(2 * FT):
                at = ST_AT + 2 * NS * f if f < ST0 else 512 + 2 * NS * (f - ST0)
                t = T_(misc[:, at:at + 2 * NS], st_rows[:, f * P:(f + 1) * P])
            t.then_inc(par_ps, 1)

            with pe.Fori(0, HP) as p:
                def tokens(dst, src):
                    for n in range(NT):
                        t = T_(dst[:, n * P:(n + 1) * P], src[:, n * P:(n + 1) * P])
                    return t

                def scores(c):
                    hh, kb, q0, W, top, last = CHUNKS[c]
                    r = slice(hh * DH, (hh + 1) * DH)
                    z = z_bank[c][:, 0:W]
                    M(z, k_st[hh][r, kb * P:(kb + 1) * P], q_lo[r, q0:q0 + W], start=True, stop=False,
                      skip_group_check=True)
                    t = M(z, k_st[hh][:, kb * P:(kb + 1) * P], q_st[hh][:, q0:q0 + W], start=False, stop=True,
                          skip_group_check=True)
                    if q0 == kb * P:
                        t = M(z[:, 0:P], ident_b[:, :], mask_b[:, :], start=False, stop=True, skip_group_check=True)
                    t.then_inc(z_ready, 1)

                def softplus_sums(c):
                    hh, kb, q0, W, top, last = CHUNKS[c]
                    z = z_bank[c][:, 0:W]
                    pe.wait_ge(sp_ready, p * NCK + (c + 4))
                    M(z, neg_tri[:, :], sp_lo[c % 3][:, 0:W], start=False, stop=False, skip_group_check=True)
                    t = M(z, neg_tri[:, :], sp_hi[c % 3][:, 0:W], start=False, stop=top, skip_group_check=True)
                    if not top:
                        Wb = CHUNKS[c - 1][3]
                        pe.wait_ge(later_ready, p * NLATER + later_upto[c])
                        t = M(z[:, W - Wb:W], neg_ones[:, :], later[(c - 1) % 4][:, 0:Wb], start=False, stop=True,
                              skip_group_check=True)
                    t.then_inc(cum_ready, 1)

                def values(c):
                    hh, kb, q0, W, top, last = CHUNKS[c]
                    r = slice(hh * DH, (hh + 1) * DH)
                    pe.wait_ge(att_ready, p * NCK + (c + 1))
                    M(misc[r, q0:q0 + W], v_tok[:, kb, r], att[c % 2][:, 0:W], start=top, stop=last,
                      skip_group_check=True).then_inc(pv_done, 1)

                def pooling_tile(step):
                    for j, (begin, end) in enumerate(A_STEPS):
                        if not begin <= step <= end:
                            continue
                        if step == begin and j == 0:
                            pe.wait_ge(w_lo_made, p * 4 + 6)
                        if step == begin and j > 0:
                            pe.wait_ge(a_out, p * NCH + j)
                        per_step = 3 * KT // (end + 1 - begin)
                        t = column_products(a_bank[:, 0:CH], 1, j, hs, (step - begin) * per_step, per_step)
                        if step == end:
                            t.then_inc(unit_done if j == NCH - 1 else a_ps, 1)

                pe.wait_ge(small_made, p * 2 + 2)
                unit(p * 4 + 1, 1, p + freed("att", 1, 0), hs)
                unit(p * 4 + 2, 0, p * 2 + freed("att", 0, 1), hs)
                pe.wait_ge(kf_made, p + 1)
                pe.wait_ge(yc_made, p + 1)
                pe.wait_ge(par_sb, 3)
                tokens(misc, k_f).then_inc(ktok_ps, 1)
                pe.wait_ge(ps_free[0], p * 2 + freed("att", 0, 2))
                pe.wait_ge(ps_free[1], p + freed("att", 1, 1))
                pe.wait_ge(stack_in, p * 64 + 64)
                for c in range(NCK + LAG_VALUES + 1):
                    if c < NCK:
                        scores(c)
                    if 0 <= c - LAG_CUM < NCK:
                        softplus_sums(c - LAG_CUM)
                    pooling_tile(c)
                    if c == 0:
                        pe.wait_ge(ktok_made, p + 1)
                        tokens(misc, v_f).then_inc(vtok_ps, 1)
                    if c == LAG_VALUES:
                        pe.wait_ge(vtok_made, p + 1)
                    if 0 <= c - LAG_VALUES < NCK:
                        values(c - LAG_VALUES)
                    if c == SMALL_STEP:
                        pe.wait_ge(tail_cols, p + 1)
                        T_(a_bank[0:NS, 0:P], q_dec[:, :])
                        T_(a_bank[0:NS, P:2 * P], k_f[:, TP:T])
                        T_(a_bank[0:NS, 2 * P:3 * P], v_f[:, TP:T])
                        T_(a_bank[0:PTAIL, 3 * P:4 * P], a_tail[:, :]).then_inc(small_ps, 1)
                    if NCK <= c < NCK + NCH:
                        if c == NCK:
                            pe.wait_ge(w_lo_made, p * 4 + 7)
                        t = column_products(ps[0][:, c - NCK, :], 0, c - NCK, hs, 0, 3 * KT)
                t.then_inc(unit_done, 1)

            def sg_part(u, c):
                name, i = ("sg", (u - U_SG) // 2) if u < U_MIXC else ("mixc", 0)
                if c == 0:
                    pe.wait_ge(w_lo_made, u + 3)
                    pe.wait_ge(ps_free[u % 2], freed(name, u % 2, i))
                xs = ys if u == U_MIXC + 1 else hs
                t = column_products(ps[u % 2][:, c, :], u % 2, c, xs, 0, 3 * len(xs))
                if c == NCH - 1:
                    t.then_inc(unit_done, 1)

            def sg_tokens(g):
                pe.wait_ge(ps_free[g % 2], freed("sg", g % 2, g // 2 + 1))
                if g > 0:
                    pe.wait_ge(spat_made, g)
                else:
                    pe.wait_ge(sg_sb, 2)
                for n in range(NT):
                    t = T_(misc[:, n * P:(n + 1) * P], vsg_f[g % 2][:, n * P:(n + 1) * P])
                t.then_inc(vsgtok_ps, 1)

            def sg_mix(g):
                pe.wait_ge(vsgtok_made, g + 1)
                for n in range(NT):
                    M(misc[:, n * P:(n + 1) * P], vsg_tok[:, n, :], sgw_t[:, g, :], start=True, stop=False)
                    t = M(misc[:, n * P:(n + 1) * P], ones[0:1, :], sgb_row[0:1, g * P:(g + 1) * P],
                          start=False, stop=True)
                t.then_inc(mixed_ps, 1)

            pe.wait_ge(small_made, 2 * HP + 2)
            for c in range(NCH):
                sg_part(U_SG + 1, c)
            pe.wait_ge(sgw_masked, SG)
            pe.wait_ge(yc_made, HP + 1)
            pe.wait_ge(st_in, 64)
            for g in range(SG):
                T_(misc[:, g * P:(g + 1) * P], sgw_rows[:, g, :])
                t = T_(misc[:, 512 + g * NS * PB:512 + (g + 1) * NS * PB], sp_rows[:, g * P:(g + 1) * P])
            t.then_inc(sg_ps, 1)
            sg_part(U_SG + 2, 0)
            sg_tokens(0)
            sg_part(U_SG + 2, 1)
            sg_mix(0)
            sg_part(U_SG + 2, 2)
            sg_tokens(1)
            sg_part(U_SG + 3, 0)
            sg_mix(1)
            sg_part(U_SG + 3, 1)
            sg_tokens(2)
            sg_part(U_SG + 3, 2)
            sg_mix(2)
            sg_part(U_MIXC, 0)
            sg_tokens(3)
            sg_part(U_MIXC, 1)
            sg_mix(3)
            pe.wait_ge(ps_free[1], freed("mixc", 1, 0))
            pe.wait_ge(dec_sp, 1)
            half = NS * H
            sp_d = t_dec[:, :, :, :].rearrange("p g b h -> p (g b h)")
            M(dec_sums, neg_tri[:, :].bitcast(F32), sp_d, start=True, stop=False, skip_group_check=True)
            M(dec_sums[:, 0:half], neg_ones[:, :], sp_d[:, half:], start=False, stop=True, skip_group_check=True
              ).then_inc(dec_cum, 1)
            for g in range(SG):
                t = T_(banks[4][0:NS, g * P:(g + 1) * P], vsg_dec[:, g, :])
            t.then_inc(sgv_ps, 1)
            sg_part(U_MIXC, 2)
            pe.wait_ge(dec_att, 1)
            pe.wait_ge(spat_made, SG)
            for e in range(NE):
                b, pg = e // NPG, e % NPG
                pe.wait_ge(page_in[e % 4], 16 * ((NE + e) // 4 + 1))
                M(dec_rows, a_pad[:, pg * NS * A_STEP + b * NS * H:pg * NS * A_STEP + (b + 1) * NS * H],
                  kv_pg[:, e % 4, :], start=(e == 0), stop=(e == NE - 1)).then_inc(dec_pv, 1)
            pe.wait_ge(sgv_sb, 1)
            sg_part(U_MIXC + 1, 0)
            pe.wait_ge(own_made, 2)
            for hp in range(HP):
                t = M(dec_o[:, hp, :], own_rows[:, hp * P:(hp + 1) * P], pick[:, :], start=True, stop=True)
            t.then_inc(dec_o_ps, 1)
            sg_part(U_MIXC + 1, 1)
            pe.wait_ge(ydec_made, 1)
            sg_part(U_MIXC + 1, 2)

            def branch(name, first, y_ready, begin=0):
                with pe.Fori(begin, KT) as d:
                    unit(d * 2 + first, 0, d + freed(name, 0, 0), hs)
                    y_ready()
                    unit(d * 2 + (first + 1), 1, d + freed(name, 1, 0), ys)

            branch("mixc", U_MIXC, lambda: pe.wait_ge(ydec_made, 1), 1)
            for g in range(SG):
                pe.wait_ge(pool_d, 3 * SG)
                pe.wait_ge(ps_free[g % 2], freed("pool", g % 2, g // 2))
                for c in range(NCH):
                    t = M(ps[g % 2][:, c, :], poolw[:, g, :], a_raw[:, g, PAD + c * CH:PAD + (c + 1) * CH],
                          start=True, stop=True)
                t.then_inc(ya_ps, 1)
            branch("mixa", U_MIXA, lambda: [pe.wait_ge(ps_free[k], freed("mixa", k, 0)) for k in range(2)])
            with pe.Fori(0, SG // 2) as i:
                for k in range(2):
                    unit(i * 2 + (U_U + k), k, i + freed("u", k, 0), hs)
            branch("mixb", U_MIXB, lambda: pe.wait_ge(yb_made, SG))

            first_three = [(k, par) for par in range(2) for k in range(3)]
            last_two = [(k, par) for par in range(2) for k in (KT - 2, KT - 1)]
            for k, par in first_three + [(k, par) for k in range(3, KT - 2) for par in range(2)] + last_two:
                if k == 0:
                    pe.wait_ge(w_lo_made, U_OUT + par + 3)
                    pe.wait_ge(ps_free[par], freed("out", par, 0))
                pe.wait_ge(m_split, k + 1)
                x_hi, x_lo = hs[k]
                for n, (w, x) in enumerate(((w_lo, x_hi), (w_hi, x_lo), (w_hi, x_hi))):
                    for c in range(NCH):
                        t = M(ps[par][:, c, :], w[par][:, k, :], x[:, cols[c]], start=(k == 0 and n == 0),
                              stop=(k == KT - 1 and n == 2), skip_group_check=True)
                if k == KT - 1:
                    t.then_inc(unit_done, 1)
            with pe.Fori(1, KT // 2 - 2) as i:
                for k in range(2):
                    unit(i * 2 + (U_OUT + k), k, i + freed("out", k, 0), hs)

            def mean_squares(c):
                pe.wait_ge(ss_added, SUMS0 + 2 * (c + 1))
                M(ps[0][:, c, :], ones[:, :], ss_acc[:, cols[c]], start=True, stop=True, skip_group_check=True
                  ).then_inc(ssm_ps, 1)

            def x1_square_sums(c):
                for k in range(KT):
                    pe.wait_ge(xsq_made, c * KT + k + 1)
                    M(ps[1][:, c, :], ones[:, :], x_sq[(c * KT + k) % len(x_sq)], start=(k == 0), stop=(k == KT - 1),
                      skip_group_check=True).then_inc(sx_used, 1)

            pe.wait_ge(xr_in, 32)
            for n, (u, c) in enumerate(M_PARTS):
                if n in (0, NCH):
                    pe.wait_ge(w_lo_made, U_OUT + u + 3)
                    pe.wait_ge(ps_free[u % 2], freed("out", u % 2, KT // 2 - 2))
                if n in (2 * NCH, 2 * NCH + 1):
                    pe.wait_ge(w_lo_made, U_OUT + u + 3)
                    pe.wait_ge(ps_free[u % 2], freed("out", u % 2, KT // 2 - 1))
                t = column_products(ps[u % 2][:, c, :], u % 2, c, hs, 0, 3 * KT // 2)
                if n == len(M_PARTS) - 1:
                    x1_square_sums(0)
                    mean_squares(1)
                t = column_products(ps[u % 2][:, c, :], u % 2, c, hs, 3 * KT // 2, 3 * KT // 2)
                if c == NCH - 1:
                    t.then_inc(unit_done, 1)
                elif n >= 2 * NCH:
                    t.then_inc(part_ps, 1)
                for g in XT_AFTER[n]:
                    half, k = XT_GROUPS[g]
                    dst = misc[:, (g % 2) * 512:(g % 2 + 1) * 512]
                    if g >= 2:
                        pe.wait_ge(xg_sb, g - 1)
                    if half < 2:
                        for j in range(XT_HALF):
                            t = T_(dst[:, j * P:(j + 1) * P], xr_tok[:, half * XT_HALF + j, k * P:(k + 1) * P])
                    else:
                        for k in range(KT):
                            t = T_(dst[:, k * NS:(k + 1) * NS], xr_tok[0:NS, NT, k * P:(k + 1) * P])
                    t.then_inc(xg_ps, 1)
                if n == 2 * NCH + 2:
                    mean_squares(0)

            pe.wait_ge(w_lo_made, U_UP[0] + 4)
            for c in range(NCH):
                order = [(k, par) for k in range(KT) for par in range(2)]
                if c == NCH - 1:
                    order = [(k, par) for par in range(2) for k in range(KT)]
                for k, par in order:
                    pe.wait_ge(h2_made, c * KT + k + 1)
                    x_hi, x_lo = hs[k]
                    for n, (w, x) in enumerate(((w_lo, x_hi), (w_hi, x_lo), (w_hi, x_hi))):
                        t = M(ps[par][:, c, :], w[par][:, k, :], x[:, cols[c]], start=(k == 0 and n == 0),
                              stop=(k == KT - 1 and n == 2), skip_group_check=True)
                    if c == NCH - 1 and k == KT - 1:
                        t.then_inc(unit_done, 1)
                if c == 0:
                    mean_squares(2)
                    x1_square_sums(1)
                    x1_square_sums(2)

            for g, (f0, size) in enumerate(FFN_GROUPS):
                with pe.Fori(1 if g == 0 else 0, size) as j:
                    for k in range(2):
                        unit(j * 2 + (U_UP[g] + k), k, j + freed(f"up{g}", k, 0), hs)
                gs = [(g_hi[:, k, :], g_lo[:, k, :]) for k in range(size)]
                with pe.Fori(0, KT // 2 - (g == len(FFN_GROUPS) - 1)) as i:
                    for k in range(2):
                        unit(i * 2 + (U_DOWN[g] + k), k, i + freed(f"down{g}", k, 0), gs,
                             (lambda kt: pe.wait_ge(g_made, f0 + kt + 2)) if k == 0 else None)

            def f_mean_squares(c):
                pe.wait_ge(ss_added, SUMS1 + 2 * (c + 1))
                M(ps[0][:, c, :], ones[:, :], ss_acc[:, cols[c]], start=True, stop=True, skip_group_check=True
                  ).then_inc(ssf_ps, 1)

            def y_tokens(first, end):
                for n in range(first, end):
                    m = P if n < NT else NS
                    if n >= 2:
                        pe.wait_ge(yt_left, n - 1)
                        if n - 2 >= Y_WHOLE:
                            pe.wait_ge(yt_right, n - 1 - Y_WHOLE)
                    for k in range(KT):
                        t = T_(yt_buf[n % 2][0:m, k * P:(k + 1) * P], trunk[:, k, n * P:n * P + m])
                    t.then_inc(yt_ps, 1)

            for n, (u, c) in enumerate(F_PARTS):
                if n < 2:
                    pe.wait_ge(w_lo_made, U_DOWN[-1] + u + 3)
                    pe.wait_ge(ps_free[u % 2], freed(LAST_DOWN, u % 2, KT // 2 - 1))
                t = column_products(ps[u % 2][:, c, :], u % 2, c, gs, 0, 3 * len(gs))
                t.then_inc(fpart_ps if c < NCH - 1 else unit_done, 1)
                if n in (2, 4):
                    f_mean_squares(n // 2 - 1)
                for r in ROWS_AFTER[n]:
                    if r >= 2:
                        pe.wait_ge(tail_sb, r - 1)
                    for j in range(4):
                        t = T_(misc[0:TAIL, (r % 2) * 512 + j * P:(r % 2) * 512 + (j + 1) * P], tails[:, 4 * r + j, :])
                    t.then_inc(tail_ps, 1)
            pe.wait_ge(tail_sb, ROW_GROUPS)
            pe.wait_ge(f_summed, len(F_PARTS))
            whole = [CH * (c + 1) // P for c in range(NCH - 1)] + [NT + 1]
            for c in range(NCH):
                if c == 1:
                    f_mean_squares(NCH - 1)
                pe.wait_ge(y_even, (c + 1) * KT // 2)
                pe.wait_ge(y_odd, (c + 1) * KT // 2)
                y_tokens(whole[c - 1] if c else 0, whole[c])


_INS = ["x_prompt", "x_sample", "state_pool", "cache_k", "cache_v", "page_table", "state_conv",
        "norm_mix_pre", "norm_mix_post", "norm_ffn_pre", "norm_ffn_post", "w_in", "pool_w",
        "pool_scale", "sg_w", "sg_b", "sb_bias", "w_branch", "w_out", "w_up", "conv_w", "conv_b",
        "w_down"]


def kernel(**inputs):
    import numpy as np
    import concourse.bacc as bacc
    from concourse.bass_utils import run_bass_kernel_spmd

    nc = bacc.Bacc("TRN2", target_bir_lowering=False, num_devices=1, dynamic_dma_scratch_size=1024)
    arrays = {n: np.ascontiguousarray(inputs[n]) for n in _INS}
    args = [nc.dram_tensor(f"in_{n}", a.shape, mybir.dt.from_np(a.dtype), kind="ExternalInput").ap()
            for n, a in arrays.items()]
    s = {n: a.shape for n, a in arrays.items()}
    depth, dec, heads = s["w_in"][0], s["x_sample"][0], s["sb_bias"][1]
    head_dim = s["cache_k"][4]
    shapes = [s["x_prompt"], s["x_sample"],
              (depth, s["x_prompt"][0]) + s["state_pool"][2:], s["state_pool"],
              *[(depth,) + s["x_prompt"][:2] + (heads, head_dim)] * 2,
              *[(depth,) + s["x_sample"][:2] + (heads, head_dim)] * 2,
              (depth, dec, s["x_sample"][1], s["sg_w"][1] * (s["w_branch"][2] // s["sg_w"][1])),
              (depth, s["x_prompt"][0]) + s["state_conv"][2:], s["state_conv"]]
    outs = [nc.dram_tensor(f"out_{i}", shape, F32, kind="ExternalOutput").ap() for i, shape in enumerate(shapes)]
    build(nc, *args, outs)
    r = run_bass_kernel_spmd(nc, [{f"in_{n}": a for n, a in arrays.items()}], core_ids=[0])
    return tuple(r.results[0][f"out_{i}"] for i in range(len(outs)))
```
